# Optimizing a Trainium2 kernel written in Bass

```python
import jax, jax.numpy as jnp
from jax import lax
import numpy as np
import math

D_MODEL = 1024
BATCH = 1
SEQ = 256
DEPTH = 2

GRID_W = 64
N_META = 16
HEAD_DIM = 64
ATTN_HEADS = 8
ATTN_KV_HEADS = 2
ATTN_GROUP = ATTN_HEADS // ATTN_KV_HEADS
ATTN_WIDTH = ATTN_HEADS * HEAD_DIM
ATTN_KV_WIDTH = ATTN_KV_HEADS * HEAD_DIM
NA_HEADS = 8
NA_WIDTH = NA_HEADS * HEAD_DIM
NA_KH_MAX = 8
NA_KW = 16
Q_BLOCK = 128
ROPE_THETA = 10000.0
EPS = 1e-6
IN_SPLITS = (ATTN_WIDTH, ATTN_KV_WIDTH, ATTN_KV_WIDTH, ATTN_WIDTH,
             NA_WIDTH, NA_WIDTH, NA_WIDTH, NA_WIDTH, D_MODEL, D_MODEL)
IN_COLS = ATTN_WIDTH * 2 + ATTN_KV_WIDTH * 2 + NA_WIDTH * 4 + D_MODEL * 2


def rms_norm(x, g):
    xf = x.astype(jnp.float32)
    y = xf * lax.rsqrt(jnp.mean(xf * xf, axis=-1, keepdims=True) + EPS)
    return (y * g.astype(jnp.float32)).astype(x.dtype)

def split_cols(p):
    outs, off = [], 0
    for w in IN_SPLITS:
        outs.append(p[..., off:off + w])
        off += w
    return outs

def axial_rope_tables(n_real):
    t = jnp.arange(n_real, dtype=jnp.int32)
    zeros = jnp.zeros((N_META,), jnp.int32)
    row = jnp.concatenate([zeros, t // GRID_W]).astype(jnp.float32)
    col = jnp.concatenate([zeros, t % GRID_W]).astype(jnp.float32)
    axis_dim = HEAD_DIM // 2
    inv = ROPE_THETA ** (-jnp.arange(0, axis_dim, 2, dtype=jnp.float32) / axis_dim)
    ang_r = row[:, None] * inv[None]
    ang_c = col[:, None] * inv[None]
    ang = jnp.concatenate([ang_r, ang_r, ang_c, ang_c], axis=-1)
    return jnp.cos(ang), jnp.sin(ang)

def apply_axial_rope(x, cos, sin):
    axis_dim = HEAD_DIM // 2
    q4 = axis_dim // 2
    xf = x.astype(jnp.float32)
    xr, xc = xf[..., :axis_dim], xf[..., axis_dim:]
    rot = jnp.concatenate([-xr[..., q4:], xr[..., :q4], -xc[..., q4:], xc[..., :q4]], axis=-1)
    return (xf * cos[None, :, None, :] + rot * sin[None, :, None, :]).astype(x.dtype)

def gqa_attention(q, k, v):
    b, l = q.shape[:2]
    n = l - N_META
    scale = HEAD_DIM ** -0.5

    def attend(qb):
        s = jnp.einsum('bqkgd,bskd->bkgqs', qb, k).astype(jnp.float32) * scale
        p = jax.nn.softmax(s, axis=-1).astype(v.dtype)
        return jnp.einsum('bkgqs,bskd->bqkgd', p, v)

    qg = q.reshape(b, l, ATTN_KV_HEADS, ATTN_GROUP, HEAD_DIM)
    o_meta = attend(qg[:, :N_META])
    q_blocks = qg[:, N_META:].reshape(b, n // Q_BLOCK, Q_BLOCK, ATTN_KV_HEADS, ATTN_GROUP, HEAD_DIM)
    q_blocks = q_blocks.transpose(1, 0, 2, 3, 4, 5)
    o_real = lax.map(attend, q_blocks).transpose(1, 0, 2, 3, 4, 5)
    o_real = o_real.reshape(b, n, ATTN_KV_HEADS, ATTN_GROUP, HEAD_DIM)
    return jnp.concatenate([o_meta, o_real], axis=1).reshape(b, l, ATTN_WIDTH)

def neighbourhood_attention(q, k, v, rpb):
    b, l = q.shape[:2]
    n = l - N_META
    rows = n // GRID_W
    kh = min(NA_KH_MAX, rows)
    scale = HEAD_DIM ** -0.5
    qm, km, vm = q[:, :N_META], k[:, :N_META], v[:, :N_META]

    s_mm = jnp.einsum('bqhd,bmhd->bhqm', qm, km).astype(jnp.float32) * scale
    o_meta = jnp.einsum('bhqm,bmhd->bqhd', jax.nn.softmax(s_mm, axis=-1).astype(v.dtype), vm)

    qg = q[:, N_META:].reshape(b, rows, GRID_W, NA_HEADS, HEAD_DIM)
    kg = k[:, N_META:].reshape(b, rows, GRID_W, NA_HEADS, HEAD_DIM)
    vg = v[:, N_META:].reshape(b, rows, GRID_W, NA_HEADS, HEAD_DIM)

    r = jnp.arange(rows)
    row_start = jnp.clip(r - kh // 2, 0, rows - kh)
    row_bias_idx = row_start[:, None] + jnp.arange(kh)[None] - r[:, None] + NA_KH_MAX - 1
    c = jnp.arange(GRID_W)
    col_start = jnp.clip(c - NA_KW // 2, 0, GRID_W - NA_KW)
    col_idx = col_start[:, None] + jnp.arange(NA_KW)[None]
    col_bias_idx = col_idx - c[:, None] + NA_KW - 1
    rpb_cols = rpb[:, :, col_bias_idx]

    def row_step(args):
        q_row, rs, rbi = args
        k_band = lax.dynamic_slice_in_dim(kg, rs, kh, axis=1)
        v_band = lax.dynamic_slice_in_dim(vg, rs, kh, axis=1)
        k_win = k_band[:, :, col_idx]
        v_win = v_band[:, :, col_idx]
        s_win = jnp.einsum('bchd,bicjhd->bhcij', q_row, k_win).astype(jnp.float32) * scale
        bias = rpb_cols[:, rbi].transpose(0, 2, 1, 3)
        s_win = s_win + bias[None].astype(jnp.float32)
        s_meta = jnp.einsum('bchd,bmhd->bhcm', q_row, km).astype(jnp.float32) * scale
        s = jnp.concatenate([s_win.reshape(b, NA_HEADS, GRID_W, kh * NA_KW), s_meta], axis=-1)
        p = jax.nn.softmax(s, axis=-1).astype(v.dtype)
        p_win = p[..., :kh * NA_KW].reshape(b, NA_HEADS, GRID_W, kh, NA_KW)
        p_meta = p[..., kh * NA_KW:]
        return (jnp.einsum('bhcij,bicjhd->bchd', p_win, v_win)
                + jnp.einsum('bhcm,bmhd->bchd', p_meta, vm))

    o_rows = lax.map(row_step, (qg.transpose(1, 0, 2, 3, 4), row_start, row_bias_idx))
    o_real = o_rows.transpose(1, 0, 2, 3, 4).reshape(b, n, NA_WIDTH)
    return jnp.concatenate([o_meta.reshape(b, N_META, NA_WIDTH), o_real], axis=1)

def hybrid_layer(x, norm_g, w_in, q_norm_g, k_norm_g, rpb, w_o_attn, w_o_na, w_out, cos, sin):
    b, l, _ = x.shape
    h = rms_norm(x, norm_g)
    proj = jnp.einsum('bld,de->ble', h, w_in)
    qa, ka, va, za, qb, kb, vb, zb, ga, gb = split_cols(proj)

    qa = apply_axial_rope(rms_norm(qa.reshape(b, l, ATTN_HEADS, HEAD_DIM), q_norm_g), cos, sin)
    ka = apply_axial_rope(rms_norm(ka.reshape(b, l, ATTN_KV_HEADS, HEAD_DIM), k_norm_g), cos, sin)
    va = va.reshape(b, l, ATTN_KV_HEADS, HEAD_DIM)
    oa = gqa_attention(qa, ka, va) * jax.nn.silu(za)

    qb = qb.reshape(b, l, NA_HEADS, HEAD_DIM)
    kb = kb.reshape(b, l, NA_HEADS, HEAD_DIM)
    vb = vb.reshape(b, l, NA_HEADS, HEAD_DIM)
    ob = neighbourhood_attention(qb, kb, vb, rpb) * jax.nn.silu(zb)

    ya = jnp.einsum('ble,ed->bld', oa, w_o_attn)
    yb = jnp.einsum('ble,ed->bld', ob, w_o_na)
    mixed = jax.nn.sigmoid(ga) * ya + jax.nn.sigmoid(gb) * yb
    return x + jnp.einsum('bld,de->ble', mixed, w_out)

def first_inputs(seed: int = 0) -> dict:
    key = jax.random.key(seed)
    ks = jax.random.split(key, 12)
    f32 = jnp.float32
    x = jax.random.normal(ks[0], (BATCH, SEQ, D_MODEL), f32)
    meta_tokens = jax.random.normal(ks[1], (N_META, D_MODEL), f32)
    norm_g = 1.0 + 0.05 * jax.random.normal(ks[2], (DEPTH, D_MODEL), f32)
    w_in = jax.random.normal(ks[3], (DEPTH, D_MODEL, IN_COLS), f32) * D_MODEL ** -0.5
    q_norm_g = 1.0 + 0.05 * jax.random.normal(ks[4], (DEPTH, HEAD_DIM), f32)
    k_norm_g = 1.0 + 0.05 * jax.random.normal(ks[5], (DEPTH, HEAD_DIM), f32)
    na_rpb = 0.1 * jax.random.normal(ks[6], (DEPTH, NA_HEADS, 2 * NA_KH_MAX - 1, 2 * NA_KW - 1), f32)
    w_o_attn = jax.random.normal(ks[7], (DEPTH, ATTN_WIDTH, D_MODEL), f32) * ATTN_WIDTH ** -0.5
    w_o_na = jax.random.normal(ks[8], (DEPTH, NA_WIDTH, D_MODEL), f32) * NA_WIDTH ** -0.5
    w_out = jax.random.normal(ks[9], (DEPTH, D_MODEL, D_MODEL), f32) * D_MODEL ** -0.5
    final_norm_g = 1.0 + 0.05 * jax.random.normal(ks[10], (D_MODEL,), f32)
    return {"x": x, "meta_tokens": meta_tokens, "norm_g": norm_g, "w_in": w_in,
            "q_norm_g": q_norm_g, "k_norm_g": k_norm_g, "na_rpb": na_rpb,
            "w_o_attn": w_o_attn, "w_o_na": w_o_na, "w_out": w_out,
            "final_norm_g": final_norm_g}

def first_block(x, meta_tokens, norm_g, w_in, q_norm_g, k_norm_g, na_rpb, w_o_attn, w_o_na, w_out, final_norm_g):
    b, s, _ = x.shape
    meta = jnp.broadcast_to(meta_tokens[None].astype(x.dtype), (b, N_META, D_MODEL))
    h = jnp.concatenate([meta, x], axis=1)
    cos, sin = axial_rope_tables(s)
    for i in range(DEPTH):
        h = hybrid_layer(h, norm_g[i], w_in[i], q_norm_g[i], k_norm_g[i], na_rpb[i],
                         w_o_attn[i], w_o_na[i], w_out[i], cos, sin)
    h = rms_norm(h, final_norm_g)
    return h[:, N_META:]


DEPTH_2 = 1

PLE_DIM = 256
D_FF = 2816
GLA_HEADS = 4
GLA_DK = 128
GLA_DV = 256
GLA_LOWRANK = 16
GLA_TAU = 16.0
GLA_CHUNK = 64
DSA_HEADS = 8
DSA_LATENT = 128
IDX_HEADS = 8
IDX_DIM = 64
TOPK_MAX = 256
REL_BUCKETS = 32
REL_MAX_DIST = 128

IN_SIZES = (
    GLA_HEADS * GLA_DK,
    GLA_HEADS * GLA_DK,
    GLA_HEADS * GLA_DV,
    GLA_HEADS * GLA_DV,
    GLA_LOWRANK,
    DSA_HEADS * DSA_LATENT,
    DSA_LATENT,
    IDX_HEADS * IDX_DIM,
    IDX_DIM,
    IDX_HEADS,
    2 * D_MODEL,
)
D_IN = sum(IN_SIZES)


def rms_norm_2(x, g):
    xf = x.astype(jnp.float32)
    y = xf * lax.rsqrt(jnp.mean(xf * xf, axis=-1, keepdims=True) + EPS)
    return (y * g.astype(jnp.float32)).astype(x.dtype)

def swiglu(x, w_in, w_out):
    gate, up = jnp.split(x @ w_in, 2, axis=-1)
    return (jax.nn.silu(gate) * up) @ w_out

def t5_bucket(dist):
    max_exact = REL_BUCKETS // 2
    d = jnp.maximum(dist, 0)
    ratio = jnp.maximum(d, 1).astype(jnp.float32) / max_exact
    large = max_exact + (jnp.log(ratio) / math.log(REL_MAX_DIST / max_exact)
                         * (REL_BUCKETS - max_exact)).astype(jnp.int32)
    large = jnp.minimum(large, REL_BUCKETS - 1)
    return jnp.where(d < max_exact, d, large)

def gla_chunked(q, k, v, log_a):
    B, H, S, dk = q.shape
    dv = v.shape[-1]
    C = GLA_CHUNK
    N = S // C

    def to_chunks(t):
        return jnp.moveaxis(t.reshape(B, H, N, C, t.shape[-1]), 2, 0)

    causal = jnp.tril(jnp.ones((C, C), dtype=bool))[:, :, None]

    def step(state, inp):
        qi, ki, vi, gi = inp
        b = jnp.cumsum(gi.astype(jnp.float32), axis=2)
        o_inter = jnp.einsum('bhtd,bhde->bhte', qi * jnp.exp(b), state)
        diff = b[:, :, :, None, :] - b[:, :, None, :, :]
        decay = jnp.exp(jnp.where(causal, diff, -jnp.inf))
        scores = jnp.einsum('bhtd,bhsd,bhtsd->bhts', qi, ki, decay)
        o_intra = jnp.einsum('bhts,bhse->bhte', scores, vi)
        b_last = b[:, :, -1:, :]
        k_dec = ki * jnp.exp(b_last - b)
        new_state = (jnp.exp(b_last[:, :, 0, :])[..., None] * state
                     + jnp.einsum('bhsd,bhse->bhde', k_dec, vi))
        return new_state, o_inter + o_intra

    state0 = jnp.zeros((B, H, dk, dv), jnp.float32)
    _, out = lax.scan(step, state0, (to_chunks(q), to_chunks(k), to_chunks(v), to_chunks(log_a)))
    return jnp.moveaxis(out, 0, 2).reshape(B, H, S, dv)

def dsa_attention(q, c_kv, q_idx, k_idx, w_idx, rel_bias):
    B, S, H, dc = q.shape
    top_k = min(TOPK_MAX, S // 4)
    nb = S // Q_BLOCK
    key_pos = jnp.arange(S, dtype=jnp.int32)
    bidx = jnp.arange(B)[:, None, None]

    def blocks(t):
        return jnp.moveaxis(t.reshape(B, nb, Q_BLOCK, *t.shape[2:]), 1, 0)

    def one_block(args):
        blk, qb, qib, wb = args
        q_pos = blk * Q_BLOCK + jnp.arange(Q_BLOCK, dtype=jnp.int32)
        dots = jnp.einsum('bthd,bsd->bths', qib, k_idx).astype(jnp.float32) * (IDX_DIM ** -0.5)
        w = wb.astype(jnp.float32) * (IDX_HEADS ** -0.5)
        score = jnp.einsum('bths,bth->bts', jax.nn.relu(dots), w)
        causal = key_pos[None, :] <= q_pos[:, None]
        score = jnp.where(causal[None], score, -jnp.inf)
        _, sel = lax.top_k(score, top_k)
        valid = sel <= q_pos[None, :, None]
        kv_sel = c_kv[bidx, sel]
        bias = rel_bias[t5_bucket(q_pos[None, :, None] - sel)]
        logits = (jnp.einsum('bthc,btkc->bthk', qb, kv_sel).astype(jnp.float32) * (dc ** -0.5)
                  + jnp.moveaxis(bias, -1, 2).astype(jnp.float32))
        logits = jnp.where(valid[:, :, None, :], logits, -jnp.inf)
        probs = jax.nn.softmax(logits, axis=-1)
        return jnp.einsum('bthk,btkc->bthc', probs.astype(kv_sel.dtype), kv_sel)

    out = lax.map(one_block, (jnp.arange(nb, dtype=jnp.int32), blocks(q), blocks(q_idx), blocks(w_idx)))
    return jnp.moveaxis(out, 0, 1).reshape(B, S, H, dc)

def hybrid_mixer(u, w_in, alpha_w, alpha_b, gla_norm_g, gla_w_out, ckv_g, dsa_w_out, rel_bias, w_out):
    B, S, _ = u.shape
    split_pts = np.cumsum(IN_SIZES)[:-1].tolist()
    (gq, gk, gv, gr, ga, dq, dkv, iq, ik, iw, gates) = jnp.split(u @ w_in, split_pts, axis=-1)

    def heads(t, n):
        return t.reshape(B, S, n, -1).transpose(0, 2, 1, 3)

    log_a = jax.nn.log_sigmoid((ga @ alpha_w + alpha_b).astype(jnp.float32)) / GLA_TAU
    o = gla_chunked(heads(gq, GLA_HEADS) * (GLA_DK ** -0.5), heads(gk, GLA_HEADS),
                    heads(gv, GLA_HEADS), heads(log_a, GLA_HEADS))
    o = rms_norm_2(o, gla_norm_g.reshape(GLA_HEADS, 1, GLA_DV)).astype(u.dtype)
    o = o.transpose(0, 2, 1, 3).reshape(B, S, GLA_HEADS * GLA_DV) * jax.nn.silu(gr)
    y_gla = o @ gla_w_out

    c_kv = rms_norm_2(dkv, ckv_g)
    od = dsa_attention(dq.reshape(B, S, DSA_HEADS, DSA_LATENT), c_kv,
                       iq.reshape(B, S, IDX_HEADS, IDX_DIM), ik, iw, rel_bias)
    y_dsa = od.reshape(B, S, DSA_HEADS * DSA_LATENT) @ dsa_w_out

    g_gla, g_dsa = jnp.split(jax.nn.sigmoid(gates), 2, axis=-1)
    return (g_gla * y_gla + g_dsa * y_dsa) @ w_out

def second_inputs(seed: int = 0) -> dict:
    key = jax.random.key(seed)
    ks = jax.random.split(key, 24)
    L, D, F = DEPTH_2, D_MODEL, D_FF

    def dense(k, shape, fan_in):
        return jax.random.normal(k, shape, jnp.float32) * (fan_in ** -0.5)

    def gain(k, shape):
        return 1.0 + 0.05 * jax.random.normal(k, shape, jnp.float32)

    return {
        "x": jax.random.normal(ks[0], (BATCH, SEQ, D), jnp.float32),
        "p": jax.random.normal(ks[1], (DEPTH_2, BATCH, SEQ, PLE_DIM), jnp.float32),
        "ffn1_norm": gain(ks[2], (L, D)),
        "ffn1_w_in": dense(ks[3], (L, D, 2 * F), D),
        "ffn1_w_out": dense(ks[4], (L, F, D), F),
        "mix_norm": gain(ks[5], (L, D)),
        "mix_w_in": dense(ks[6], (L, D, D_IN), D),
        "gla_alpha_w": dense(ks[7], (L, GLA_LOWRANK, GLA_HEADS * GLA_DK), GLA_LOWRANK),
        "gla_alpha_b": 0.1 * jax.random.normal(ks[8], (L, GLA_HEADS * GLA_DK), jnp.float32),
        "gla_out_norm": gain(ks[9], (L, GLA_HEADS * GLA_DV)),
        "gla_w_out": dense(ks[10], (L, GLA_HEADS * GLA_DV, D), GLA_HEADS * GLA_DV),
        "ckv_norm": gain(ks[11], (L, DSA_LATENT)),
        "dsa_w_out": dense(ks[12], (L, DSA_HEADS * DSA_LATENT, D), DSA_HEADS * DSA_LATENT),
        "rel_bias": 0.5 * jax.random.normal(ks[13], (REL_BUCKETS, DSA_HEADS), jnp.float32),
        "mix_w_out": dense(ks[14], (L, D, D), D),
        "ffn2_norm": gain(ks[15], (L, D)),
        "ffn2_w_in": dense(ks[16], (L, D, 2 * F), D),
        "ffn2_w_out": dense(ks[17], (L, F, D), F),
        "ple_norm": gain(ks[18], (L, D)),
        "ple_w_gate": dense(ks[19], (L, D, D), D),
        "ple_w_proj": dense(ks[20], (L, PLE_DIM, D), PLE_DIM),
        "final_norm": gain(ks[21], (D,)),
    }

def second_block(x, p, ffn1_norm, ffn1_w_in, ffn1_w_out, mix_norm, mix_w_in, gla_alpha_w, gla_alpha_b,
              gla_out_norm, gla_w_out, ckv_norm, dsa_w_out, rel_bias, mix_w_out, ffn2_norm, ffn2_w_in,
              ffn2_w_out, ple_norm, ple_w_gate, ple_w_proj, final_norm):
    h = x
    for i in range(DEPTH_2):
        h = h + 0.5 * swiglu(rms_norm_2(h, ffn1_norm[i]), ffn1_w_in[i], ffn1_w_out[i])
        h = h + hybrid_mixer(rms_norm_2(h, mix_norm[i]), mix_w_in[i], gla_alpha_w[i], gla_alpha_b[i],
                             gla_out_norm[i], gla_w_out[i], ckv_norm[i], dsa_w_out[i], rel_bias,
                             mix_w_out[i])
        h = h + 0.5 * swiglu(rms_norm_2(h, ffn2_norm[i]), ffn2_w_in[i], ffn2_w_out[i])
        hn = rms_norm_2(h, ple_norm[i])
        h = h + jax.nn.sigmoid(hn @ ple_w_gate[i]) * (p[i] @ ple_w_proj[i])
    return rms_norm_2(h, final_norm)


def setup_inputs(seed=0):
    out = dict(first_inputs(seed))
    for name, value in second_inputs(seed + 1).items():
        if name != "x":
            out[name + "_2"] = value
    return out


def reference(
    x, meta_tokens, norm_g, w_in, q_norm_g, k_norm_g, na_rpb, w_o_attn, w_o_na, w_out,
    final_norm_g, p_2, ffn1_norm_2, ffn1_w_in_2, ffn1_w_out_2, mix_norm_2, mix_w_in_2,
    gla_alpha_w_2, gla_alpha_b_2, gla_out_norm_2, gla_w_out_2, ckv_norm_2, dsa_w_out_2,
    rel_bias_2, mix_w_out_2, ffn2_norm_2, ffn2_w_in_2, ffn2_w_out_2, ple_norm_2, ple_w_gate_2,
    ple_w_proj_2, final_norm_2,
):
    x = first_block(
        x, meta_tokens, norm_g, w_in, q_norm_g, k_norm_g, na_rpb, w_o_attn, w_o_na, w_out,
        final_norm_g,
    )
    return second_block(
        x, p_2, ffn1_norm_2, ffn1_w_in_2, ffn1_w_out_2, mix_norm_2, mix_w_in_2, gla_alpha_w_2,
        gla_alpha_b_2, gla_out_norm_2, gla_w_out_2, ckv_norm_2, dsa_w_out_2, rel_bias_2,
        mix_w_out_2, ffn2_norm_2, ffn2_w_in_2, ffn2_w_out_2, ple_norm_2, ple_w_gate_2,
        ple_w_proj_2, final_norm_2,
    )


_drawn_inputs = setup_inputs


def setup_inputs(seed=0):
    import zlib

    import numpy as np

    out = dict(_drawn_inputs(seed))
    spreads = {}
    factors = {'norm_g': 3.783,
     'q_norm_g': 8.0,
     'k_norm_g': 8.0,
     'na_rpb': 4.697,
     'gla_alpha_b_2': 4.781,
     'gla_out_norm_2': 3.929,
     'ckv_norm_2': 5.708,
     'ffn2_norm_2': 3.33,
     'ple_norm_2': 6.654}
    for name, (base, spread) in spreads.items():
        noise = np.random.default_rng([zlib.crc32(name.encode()), seed]).standard_normal(out[name].shape)
        drawn = base * np.exp(spread * noise) if base else spread * noise
        out[name] = __import__('jax').numpy.asarray(drawn.astype(out[name].dtype))
    for name, factor in factors.items():
        out[name] = (out[name] * factor).astype(out[name].dtype)
    return out
```

```python
from contextlib import ExitStack

import numpy as np

import concourse.bass as bass
from concourse import mybir

P = 128
DM = 1024
KT = DM // P
EPS = 1e-6
F32 = mybir.dt.float32
F32R = mybir.dt.float32r
U32 = mybir.dt.uint32
ALU = mybir.AluOpType
ACT = mybir.ActivationFunctionType
AX = mybir.AxisListType

DEPTH = 2
SEQ = 256
META = 16
TOK = SEQ + META
HD = 64
HEADS = 8
PAIRS = HEADS // 2
GRID_W = 64
ROWS = SEQ // GRID_W
WIN = 16
RPB_R, RPB_C = 15, 31
NEG = -1.0e30
TILES = SEQ // P

DFF = 2816
FT = DFF // P
GH, GDK, GDV, CHUNK = 4, 128, 256, 64
LOWRANK, TAU = 16, 16.0
SH = 8
TOPK = min(256, SEQ // 4)
HALVES = (32, 16, 8, 4, 2, 1)
TAKEN = -3.0e38

RAW = 4
CUT = 3
UB = 16


def key_tiles(n):
    return [(i, min(P, n - i * P)) for i in range((n + P - 1) // P)]


def units_of_layer():
    u = [[("ka",)] + [("va", t) for t in range(3)]]
    for name in ("qa", "kb", "qb"):
        u += [[(name, 2 * i), (name, 2 * i + 1)] for i in range(2)]
    u += [[("vb", i, t) for t in range(3)] for i in range(2)]
    for name in ("za", "zb"):
        u += [[(name, 2 * i), (name, 2 * i + 1)] for i in range(2)]
    for name in ("ga", "gb"):
        u += [[(name, 2 * i), (name, 2 * i + 1)] for i in range(4)]
    u += [[("ya", 2 * i), ("yb", 2 * i), ("ya", 2 * i + 1), ("yb", 2 * i + 1)] for i in range(4)]
    u += [[("out", 2 * i), ("out", 2 * i + 1)] for i in range(4)]
    return u


def units_of_ffn():
    return [[("gate", j), ("up", j)] for j in range(FT)] + [
        [("down", m, half)] for m in range(KT) for half in range(2)]


def units_of_mixer():
    u = [[("low",), ("index_w", 0), ("index_w", 1), ("ckv",)]]
    for name in ("gk", "gq"):
        u += [[(name, 2 * i), (name, 2 * i + 1)] for i in range(2)]
    u += [[("gv", i, t) for t in range(TILES)] for i in range(4)]
    for name, n in (("iq", 4), ("gr", 8), ("dq", 8), ("mg", 8), ("ms", 8)):
        u += [[(name, 2 * i), (name, 2 * i + 1)] for i in range(n // 2)]
    u += [[("yg", m), ("ys", m)] for m in range(KT)]
    u += [[("mix", 2 * i), ("mix", 2 * i + 1)] for i in range(4)]
    return u


def units_of_embedding():
    return [[("pp", m) for m in range(KT)]] + [[("pg", 2 * i), ("pg", 2 * i + 1)] for i in range(4)]


def plan():
    stages = {}
    units = []
    for stage, u in ([(f"layer{i}", units_of_layer()) for i in range(DEPTH)]
                     + [("ffn0", units_of_ffn()), ("mixer", units_of_mixer()), ("ffn1", units_of_ffn()),
                        ("embed", units_of_embedding())]):
        stages[stage] = len(units)
        units += [[(stage, *g) for g in unit] for unit in u]
    blocks = [UB] * len(units)
    for s in ("ffn0", "ffn1"):
        for i in range(2 * KT):
            blocks[stages[s] + FT + i] = FT // 2
    return stages, units, blocks


STAGES, UNITS, BLOCKS = plan()
LINES = [g for unit in UNITS for g in unit]
LINE = {g: i for i, g in enumerate(LINES)}
UNIT = {g: u for u, unit in enumerate(UNITS) for g in unit}


def last_line(u):
    return LINE[UNITS[u][-1]]


def attention_jobs():
    a = [("A", c, half, t) for c in range(PAIRS) for half in range(2) for t in range(TILES)]
    b = [("B", c, half, t) for c in range(PAIRS) for half in range(2) for t in range(TILES)]
    return a + [("Am", 0), ("Am", 1)] + b + [("Bm",)]


JOBS = attention_jobs()
FILLERS = [(n, m) for n, k in (("za", 4), ("zb", 4), ("ga", 8), ("gb", 8)) for m in range(k)]

STATS = []
for _l in range(DEPTH):
    STATS += [(f"layer{_l}", "norm")] + [(f"layer{_l}", "head", i) for i in range(PAIRS + 1)]
STATS += [("final0", "norm"), ("ffn0", "norm"), ("mixer", "norm"), ("mixer", "ckv")]
STATS += [("mixer", "gla", h) for h in range(GH)] + [("ffn1", "norm"), ("embed", "norm"), ("final1", "norm")]
STAT = {k: i for i, k in enumerate(STATS)}
NORMS = ["layer0", "layer1", "final0", "ffn0", "mixer", "ffn1", "embed", "final1"]

SCORES = [(f"layer{_l}", *j) for _l in range(DEPTH) for j in JOBS]
SCORES += [("mixer", "alpha", i) for i in range(2)]
SCORES += [("mixer", "level", n, t) for n in range(len(HALVES) + 1) for t in range(TILES)]
SCORES += [("mixer", "kdt", t) for t in range(TILES)]
SCORES += [("mixer", "state", h, c) for h in range(GH) for c in range(3)]
SCORES += [("mixer", "dots", t, h) for t in range(TILES) for h in range(SH)]
SCORES += [("mixer", "dsa", h, t) for h in range(SH) for t in range(TILES)]
SCORE = {k: i for i, k in enumerate(SCORES)}

RESULTS = []
for _l in range(DEPTH):
    RESULTS += [(f"layer{_l}", "rot", i) for i in range(PAIRS + 1)]
    RESULTS += [(f"layer{_l}", "A", c) for c in range(PAIRS)] + [(f"layer{_l}", "Am")]
    RESULTS += [(f"layer{_l}", "B", c) for c in range(PAIRS)] + [(f"layer{_l}", "Bm")]
RESULTS += [("mixer", "rel")]
RESULTS += [("mixer", "gla", h, e) for h in range(GH) for e in range(2)]
RESULTS += [("mixer", "dsa", h) for h in range(SH)]
RESULT = {k: i for i, k in enumerate(RESULTS)}

TURNS = [(f"layer{_l}", *j) for _l in range(DEPTH) for j in JOBS]
TURNS += [("mixer", "ckv")] + [("mixer", "dsa", h, t) for h in range(SH) for t in range(TILES)]
TURN = {k: i for i, k in enumerate(TURNS)}



def columns(widths):
    at, places = 0, {}
    for name, w in widths:
        places[name] = (at, w)
        at += w
    return places, at


SMALL, SMALL_W = columns([(f"g_{n}", KT) for n in NORMS] + [(f"q_gain{i}", 1) for i in range(DEPTH)]
                         + [(f"k_gain{i}", 1) for i in range(DEPTH)])
SMALL2, SMALL2_W = columns([("gla_gain", KT), ("ckv_gain", 1), ("alpha_b", GH), ("alpha_w", GH * GDK), ("rel", SH)])
CONST, CONST_W = columns([("ident", P), ("flip", P), ("head_mean", P), ("rot", P), ("cos", TOK), ("sin", TOK), ("window", GRID_W)])
CONST2, CONST2_W = columns([("keep", GH * SEQ), ("later", P), ("bucket", 2 * SEQ)])


SQUARES, _n = {}, 0
for _k in STATS:
    SQUARES[_k] = _n
    _n += {"norm": KT, "head": 1, "ckv": 1, "gla": 2}[_k[1]]
X_BATCH = {k: KT * i for i, k in enumerate(["layer0", "mixed0", "layer1", "mixed1", "ffn0", "mixer", "mixed2", "ffn1",
                                            "embed"])}
H_BATCH = {k: KT * i for i, k in enumerate(["layer0", "layer1", "final0", "ffn0", "mixer", "ffn1", "embed"])}
READS = {"layer1": "layer0", "final0": "layer1", "ffn0": "final0", "mixer": "ffn0", "ffn1": "mixer", "embed": "ffn1",
         "final1": "embed"}
J = len(JOBS)
TURN_OF_JOB = [i for i, k in enumerate(TURNS) if k != ("mixer", "ckv")]
NU = len(UNITS)


LINE_READ, SCORE_READ, RESULT_READ = {}, {}, {}
for _i in range(DEPTH):
    _l = f"layer{_i}"
    for _c in range(PAIRS + 1):
        LINE_READ[(_l, "qa", _c - 1) if _c else (_l, "ka")] = ("squares_ready", SQUARES[(_l, "head", _c)] + 1)
        RESULT_READ[(_l, "rot", _c)] = ("rot_used", 5 * _i + _c + 1)
    for _t in range(3):
        LINE_READ[(_l, "va", _t)] = ("v_ready", 9 * _i + _t + 1)
        for _c in range(2):
            LINE_READ[(_l, "vb", _c, _t)] = ("v_ready", 9 * _i + 4 + 3 * _c + _t)
    for _c in range(PAIRS):
        for _n in range(2):
            LINE_READ[(_l, ("kb", "qb")[_n], _c)] = ("kq_ready", 8 * _i + 4 * _n + _c + 1)
            LINE_READ[(_l, ("za", "zb")[_n], _c)] = ("gates_ready", 8 * _i + 4 * _n + _c + 1)
            RESULT_READ[(_l, "AB"[_n], _c)] = ("pair_gated", 8 * _i + 4 * _n + _c + 1)
            RESULT_READ[(_l, "AB"[_n] + "m")] = ("gated", 2 * _i + _n + 1)
    for _m in range(KT):
        for _n in range(2):
            LINE_READ[(_l, ("ga", "gb")[_n], _m)] = ("gate_ready", 16 * _i + 8 * _n + _m + 1)
            LINE_READ[(_l, ("ya", "yb")[_n], _m)] = ("y_used", 16 * _i + 2 * _m + _n + 1)
        LINE_READ[(_l, "out", _m)] = ("h_ready", H_BATCH[_l] + _m + 1)
    for _n, _j in enumerate(JOBS):
        SCORE_READ[(_l, *_j)] = ("maxed" if _j[0] == "Bm" else "exped", J * _i + _n + 1)
for _f in range(2):
    for _n in range(FT):
        LINE_READ[(f"ffn{_f}", "gate", _n)] = ("act_half", FT * _f + _n + 1)
        LINE_READ[(f"ffn{_f}", "up", _n)] = ("act_full", FT * _f + _n + 1)
    for _m in range(KT):
        LINE_READ[(f"ffn{_f}", "down", _m, 0)] = ("down_used", KT * _f + _m + 1)
        LINE_READ[(f"ffn{_f}", "down", _m, 1)] = ("h_ready", H_BATCH[f"ffn{_f}"] + _m + 1)
_m = "mixer"
LINE_READ[(_m, "low")] = ("low_ready", 3)
LINE_READ[(_m, "ckv")] = ("squares_ready", SQUARES[(_m, "ckv")] + 1)
RESULT_READ[(_m, "rel")] = ("row_ready", 1)
for _t in range(TILES):
    LINE_READ[(_m, "index_w", _t)] = ("index_w_ready", _t + 1)
    SCORE_READ[(_m, "alpha", _t)] = ("alpha_used", 2 * _t + 2)
    SCORE_READ[(_m, "kdt", _t)] = ("kdt_ready", _t + 1)
    for _n in range(len(HALVES) + 1):
        SCORE_READ[(_m, "level", _n, _t)] = ("level_used", TILES * _n + _t + 1)
    for _n in range(4):
        LINE_READ[(_m, "gv", _n, _t)] = ("gv_ready", TILES * _n + _t + 1)
    for _h in range(SH):
        SCORE_READ[(_m, "dots", _t, _h)] = ("relued", SH * _t + _h + 1)
        SCORE_READ[(_m, "dsa", _h, _t)] = ("exped", DEPTH * J + TILES * _h + _t + 1)
for _n in range(4):
    LINE_READ[(_m, "gk", _n)] = ("gla_in", _n + 1)
    LINE_READ[(_m, "gq", _n)] = ("gla_in", GH + _n + 1)
    LINE_READ[(_m, "iq", _n)] = ("index_q_ready", _n + 1)
    for _t in range(3):
        SCORE_READ[(_m, "state", _n, _t)] = ("state_ready", 3 * _n + _t + 1)
    for _t in range(2):
        RESULT_READ[(_m, "gla", _n, _t)] = ("squares_ready", SQUARES[(_m, "gla", _n)] + _t + 1)
for _n in range(KT):
    LINE_READ[(_m, "gr", _n)] = ("gates_ready", 8 * DEPTH + _n + 1)
    LINE_READ[(_m, "dq", _n)] = ("dq_ready", _n + 1)
    LINE_READ[(_m, "mg", _n)] = ("gate_ready", 16 * DEPTH + _n + 1)
    LINE_READ[(_m, "ms", _n)] = ("gate_ready", 16 * DEPTH + KT + _n + 1)
    LINE_READ[(_m, "yg", _n)] = ("y_used", 16 * DEPTH + 2 * _n + 1)
    LINE_READ[(_m, "ys", _n)] = ("y_used", 16 * DEPTH + 2 * _n + 2)
    LINE_READ[(_m, "mix", _n)] = ("h_ready", H_BATCH[_m] + _n + 1)
    RESULT_READ[(_m, "dsa", _n)] = ("od_ready", _n + 1)
    LINE_READ[("embed", "pp", _n)] = ("pp_ready", _n + 1)
    LINE_READ[("embed", "pg", _n)] = ("tanh_ready", 8 * DEPTH + KT + _n + 1)
assert set(LINE_READ) == set(LINES) and set(SCORE_READ) == set(SCORES) and set(RESULT_READ) == set(RESULTS)

LEVEL_FILLERS = [("gv", n, t) for n in range(4) for t in range(TILES)] + [("iq", c) for c in range(4)]
DSA_JOBS = [(h, t) for h in range(SH) for t in range(TILES)]


class Alloc:

    def __init__(self, nc):
        self.nc, self.stack = nc, ExitStack()

    def sb(self, name, shape, dt=F32):
        return self.stack.enter_context(self.nc.sbuf_tensor(name, [P, *shape], dt))

    def bank(self, name):
        return self.stack.enter_context(self.nc.psum_tensor(name, [P, 512], F32))

    def sem(self, name):
        return self.stack.enter_context(self.nc.semaphore(name))

    def close(self):
        self.stack.close()


def hybrid_blocks_kernel(nc, weights, tokens, embeds, small_in, small2_in, rpb, consts_in, consts2_in, levels_in,
                         out):
    al = Alloc(nc)
    sb, sem = al.sb, al.sem

    raw = sb("raw", [RAW, UB * P])
    w_hi = sb("w_hi", [CUT, UB * P], F32R)
    w_lo = sb("w_lo", [CUT, UB * P], F32R)
    h = sb("h", [KT, TOK])
    x_hi = sb("x_hi", [KT, TOK], F32R)
    x_lo = sb("x_lo", [KT, TOK], F32R)
    wide = sb("wide", [KT, TOK])
    root = sb("root", [2, TOK])
    rstd = sb("rstd", [2, TOK])
    consts = sb("consts", [CONST_W])
    small = sb("small", [SMALL_W])
    q_gain = sb("q_gain", [DEPTH])
    mean_dm = sb("mean_dm", [P])
    eps = sb("eps", [1])
    th = sb("th", [2, TOK])
    prod = sb("prod", [2, TOK])
    prod2 = sb("prod2", [2, TOK])
    probs = sb("probs", [2, TOK])
    turned = sb("turned", [2, 3 * P])
    top = sb("top", [2, 8])
    total = sb("total", [2, 8])
    share = sb("share", [2, 8])
    best = sb("best", [8])

    def const(name, rows=P):
        at, w = (CONST.get(name) or CONST2[name])
        return (consts if name in CONST else consts2)[0:rows, at:at + w]

    def operand(name, rows=P):
        at, w = (SMALL.get(name) or SMALL2[name])
        return (small if name in SMALL else small2)[0:rows, at:at + w]

    line_bank = [al.bank(f"line{i}") for i in range(2)]
    stat_bank = al.bank("stat")
    score_bank = [al.bank(f"score{i}") for i in range(2)]
    turn_bank = al.bank("turn")
    result_bank = [al.bank(f"result{i}") for i in range(2)]

    raw_in = [sem(f"raw_in{i}") for i in range(RAW)]
    hi_cut, lo_cut = sem("hi_cut"), sem("lo_cut")
    loaded, loaded2, masks_in = sem("loaded"), sem("loaded2"), sem("masks_in")
    embeds_in = sem("embeds_in")
    rel_in = [sem(f"rel_in{i}") for i in range(2)]
    rel_ready = sem("rel_ready")
    set_up = sem("set_up")
    gains_ready = sem("gains_ready")
    line_done = sem("line_done")
    squares_ready, stat_done, root_ready = sem("squares_ready"), sem("stat_done"), sem("root_ready")
    stat_read = sem("stat_read")
    full_ready, x_hi_ready, x_ready, h_ready = sem("full_ready"), sem("x_hi_ready"), sem("x_ready"), sem("h_ready")
    raw_head, normed, rot_done, roped = sem("raw_head"), sem("normed"), sem("rot_done"), sem("roped")
    kq_ready, v_ready = sem("kq_ready"), sem("v_ready")
    score_done = sem("score_done")
    maxed, exped, probs_ready = sem("maxed"), sem("exped"), sem("probs_ready")
    turn_done, turned_most, turned_rest = sem("turn_done"), sem("turned_most"), sem("turned_rest")
    valued, even_scores = sem("valued"), sem("even_scores")
    rot_used, pair_gated, y_used = sem("rot_used"), sem("pair_gated"), sem("y_used")
    act_half, down_used = sem("act_half"), sem("down_used")
    tanh_ready, gates_ready = sem("tanh_ready"), sem("gates_ready")
    gated, y_hi_ready, y_ready = sem("gated"), sem("y_hi_ready"), sem("y_ready")
    act_full, act_hi_ready, act_ready = sem("act_full"), sem("act_hi_ready"), sem("act_ready")
    dve_step = sem("dve_step")
    act_tanh, out_ready = sem("act_tanh"), sem("out_ready")
    low_ready, index_w_ready, index_q_ready = sem("low_ready"), sem("index_w_ready"), sem("index_q_ready")
    row_done = sem("row_done")
    row_ready, row_stored = sem("row_ready"), sem("row_stored")
    rbias_in = [sem(f"rbias_in{i}") for i in range(2)]
    ckv_raw, ckv_ready = sem("ckv_raw"), sem("ckv_ready")
    alpha_used, soft_in, soft_out = sem("alpha_used"), sem("soft_in"), sem("soft_out")
    soft_step = sem("soft_step")
    gla_in, gv_ready, fallen, risen = sem("gla_in"), sem("gv_ready"), sem("fallen"), sem("risen")
    grown_ready, level_ready, level_used = sem("grown_ready"), sem("level_ready"), sem("level_used")
    kdt_ready, state_ready, gla_done, gla_raw = sem("kdt_ready"), sem("state_ready"), sem("gla_done"), sem("gla_raw")
    gla_full, gg_hi_ready, gg_ready = sem("gla_full"), sem("gg_hi_ready"), sem("gg_ready")
    dq_ready, relued, scored, selected = sem("dq_ready"), sem("relued"), sem("scored"), sem("selected")
    od_hi_ready, od_ready = sem("od_hi_ready"), sem("od_ready")
    p_hi_ready, p_ready, pp_ready, pg_used = sem("p_hi_ready"), sem("p_ready"), sem("pp_ready"), sem("pg_used")
    means_ready = sem("means_ready")
    gate_ready = sem("gate_ready")
    stored = sem("stored")
    signals = dict(squares_ready=squares_ready, v_ready=v_ready, kq_ready=kq_ready, gates_ready=gates_ready,
                   gate_ready=gate_ready, y_used=y_used, h_ready=h_ready, act_half=act_half, act_full=act_full,
                   down_used=down_used, exped=exped, maxed=maxed, rot_used=rot_used, pair_gated=pair_gated, gated=gated,
                   low_ready=low_ready, row_ready=row_ready, index_w_ready=index_w_ready, alpha_used=alpha_used,
                   kdt_ready=kdt_ready, level_used=level_used, gv_ready=gv_ready, relued=relued, gla_in=gla_in,
                   index_q_ready=index_q_ready, state_ready=state_ready, dq_ready=dq_ready, od_ready=od_ready,
                   pp_ready=pp_ready, tanh_ready=tanh_ready)
    row_dram = nc.dram_tensor("bias_by_distance", (SH, 2 * SEQ), F32).ap()

    a1 = Alloc(nc)
    y_hi = a1.sb("y_hi", [KT, TOK], F32R)
    y_lo = a1.sb("y_lo", [KT, TOK], F32R)
    gate = {n: a1.sb(f"gate_{n}", [KT, TOK]) for n in "ab"}
    silu = {n: a1.sb(f"silu_{n}", [PAIRS, TOK]) for n in "ab"}
    qa = a1.sb("qa", [PAIRS, TOK])
    ka = a1.sb("ka", [TOK])
    q_meta = a1.sb("q_meta", [PAIRS * META])
    qb = a1.sb("qb", [PAIRS, TOK])
    kb = a1.sb("kb", [PAIRS, TOK])
    va = a1.sb("va", [3, P])
    vb = a1.sb("vb", [3, HEADS * HD])
    rel = a1.sb("rel", [2, TILES, 2, SEQ])
    a1.close()
    a2 = Alloc(nc)
    consts2 = a2.sb("consts2", [CONST2_W])
    small2 = a2.sb("small2", [SMALL2_W])
    gla_gain = a2.sb("gla_gain", [KT])
    mean_gdv = a2.sb("mean_gdv", [P])
    mean_p = a2.sb("mean_p", [P])
    levels = a2.sb("levels", [len(HALVES) + 1, P], U32)
    a3 = Alloc(nc)
    act_hi = a3.sb("act_hi", [FT, SEQ], F32R)
    act_lo = a3.sb("act_lo", [FT, SEQ], F32R)
    a3.close()
    a3 = Alloc(nc)
    gg_hi = a3.sb("gg_hi", [KT, SEQ], F32R)
    gg_lo = a3.sb("gg_lo", [KT, SEQ], F32R)
    low = turned[:, 0, 0:SEQ]
    index_k = a3.sb("index_k", [SEQ])
    index_q = a3.sb("index_q", [PAIRS, SEQ])
    index_w = a3.sb("index_w", [TILES, SH])
    ckv = a3.sb("ckv", [SEQ])
    ckv_t = a3.sb("ckv_t", [TILES, P])
    a4 = Alloc(nc)
    gk_decay = a4.sb("gk_decay", [2, GH * SEQ])
    gk, decay = gk_decay[:, 0], gk_decay[:, 1]
    gr = gk_decay[:, :, :].rearrange("p a (k t) -> p (a k) t", t=SEQ)
    gq, grown = wide[:, 0:GH, 0:SEQ], wide[:, GH:2 * GH, 0:SEQ]
    fall = a4.sb("fall", [GH * SEQ])
    gate_q = a4.sb("gate_q", [GH * SEQ])
    gate_k = a4.sb("gate_k", [GH * SEQ])
    pairs = a4.sb("pairs", [TILES, GH, P])
    gv = a4.sb("gv", [TILES, GH * GDV])
    states = a4.sb("states", [3, GDV])
    a4.close()
    a4 = Alloc(nc)
    dq = wide[:, :, 0:SEQ]
    mgate = {n: a4.sb(f"mgate_{n}", [KT, SEQ]) for n in "gs"}
    od_hi = a4.sb("od_hi", [SH, SEQ], F32R)
    od_lo = a4.sb("od_lo", [SH, SEQ], F32R)
    rbias = a4.sb("rbias", [2, SEQ + P])
    score = root[:, :, 0:SEQ]
    work = prod2[:, :, 0:SEQ]
    a4.close()
    a3.close()
    a3 = Alloc(nc)
    bias_row = turned[0:SH].rearrange("p a b -> p (a b)")[:, SEQ:3 * SEQ]
    pp = a3.sb("pp", [KT, SEQ])
    p_in = a3.sb("p_in", [2, SEQ])
    p_hi = a3.sb("p_hi", [2, SEQ], F32R)
    p_lo = a3.sb("p_lo", [2, SEQ], F32R)
    a3.close()
    a2.close()

    block = al.stack.enter_context(nc.Block())

    @block.sync
    def _(sp):
        def load_unit(u):
            if u >= RAW:
                sp.wait_ge(lo_cut, u - RAW + 1)
            n = BLOCKS[u] * P
            sp.dma_start(raw[:, u % RAW, 0:n], weights[u, :, 0:n]).then_inc(raw_in[u % RAW], 16)

        def load_rel(i, c):
            n = PAIRS * i + c
            if n >= 2:
                sp.wait_ge(score_done, SCORE[(f"layer{(n - 2) // PAIRS}", "B", (n - 2) % PAIRS, 1, TILES - 1)] + 1)
            for half in range(2):
                for r in range(ROWS):
                    at = ((i * HEADS + 2 * c + half) * RPB_R + 7 - r) * RPB_C + WIN - GRID_W
                    src = bass.AP(rpb.tensor, at, [[1, GRID_W], [RPB_C, ROWS], [1, GRID_W]])
                    dst = rel[(1 - r % 2) * GRID_W:(2 - r % 2) * GRID_W, n % 2, r // 2, half]
                    sp.dma_start(dst.rearrange("p (r c) -> p r c", c=GRID_W), src).then_inc(rel_in[n % 2], 16)

        def load_rbias(hd):
            if hd >= 2:
                sp.wait_ge(score_done, SCORE[("mixer", "dsa", hd - 2, TILES - 1)] + 1)
            for t in range(TILES):
                at = hd * 2 * SEQ + SEQ - (t + 1) * P
                src = bass.AP(row_dram.tensor, at, [[1, P], [1, (t + 1) * P]])
                sp.dma_start(rbias[:, hd % 2, t * P:t * P + (t + 1) * P], src).then_inc(rbias_in[hd % 2], 16)

        sp.dma_start(h[:, 0:KT // 2], tokens[:, 0:KT // 2]).then_inc(loaded, 16)
        sp.dma_start(h[:, KT // 2:KT], tokens[:, KT // 2:KT]).then_inc(loaded, 16)
        sp.dma_start(small[:, :], small_in).then_inc(loaded, 16)
        load_unit(0)
        sp.dma_start(consts[:, :], consts_in).then_inc(loaded, 16)
        for u in range(1, NU):
            load_unit(u)
            for i in range(DEPTH):
                for c, behind in enumerate((7, 8, 21, 22)):
                    if u == STAGES[f"layer{i}"] + behind:
                        load_rel(i, c)
            if u == STAGES["ffn0"] + 4:
                sp.wait_ge(h_ready, H_BATCH["final0"] + KT)
                sp.dma_start(consts2[:, :], consts2_in).then_inc(loaded2, 16)
                sp.dma_start(small2[:, :], small2_in).then_inc(loaded2, 16)
                sp.dma_start(levels[:, :, :], levels_in).then_inc(loaded2, 16)
            if u == UNIT[("mixer", "gv", 3, 0)]:
                sp.wait_ge(row_ready, 1)
                sp.dma_start(row_dram, bias_row).then_inc(row_stored, 16)
            if u == UNIT[("mixer", "mg", 0)]:
                sp.wait_ge(row_stored, 16)
                sp.wait_ge(gg_ready, KT)
                load_rbias(0)
                load_rbias(1)
            if UNIT[("mixer", "ms", 0)] <= u < UNIT[("mixer", "yg", 2)]:
                load_rbias(u - UNIT[("mixer", "ms", 0)] + 2)

        sp.wait_ge(h_ready, H_BATCH["ffn1"] + KT)
        sp.dma_start(p_in[:, :, :], embeds).then_inc(embeds_in, 16)
        for half in range(2):
            k = slice(half * KT // 2, (half + 1) * KT // 2)
            sp.wait_ge(out_ready, (half + 1) * KT // 2)
            sp.dma_start(out[:, k], wide[:, k, 0:SEQ]).then_inc(stored, 16)
        sp.wait_ge(stored, 32)

    @block.gpsimd
    def _(pool):
        pool.memset(mean_dm[:, :], 1.0 / DM).then_inc(set_up, 1)
        pool.memset(eps[:, :], EPS).then_inc(set_up, 1)
        for u in range(NU):
            n = BLOCKS[u] * P
            if u == STAGES["ffn0"] + CUT:
                pool.wait_ge(h_ready, H_BATCH["final0"] + KT)
                pool.memset(mean_gdv[:, :], 1.0 / GDV).then_inc(means_ready, 1)
                pool.memset(mean_p[:, :], 1.0 / P).then_inc(means_ready, 1)
            pool.wait_ge(hi_cut, u + 1)
            pool.tensor_tensor(w_lo[:, u % CUT, 0:n], raw[:, u % RAW, 0:n], w_hi[:, u % CUT, 0:n].bitcast(F32),
                               ALU.subtract).then_inc(lo_cut, 1)

    @block.scalar
    def _(act):
        cut = [0]

        def cut_to(u):
            while cut[0] <= min(u, NU - 1):
                v = cut[0]
                n = BLOCKS[v] * P
                act.wait_ge(raw_in[v % RAW], 16 * (v // RAW + 1))
                if v >= CUT:
                    act.wait_ge(line_done, last_line(v - CUT) + 1)
                act.activation(w_hi[:, v % CUT, 0:n], raw[:, v % RAW, 0:n], ACT.Copy).then_inc(hi_cut, 1)
                cut[0] += 1

        def line_wait(key):
            cut_to(UNIT[key] + CUT - 1)
            act.wait_ge(line_done, LINE[key] + 1)
            return line_bank[LINE[key] % 2]

        def squares_of_h(name, n, before=None):
            for k in range(KT):
                if before:
                    cut_to(UNIT[before(k)] + CUT - 1)
                if name == "layer0":
                    act.wait_ge(loaded, 64)
                else:
                    act.wait_ge(h_ready, H_BATCH[READS[name]] + k + 1)
                act.activation(wide[:, k, 0:n], h[:, k, 0:n], ACT.Square).then_inc(squares_ready, 1)

        def root_of(key, n):
            act.wait_ge(stat_done, STAT[key] + 1)
            act.activation(root[:, STAT[key] % 2, 0:n], stat_bank[:, 0:n], ACT.Sqrt,
                           bias=eps[:, :]).then_inc(root_ready, 1)

        def round_x(batch, n):
            for k in range(KT):
                act.wait_ge(full_ready, X_BATCH[batch] + k + 1)
                act.activation(x_hi[:, k, 0:n], wide[:, k, 0:n], ACT.Copy).then_inc(x_hi_ready, 1)

        def layer(i):
            name = f"layer{i}"
            squares_of_h(name, TOK, (lambda k: (f"layer{i - 1}", "out", k)) if i else None)
            cut_to(STAGES[name] + CUT - 1)
            root_of((name, "norm"), TOK)
            round_x(name, TOK)

            def raw_head_of(key, dst, n):
                bank = line_wait(key)
                act.activation(dst, bank[:, 0:TOK], ACT.Copy).then_inc(raw_head, 1)
                if n >= 2:
                    act.wait_ge(stat_done, STAT[(name, "head", n - 2)] + 1)
                act.activation(th[:, n % 2, :], bank[:, 0:TOK], ACT.Square).then_inc(squares_ready, 1)

            def copy_of(key, dst, scale):
                bank = line_wait(key)
                act.activation(dst, bank[:, 0:TOK], ACT.Copy, scale=scale).then_inc(kq_ready, 1)

            raw_head_of((name, "ka"), ka[:, :], 0)
            for c in range(PAIRS):
                raw_head_of((name, "qa", c), qa[:, c], c + 1)
                root_of((name, "head", c), TOK)
            copy_of((name, "kb", 0), kb[:, 0], 1.0)
            root_of((name, "head", PAIRS), TOK)
            for c in range(1, PAIRS):
                copy_of((name, "kb", c), kb[:, c], 1.0)
            for c in range(PAIRS):
                copy_of((name, "qb", c), qb[:, c], HD ** -0.5)

            for half in range(2):
                cut_to(UNIT[(name, "vb", half, 0)] + CUT - 1)

            def exps(job, n):
                s = SCORE[(name, *job)]
                act.wait_ge(maxed, n + 1)
                if n >= 2:
                    act.wait_ge(turn_done, TURN_OF_JOB[n - 2] + 1)
                if job[0] == "Bm":
                    at = probs[0:META, n % 2, 0:HEADS * META]
                    act.activation(at, at, ACT.Exp).then_inc(exped, 1)
                    return
                m = PAIRS * META if job[0] == "Am" else P
                act.activation(probs[0:m, n % 2, :], score_bank[s % 2][0:m, 0:TOK], ACT.Exp,
                               bias=top[0:m, n % 2, 0:1], accum_out=total[0:m, n % 2, 0:1]).then_inc(exped, 1)

            def turned_of(job, n):
                act.wait_ge(turn_done, TURN[(name, *job)] + 1)
                if n >= 2:
                    act.wait_ge(valued, n - 1)
                if job[0] == "Bm":
                    out_, in_ = turned[0:META, n % 2, 0:HD], turn_bank[0:META, 0:HD]
                else:
                    m = PAIRS * META if job[0] == "Am" else P
                    out_ = turned[:, n % 2, 0:2 * P].rearrange("p (b q) -> p b q", q=P)[:, :, 0:m]
                    in_ = turn_bank[:, 0:2 * P].rearrange("p (b q) -> p b q", q=P)[:, :, 0:m]
                act.activation(out_, in_, ACT.Copy).then_inc(turned_most, 1)

            def filler(f):
                key = (name, *f)
                bank = line_wait(key)
                if f[0] in ("za", "zb"):
                    n = 8 * i + 4 * (f[0] == "zb") + f[1]
                    if n >= 2:
                        act.wait_ge(gates_ready, n - 1)
                    act.activation(th[:, f[1] % 2, :], bank[:, 0:TOK], ACT.Tanh, scale=0.5).then_inc(tanh_ready, 1)
                else:
                    act.activation(gate[f[0][1]][:, f[1]], bank[:, 0:TOK], ACT.Tanh, scale=0.5).then_inc(gate_ready, 1)

            def round_y(part, n):
                act.wait_ge(gated, n + 1)
                act.activation(y_hi[:, part:part + PAIRS], wide[:, part:part + PAIRS], ACT.Copy).then_inc(y_hi_ready, 1)

            for t in range(J + 2):
                if t < J:
                    exps(JOBS[t], J * i + t)
                if t < len(FILLERS):
                    filler(FILLERS[t])
                if 1 <= t <= J:
                    turned_of(JOBS[t - 1], J * i + t - 1)
                if t == JOBS.index(("Am", 1)) + 3:
                    round_y(0, 2 * i)
            round_y(PAIRS, 2 * i + 1)
            for m in range(KT):
                cut_to(UNIT[(name, "yb", m)] + CUT - 1)
                act.wait_ge(full_ready, X_BATCH[f"mixed{i}"] + m + 1)
                act.activation(x_hi[:, m], wide[:, m], ACT.Copy).then_inc(x_hi_ready, 1)

        for i in range(DEPTH):
            layer(i)
        squares_of_h("final0", SEQ, lambda k: (f"layer{DEPTH - 1}", "out", k))
        root_of(("final0", "norm"), SEQ)

        def ffn(f):
            name = f"ffn{f}"
            cut_to(STAGES[name] + CUT - 1)
            root_of((name, "norm"), SEQ)
            round_x(name, SEQ)

            def round_act(j):
                act.wait_ge(act_full, FT * f + j + 1)
                act.activation(act_hi[:, j], prod2[:, j % 2, 0:SEQ], ACT.Copy).then_inc(act_hi_ready, 1)

            for j in range(FT):
                bank = line_wait((name, "gate", j))
                n = FT * f + j
                if n >= 2:
                    act.wait_ge(act_half, n - 1)
                act.activation(th[:, j % 2, 0:SEQ], bank[:, 0:SEQ], ACT.Tanh, scale=0.5).then_inc(act_tanh, 1)
                if j:
                    round_act(j - 1)
            round_act(FT - 1)

        squares_of_h("ffn0", SEQ)
        ffn(0)

        squares_of_h("mixer", SEQ, lambda k: ("ffn0", "down", k, 1))
        root_of(("mixer", "norm"), SEQ)
        round_x("mixer", SEQ)
        bank = line_wait(("mixer", "low"))
        act.activation(low[0:LOWRANK], bank[0:LOWRANK, 0:SEQ], ACT.Copy).then_inc(low_ready, 1)
        act.activation(index_k[HD:P], bank[HD:P, 0:SEQ], ACT.Copy).then_inc(low_ready, 1)
        act.activation(index_k[0:HD], bank[HD:P, 0:SEQ], ACT.Copy).then_inc(low_ready, 1)
        bank = line_wait(("mixer", "ckv"))
        act.activation(ckv[:, :], bank[:, 0:SEQ], ACT.Copy).then_inc(ckv_raw, 1)
        act.activation(th[:, 0, 0:SEQ], bank[:, 0:SEQ], ACT.Square).then_inc(squares_ready, 1)

        def gla_copy(name, c):
            bank = line_wait(("mixer", name, c))
            if name == "gk":
                act.activation(gk[:, c * SEQ:(c + 1) * SEQ], bank[:, 0:SEQ], ACT.Copy).then_inc(gla_in, 1)
            else:
                act.activation(gq[:, c], bank[:, 0:SEQ], ACT.Copy, scale=GDK ** -0.5).then_inc(gla_in, 1)

        gla_copy("gk", 0)
        act.wait_ge(row_done, 1)
        act.activation(bias_row, result_bank[RESULT[("mixer", "rel")] % 2][0:SH, :], ACT.Copy).then_inc(row_ready, 1)
        gla_copy("gk", 1)
        root_of(("mixer", "ckv"), SEQ)
        gla_copy("gk", 2)
        gla_copy("gk", 3)
        act.wait_ge(soft_in, 1)
        act.activation(gate_k[:, :], gate_k[:, :], ACT.Exp).then_inc(soft_step, 1)
        act.wait_ge(soft_step, 1)
        act.activation(gate_k[:, :], gate_k[:, :], ACT.Ln, bias=1.0).then_inc(soft_out, 1)
        for c in range(GH):
            gla_copy("gq", c)
        act.wait_ge(turn_done, TURN[("mixer", "ckv")] + 1)
        act.activation(ckv_t[:, :, :], turn_bank[:, 0:TILES * P].rearrange("p (t c) -> p t c", c=P),
                       ACT.Copy).then_inc(turned_most, 1)

        def rise(n):
            act.wait_ge(fallen, n + 1)
            act.activation(fall[:, :], fall[:, :], ACT.Exp).then_inc(risen, 1)

        rise(0)
        act.activation(grown, decay.rearrange("p (g t) -> p g t", t=SEQ), ACT.Exp).then_inc(grown_ready, 1)
        for n in range(len(HALVES)):
            for f in LEVEL_FILLERS[2 * n:2 * n + 2]:
                bank = line_wait(("mixer", *f))
                if f[0] == "gv":
                    act.activation(gv[:, f[2], f[1] * 256:(f[1] + 1) * 256], bank[:, 0:256],
                                   ACT.Copy).then_inc(gv_ready, 1)
                else:
                    act.activation(index_q[:, f[1]], bank[:, 0:SEQ], ACT.Copy).then_inc(index_q_ready, 1)
            rise(n + 1)
        cut_to(UNIT[("mixer", "gr", 0)] + CUT - 2)
        for t in range(TILES):
            s = SCORE[("mixer", "kdt", t)]
            act.wait_ge(score_done, s + 1)
            act.activation(fall[:, t * GH * P:(t + 1) * GH * P], score_bank[s % 2][:, :], ACT.Copy).then_inc(kdt_ready, 1)

        def tanh_gr(m):
            bank = line_wait(("mixer", "gr", m))
            if m >= 2:
                act.wait_ge(gates_ready, 8 * DEPTH + m - 1)
            act.activation(probs[:, m % 2, 0:SEQ], bank[:, 0:SEQ], ACT.Tanh, scale=0.5).then_inc(tanh_ready, 1)

        def round_gg(m):
            act.wait_ge(gla_full, m + 1)
            act.activation(gg_hi[:, m], prod2[:, m % 2, 0:SEQ], ACT.Copy).then_inc(gg_hi_ready, 1)

        def head_out(g):
            if g:
                act.wait_ge(stat_done, STAT[("mixer", "gla", g - 1)] + 1)
                act.wait_ge(gla_full, 2 * g)
            for e in range(2):
                bank = result_bank[RESULT[("mixer", "gla", g, e)] % 2]
                act.wait_ge(gla_done, 2 * g + e + 1)
                act.activation(prod[:, e, 0:SEQ], bank[:, 0:SEQ], ACT.Copy).then_inc(gla_raw, 1)
                act.activation(th[:, e, 0:SEQ], bank[:, 0:SEQ], ACT.Square).then_inc(squares_ready, 1)

        for g in range(GH):
            tanh_gr(2 * g)
            tanh_gr(2 * g + 1)
            head_out(g)
            root_of(("mixer", "gla", g), SEQ)
            round_gg(2 * g)
            round_gg(2 * g + 1)

        for n, (t, hd) in enumerate((t, hd) for t in range(TILES) for hd in range(SH)):
            s = SCORE[("mixer", "dots", t, hd)]
            keys = (t + 1) * P
            act.wait_ge(score_done, s + 1)
            if n >= 2:
                act.wait_ge(scored, n - 1)
            act.activation(th[:, n % 2, 0:keys], score_bank[s % 2][:, 0:keys], ACT.Relu).then_inc(relued, 1)
            if n % 2:
                bank = line_wait(("mixer", "dq", n // 2))
                act.activation(dq[:, n // 2], bank[:, 0:SEQ], ACT.Copy, scale=P ** -0.5).then_inc(dq_ready, 1)

        def dsa_exps(i):
            hd, t = DSA_JOBS[i]
            n, s, keys = DEPTH * J + i, SCORE[("mixer", "dsa", hd, t)], (t + 1) * P
            act.wait_ge(maxed, n + 1)
            act.wait_ge(turn_done, TURN_OF_JOB[n - 2] + 1)
            act.activation(probs[:, n % 2, 0:keys], score_bank[s % 2][:, 0:keys], ACT.Exp, bias=top[:, n % 2, 0:1],
                           accum_out=total[:, n % 2, 0:1]).then_inc(exped, 1)

        def dsa_turned(i):
            hd, t = DSA_JOBS[i]
            n, keys = DEPTH * J + i, (t + 1) * P
            act.wait_ge(turn_done, TURN[("mixer", "dsa", hd, t)] + 1)
            act.wait_ge(valued, n - 1)
            act.activation(turned[:, n % 2, 0:keys], turn_bank[:, 0:keys], ACT.Copy).then_inc(turned_most, 1)

        def round_od(i):
            hd, t = DSA_JOBS[i]
            if t == TILES - 1:
                act.wait_ge(valued, DEPTH * J + i + 1)
                act.activation(od_hi[:, hd], result_bank[RESULT[("mixer", "dsa", hd)] % 2][:, 0:SEQ],
                               ACT.Copy).then_inc(od_hi_ready, 1)

        for i in range(len(DSA_JOBS) + 2):
            if i < len(DSA_JOBS):
                dsa_exps(i)
                f = ("mg", "ms")[i // KT], i % KT
                bank = line_wait(("mixer", *f))
                act.activation(mgate[f[0][1]][:, f[1]], bank[:, 0:SEQ], ACT.Tanh, scale=0.5).then_inc(gate_ready, 1)
            if 1 <= i <= len(DSA_JOBS):
                dsa_turned(i - 1)
            if i >= 2:
                round_od(i - 2)
        for m in range(KT):
            cut_to(UNIT[("mixer", "ys", m)] + CUT - 1)
            act.wait_ge(full_ready, X_BATCH["mixed2"] + m + 1)
            act.activation(x_hi[:, m, 0:SEQ], wide[:, m, 0:SEQ], ACT.Copy).then_inc(x_hi_ready, 1)

        squares_of_h("ffn1", SEQ, lambda k: ("mixer", "mix", k))
        ffn(1)

        squares_of_h("embed", SEQ, lambda k: ("ffn1", "down", k, 1))
        root_of(("embed", "norm"), SEQ)
        act.wait_ge(embeds_in, 16)
        act.activation(p_hi[:, :, :], p_in[:, :, :], ACT.Copy).then_inc(p_hi_ready, 1)
        for m in range(KT):
            bank = line_wait(("embed", "pp", m))
            act.activation(pp[:, m], bank[:, 0:SEQ], ACT.Copy, scale=0.5).then_inc(pp_ready, 1)
        round_x("embed", SEQ)
        for m in range(KT):
            bank = line_wait(("embed", "pg", m))
            if m >= 2:
                act.wait_ge(pg_used, m - 1)
            act.activation(th[:, m % 2, 0:SEQ], bank[:, 0:SEQ], ACT.Tanh, scale=0.5).then_inc(tanh_ready, 1)
        squares_of_h("final1", SEQ)
        root_of(("final1", "norm"), SEQ)

    @block.vector
    def _(dve):
        steps = [0]

        def link(ins):
            steps[0] += 1
            ins.then_inc(dve_step, 1)
            dve.wait_ge(dve_step, steps[0])

        def line_wait(key):
            dve.wait_ge(line_done, LINE[key] + 1)
            return line_bank[LINE[key] % 2]

        def rstd_of(key, n):
            s = STAT[key] % 2
            r, v = rstd[:, s, 0:n], root[:, s, 0:n]
            dve.wait_ge(root_ready, STAT[key] + 1)
            link(dve.reciprocal(r, v))
            dve.scalar_tensor_tensor(v, stat_bank[:, 0:n], EPS, r, ALU.add, ALU.mult).then_inc(stat_read, 1)
            dve.wait_ge(stat_read, STAT[key] + 1)
            link(dve.tensor_tensor(v, v, r, ALU.mult))
            link(dve.scalar_tensor_tensor(r, v, -3.0, r, ALU.add, ALU.mult))
            return r

        def normalise(name, n):
            r = rstd_of((name, "norm"), n)
            g = operand(f"g_{name}")
            for k in range(KT):
                dve.scalar_tensor_tensor(wide[:, k, 0:n], h[:, k, 0:n], g[:, k:k + 1], r, ALU.mult,
                                         ALU.mult).then_inc(full_ready, 1)
            rest_of_x(name, n)

        def rest_of_x(batch, n):
            for k in range(KT):
                dve.wait_ge(x_hi_ready, X_BATCH[batch] + k + 1)
                dve.tensor_tensor(x_lo[:, k, 0:n], wide[:, k, 0:n], x_hi[:, k, 0:n].bitcast(F32),
                                  ALU.subtract).then_inc(x_ready, 1)

        def layer(i):
            name = f"layer{i}"
            normalise(name, TOK)

            for t in range(3):
                key = (name, "va", t)
                rows = P if t < TILES else META
                dve.tensor_copy(va[0:rows, t], line_wait(key)[0:rows, 0:P]).then_inc(v_ready, 1)

            def head_norm(n):
                dst = ka[:, :] if n == 0 else qa[:, n - 1]
                g = operand(f"k_gain{i}") if n == 0 else q_gain[:, i:i + 1]
                r = rstd_of((name, "head", n), TOK)
                dve.wait_ge(raw_head, 5 * i + n + 1)
                dve.scalar_tensor_tensor(dst, dst, g, r, ALU.mult, ALU.mult).then_inc(normed, 1)

            def rope(n):
                dst = ka[:, :] if n == 0 else qa[:, n - 1]
                key = (name, "rot", n)
                dve.wait_ge(normed, 5 * i + n + 1)
                dve.tensor_tensor(prod[:, 0, :], dst, const("cos"), ALU.mult)
                dve.wait_ge(rot_done, 5 * i + n + 1)
                dve.tensor_tensor(prod[:, 1, :], result_bank[RESULT[key] % 2][:, 0:TOK], const("sin"),
                                  ALU.mult).then_inc(rot_used, 1)
                dve.wait_ge(rot_used, 5 * i + n + 1)
                dve.tensor_tensor(dst, prod[:, 0, :], prod[:, 1, :], ALU.add).then_inc(roped, 1)
                if n:
                    dve.wait_ge(roped, 9 * i + 2 * n)
                    dve.tensor_copy(q_meta[:, (n - 1) * META:n * META], dst[:, SEQ:TOK]).then_inc(roped, 1)

            for n in range(PAIRS + 1):
                head_norm(n)
                rope(n)
            for half in range(2):
                for t in range(3):
                    key = (name, "vb", half, t)
                    rows = P if t < TILES else META
                    dve.tensor_copy(vb[0:rows, t, half * 256:(half + 1) * 256],
                                    line_wait(key)[0:rows, 0:256]).then_inc(v_ready, 1)

            def window_bias(c):
                n = PAIRS * i + c
                dve.wait_ge(rel_in[n % 2], 16 * 2 * ROWS * (n // 2 + 1))
                at = rel[:, n % 2].rearrange("p t h (r c) -> p (t h r) c", c=GRID_W)
                w = const("window").unsqueeze(1).to_broadcast([P, TILES * 2 * ROWS, GRID_W])
                dve.tensor_tensor(at, at, w, ALU.add).then_inc(rel_ready, 1)

            def maxes(job, n):
                s = SCORE[(name, *job)]
                bank = score_bank[s % 2]
                for c in range(PAIRS):
                    if n - J * i == JOBS.index(("B", c, 0, 0)) - 2:
                        window_bias(c)
                dve.wait_ge(score_done, s + 1)
                if job[0] == "Bm":
                    at = bank[0:META, 0:HEADS * META].rearrange("p (h k) -> p h k", k=META)
                    link(dve.tensor_reduce(top[0:META, n % 2, :], at, AX.X, ALU.max))
                    dve.tensor_tensor(probs[0:META, n % 2, 0:HEADS * META].rearrange("p (h k) -> p h k", k=META), at,
                                      top[0:META, n % 2, :].unsqueeze(2).to_broadcast([META, HEADS, META]),
                                      ALU.subtract).then_inc(maxed, 1)
                    return
                m = PAIRS * META if job[0] == "Am" else P
                dve.tensor_reduce(top[0:m, n % 2, 0:1], bank[0:m, 0:TOK], AX.X, ALU.max, negate=True).then_inc(maxed, 1)

            def shares(job, n):
                dve.wait_ge(exped, n + 1)
                if job[0] == "Bm":
                    at = probs[0:META, n % 2, 0:HEADS * META].rearrange("p (h k) -> p h k", k=META)
                    link(dve.tensor_reduce(total[0:META, n % 2, :], at, AX.X, ALU.add))
                    link(dve.reciprocal(share[0:META, n % 2, :], total[0:META, n % 2, :]))
                    dve.tensor_tensor(at, at, share[0:META, n % 2, :].unsqueeze(2).to_broadcast([META, HEADS, META]),
                                      ALU.mult).then_inc(probs_ready, 1)
                    return
                m = PAIRS * META if job[0] == "Am" else P
                link(dve.reciprocal(share[0:m, n % 2, 0:1], total[0:m, n % 2, 0:1]))
                dve.tensor_scalar(probs[0:m, n % 2, :], probs[0:m, n % 2, :], share[0:m, n % 2, 0:1], None,
                                  ALU.mult).then_inc(probs_ready, 1)

            def turned_of(job, n):
                dve.wait_ge(turned_most, TURN[(name, *job)] + 1)
                if job[0] == "Bm":
                    out_, in_ = turned[0:META, n % 2, HD:P], turn_bank[0:META, HD:P]
                else:
                    m = PAIRS * META if job[0] == "Am" else P
                    out_, in_ = turned[0:META, n % 2, 2 * P:2 * P + m], turn_bank[0:META, 2 * P:2 * P + m]
                dve.tensor_copy(out_, in_).then_inc(turned_rest, 1)

            def filler(f):
                key = (name, *f)
                if f[0] not in ("za", "zb"):
                    return
                n = 8 * i + 4 * (f[0] == "zb") + f[1]
                bank = line_wait(key)
                dve.wait_ge(tanh_ready, n + 1)
                dve.scalar_tensor_tensor(silu[f[0][1]][:, f[1]], th[:, f[1] % 2, :], 1.0, bank[:, 0:TOK], ALU.add,
                                         ALU.mult).then_inc(gates_ready, 1)

            def result_of(job, n):
                kind = job[0][0]
                part = 0 if kind == "A" else PAIRS
                if job in (("Am", 1), ("Bm",)):
                    key = (name, kind + "m")
                    dve.wait_ge(valued, n + 1)
                    dve.tensor_tensor(wide[:, part:part + PAIRS, SEQ:TOK],
                                      result_bank[RESULT[key] % 2][:, 0:PAIRS * META].rearrange(
                                          "p (c q) -> p c q", q=META),
                                      silu[kind.lower()][:, :, SEQ:TOK], ALU.mult).then_inc(gated, 1)
                elif len(job) == 4 and job[2:] == (1, TILES - 1):
                    key = (name, kind, job[1])
                    dve.wait_ge(valued, n + 1)
                    dve.tensor_tensor(wide[:, part + job[1], 0:SEQ], result_bank[RESULT[key] % 2][:, 0:SEQ],
                                      silu[kind.lower()][:, job[1], 0:SEQ],
                                      ALU.mult).then_inc(pair_gated, 1)

            def rest_of_y(part, n):
                dve.wait_ge(y_hi_ready, n + 1)
                dve.tensor_tensor(y_lo[:, part:part + PAIRS], wide[:, part:part + PAIRS],
                                  y_hi[:, part:part + PAIRS].bitcast(F32), ALU.subtract).then_inc(y_ready, 1)

            for t in range(J + 2):
                if t < J:
                    maxes(JOBS[t], J * i + t)
                    shares(JOBS[t], J * i + t)
                if t < len(FILLERS):
                    filler(FILLERS[t])
                if 1 <= t <= J:
                    turned_of(JOBS[t - 1], J * i + t - 1)
                if t >= 2:
                    result_of(JOBS[t - 2], J * i + t - 2)
                if t == JOBS.index(("Am", 1)) + 4:
                    rest_of_y(0, 2 * i)
            rest_of_y(PAIRS, 2 * i + 1)

            def rest_of_mixed(m):
                dve.wait_ge(x_hi_ready, X_BATCH[f"mixed{i}"] + m + 1)
                dve.tensor_tensor(x_lo[:, m], wide[:, m], x_hi[:, m].bitcast(F32), ALU.subtract).then_inc(x_ready, 1)

            for m in range(KT):
                for n, (line, tmp) in enumerate((("ya", prod), ("yb", prod2))):
                    key = (name, line, m)
                    bank = line_wait(key)
                    dve.wait_ge(gate_ready, 16 * i + 8 * n + m + 1)
                    dve.scalar_tensor_tensor(tmp[:, m % 2, :], gate["ab"[n]][:, m], 1.0, bank[:, 0:TOK], ALU.add,
                                             ALU.mult).then_inc(y_used, 1)
                dve.wait_ge(y_used, 16 * i + 2 * m + 2)
                dve.tensor_tensor(wide[:, m], prod[:, m % 2, :], prod2[:, m % 2, :], ALU.add).then_inc(full_ready, 1)
                if m >= 1:
                    rest_of_mixed(m - 1)
            rest_of_mixed(KT - 1)
            for m in range(KT):
                key = (name, "out", m)
                dve.scalar_tensor_tensor(h[:, m], line_wait(key)[:, 0:TOK], 0.25, h[:, m], ALU.mult,
                                         ALU.add).then_inc(h_ready, 1)

        dve.wait_ge(loaded, 64)
        link(dve.tensor_scalar(small[:, :], small[:, :], -0.5, None, ALU.mult))
        for i in range(DEPTH):
            link(dve.tensor_scalar(q_gain[:, i:i + 1], operand(f"q_gain{i}"), HD ** -0.5, None, ALU.mult))
        for i in range(DEPTH):
            layer(i)
        r = rstd_of(("final0", "norm"), SEQ)
        for k in range(KT):
            dve.scalar_tensor_tensor(h[:, k, 0:SEQ], h[:, k, 0:SEQ], operand("g_final0")[:, k:k + 1], r, ALU.mult,
                                     ALU.mult).then_inc(h_ready, 1)

        def ffn(f):
            name = f"ffn{f}"
            normalise(name, SEQ)

            def rest_of_act(j):
                dve.wait_ge(act_hi_ready, FT * f + j + 1)
                dve.tensor_tensor(act_lo[:, j], prod2[:, j % 2, 0:SEQ], act_hi[:, j].bitcast(F32),
                                  ALU.subtract).then_inc(act_ready, 1)

            for j in range(FT):
                bank = line_wait((name, "gate", j))
                dve.wait_ge(act_tanh, FT * f + j + 1)
                dve.scalar_tensor_tensor(prod[:, j % 2, 0:SEQ], th[:, j % 2, 0:SEQ], 1.0, bank[:, 0:SEQ], ALU.add,
                                         ALU.mult).then_inc(act_half, 1)
                bank = line_wait((name, "up", j))
                dve.wait_ge(act_half, FT * f + j + 1)
                dve.tensor_tensor(prod2[:, j % 2, 0:SEQ], prod[:, j % 2, 0:SEQ], bank[:, 0:SEQ],
                                  ALU.mult).then_inc(act_full, 1)
                if j:
                    rest_of_act(j - 1)
            rest_of_act(FT - 1)
            for m in range(KT):
                dve.scalar_tensor_tensor(h[:, m, 0:SEQ], line_wait((name, "down", m, 0))[:, 0:SEQ], 0.25,
                                         h[:, m, 0:SEQ], ALU.mult, ALU.add).then_inc(down_used, 1)
                dve.wait_ge(down_used, KT * f + m + 1)
                dve.scalar_tensor_tensor(h[:, m, 0:SEQ], line_wait((name, "down", m, 1))[:, 0:SEQ], 0.25,
                                         h[:, m, 0:SEQ], ALU.mult, ALU.add).then_inc(h_ready, 1)

        dve.wait_ge(h_ready, H_BATCH["final0"] + KT)
        ffn(0)

        dve.wait_ge(h_ready, H_BATCH["ffn0"] + KT)
        normalise("mixer", SEQ)
        for t in range(TILES):
            dve.tensor_scalar(index_w[:, t], line_wait(("mixer", "index_w", t))[:, 0:SH], (HD * SH) ** -0.5, None,
                              ALU.mult).then_inc(index_w_ready, 1)
        dve.wait_ge(loaded2, 48)
        link(dve.tensor_scalar(gla_gain[:, :], operand("gla_gain"), -0.25, None, ALU.mult))
        link(dve.tensor_scalar(operand("ckv_gain"), operand("ckv_gain"), -0.5, None, ALU.mult))
        dve.memset(pairs[:, :, :, :], 0.0)
        for g in range(GH):
            s = SCORE[("mixer", "alpha", g // 2)]
            dve.wait_ge(score_done, s + 1)
            dve.tensor_scalar(gate_q[:, g * SEQ:(g + 1) * SEQ], score_bank[s % 2][:, g % 2 * SEQ:(g % 2 + 1) * SEQ],
                              operand("alpha_b")[:, g:g + 1], None, ALU.add).then_inc(alpha_used, 1)
        dve.wait_ge(alpha_used, GH)
        dve.scalar_tensor_tensor(gate_k[:, :], gate_q[:, :], -1.0, gate_q[:, :], ALU.mult, ALU.min).then_inc(soft_in, 1)
        link(dve.tensor_scalar(gate_q[:, :], gate_q[:, :], 0.0, 1.0 / TAU, ALU.min, ALU.mult))
        r = rstd_of(("mixer", "ckv"), SEQ)
        dve.wait_ge(ckv_raw, 1)
        dve.scalar_tensor_tensor(ckv[:, :], ckv[:, :], operand("ckv_gain"), r, ALU.mult, ALU.mult).then_inc(ckv_ready, 1)
        dve.wait_ge(soft_out, 1)
        link(dve.scalar_tensor_tensor(fall[:, :], gate_k[:, :], -1.0 / TAU, gate_q[:, :], ALU.mult, ALU.add))
        link(dve.tensor_tensor_scan(decay, const("keep"), fall[:, :], 0.0, ALU.mult, ALU.add))

        def falls(n):
            if n == len(HALVES):
                d, f = (x.rearrange("p (b t) -> p b t", t=CHUNK) for x in (decay, fall[:, :]))
                dve.tensor_tensor(f, d[:, :, CHUNK - 1:CHUNK].to_broadcast([P, GH * SEQ // CHUNK, CHUNK]), d,
                                  ALU.subtract).then_inc(fallen, 1)
                return
            half = HALVES[n]
            d, f = (x.rearrange("p (b s t) -> p b s t", s=2, t=half) for x in (decay, fall[:, :]))
            ref = d[:, :, 0, half - 1:half].to_broadcast([P, GH * SEQ // (2 * half), half])
            link(dve.tensor_tensor(f[:, :, 0], ref, d[:, :, 0], ALU.subtract))
            dve.tensor_tensor(f[:, :, 1], d[:, :, 1], ref, ALU.subtract).then_inc(fallen, 1)

        def by_head(x):
            return x.rearrange("p (g t) -> p g t", t=SEQ)

        falls(0)
        for n in range(len(HALVES) + 1):
            if n == 0:
                dve.wait_ge(gla_in, 2 * GH)
            dve.wait_ge(risen, n + 1)
            if n < len(HALVES):
                dve.tensor_tensor(by_head(gate_q[:, :]), gq, by_head(fall[:, :]), ALU.mult)
            else:
                dve.wait_ge(grown_ready, 1)
                dve.tensor_tensor(by_head(gate_q[:, :]), gq, grown, ALU.mult)
            dve.tensor_tensor(gate_k[:, :], gk, fall[:, :], ALU.mult).then_inc(level_ready, 1)
            if n < len(HALVES):
                dve.wait_ge(level_ready, n + 1)
                falls(n + 1)
            for t in range(TILES):
                s = SCORE[("mixer", "level", n, t)]
                dve.wait_ge(score_done, s + 1)
                mask = levels[:, n].unsqueeze(1).to_broadcast([P, GH, P])
                dve.copy_predicated(pairs[:, t], mask,
                                    score_bank[s % 2][:, :].rearrange("p (g t) -> p g t", t=P)).then_inc(level_used, 1)

        def silu_gr(m):
            bank = line_wait(("mixer", "gr", m))
            dve.wait_ge(tanh_ready, 8 * DEPTH + m + 1)
            dve.scalar_tensor_tensor(gr[:, m], probs[:, m % 2, 0:SEQ], 1.0, bank[:, 0:SEQ], ALU.add,
                                     ALU.mult).then_inc(gates_ready, 1)

        def head_states(g):
            if g:
                dve.wait_ge(gla_done, 2 * g)
            for c in range(3):
                s = SCORE[("mixer", "state", g, c)]
                dve.wait_ge(score_done, s + 1)
                bank = score_bank[s % 2][:, 0:GDV]
                if c == 0:
                    dve.tensor_copy(states[:, 0], bank).then_inc(state_ready, 1)
                else:
                    dve.wait_ge(state_ready, 3 * g + c)
                    end = c * CHUNK + CHUNK - 1
                    dve.scalar_tensor_tensor(states[:, c], states[:, c - 1], grown[:, g, end:end + 1], bank, ALU.mult,
                                             ALU.add).then_inc(state_ready, 1)

        def head_gated(g):
            r = rstd_of(("mixer", "gla", g), SEQ)
            dve.wait_ge(gla_raw, 2 * g + 2)
            for e in range(2):
                m = 2 * g + e
                link(dve.scalar_tensor_tensor(prod[:, e, 0:SEQ], prod[:, e, 0:SEQ], gla_gain[:, m:m + 1], r, ALU.mult,
                                              ALU.mult))
                dve.tensor_tensor(prod2[:, e, 0:SEQ], prod[:, e, 0:SEQ], gr[:, m], ALU.mult).then_inc(gla_full, 1)
            for e in range(2):
                m = 2 * g + e
                dve.wait_ge(gg_hi_ready, m + 1)
                dve.tensor_tensor(gg_lo[:, m], prod2[:, e, 0:SEQ], gg_hi[:, m].bitcast(F32),
                                  ALU.subtract).then_inc(gg_ready, 1)

        for g in range(GH):
            silu_gr(2 * g)
            head_states(g)
            silu_gr(2 * g + 1)
            head_gated(g)

        def choose(t):
            keys = (t + 1) * P
            own = score[:, t, t * P:keys]
            link(dve.tensor_tensor(own, own, const("later"), ALU.add))
            for r in range(TOPK // 8):
                src = work[:, t, 0:keys] if r else score[:, t, 0:keys]
                link(dve.max(best[:, :], src))
                link(dve.match_replace(work[:, t, 0:keys], best[:, :], src, TAKEN))
            link(dve.tensor_scalar(score[:, t, 0:keys], work[:, t, 0:keys], TAKEN / 2, NEG, ALU.is_gt, ALU.mult))
            link(dve.tensor_tensor(own, own, const("later"), ALU.add))

        for n, (t, hd) in enumerate((t, hd) for t in range(TILES) for hd in range(SH)):
            keys = (t + 1) * P
            dve.wait_ge(relued, n + 1)
            w = index_w[:, t, hd:hd + 1]
            if hd == 0:
                dve.tensor_scalar(score[:, t, 0:keys], th[:, n % 2, 0:keys], w, None, ALU.mult).then_inc(scored, 1)
            else:
                dve.wait_ge(scored, n)
                dve.scalar_tensor_tensor(score[:, t, 0:keys], th[:, n % 2, 0:keys], w, score[:, t, 0:keys], ALU.mult,
                                         ALU.add).then_inc(scored, 1)
        dve.wait_ge(scored, TILES * SH)
        for t in range(TILES):
            choose(t)

        def dsa_maxes(i):
            hd, t = DSA_JOBS[i]
            n, s, keys = DEPTH * J + i, SCORE[("mixer", "dsa", hd, t)], (t + 1) * P
            bank = score_bank[s % 2][:, 0:keys]
            dve.wait_ge(score_done, s + 1)
            link(dve.tensor_tensor(bank, bank, score[:, t, 0:keys], ALU.add))
            dve.tensor_reduce(top[:, n % 2, 0:1], bank, AX.X, ALU.max, negate=True).then_inc(maxed, 1)

        def dsa_shares(i):
            hd, t = DSA_JOBS[i]
            n, keys = DEPTH * J + i, (t + 1) * P
            dve.wait_ge(exped, n + 1)
            link(dve.reciprocal(share[:, n % 2, 0:1], total[:, n % 2, 0:1]))
            dve.tensor_scalar(probs[:, n % 2, 0:keys], probs[:, n % 2, 0:keys], share[:, n % 2, 0:1], None,
                              ALU.mult).then_inc(probs_ready, 1)

        def rest_of_od(i):
            hd, t = DSA_JOBS[i]
            if t == TILES - 1:
                dve.wait_ge(od_hi_ready, hd + 1)
                dve.tensor_tensor(od_lo[:, hd], result_bank[RESULT[("mixer", "dsa", hd)] % 2][:, 0:SEQ],
                                  od_hi[:, hd].bitcast(F32), ALU.subtract).then_inc(od_ready, 1)

        for i in range(len(DSA_JOBS) + 2):
            if i < len(DSA_JOBS):
                dsa_maxes(i)
                dsa_shares(i)
            if i >= 2:
                rest_of_od(i - 2)

        def rest_of_mix(m):
            dve.wait_ge(x_hi_ready, X_BATCH["mixed2"] + m + 1)
            dve.tensor_tensor(x_lo[:, m, 0:SEQ], wide[:, m, 0:SEQ], x_hi[:, m, 0:SEQ].bitcast(F32),
                              ALU.subtract).then_inc(x_ready, 1)

        dve.wait_ge(gate_ready, 16 * DEPTH + 2 * KT)
        for m in range(KT):
            for n, (line, tmp, gates) in enumerate((("yg", prod, "g"), ("ys", prod2, "s"))):
                bank = line_wait(("mixer", line, m))
                dve.scalar_tensor_tensor(tmp[:, m % 2, 0:SEQ], mgate[gates][:, m], 1.0, bank[:, 0:SEQ], ALU.add,
                                         ALU.mult).then_inc(y_used, 1)
            dve.wait_ge(y_used, 16 * DEPTH + 2 * m + 2)
            dve.tensor_tensor(wide[:, m, 0:SEQ], prod[:, m % 2, 0:SEQ], prod2[:, m % 2, 0:SEQ],
                              ALU.add).then_inc(full_ready, 1)
            if m:
                rest_of_mix(m - 1)
        rest_of_mix(KT - 1)
        for m in range(KT):
            dve.scalar_tensor_tensor(h[:, m, 0:SEQ], line_wait(("mixer", "mix", m))[:, 0:SEQ], 0.5, h[:, m, 0:SEQ],
                                     ALU.mult, ALU.add).then_inc(h_ready, 1)
        dve.wait_ge(h_ready, H_BATCH["mixer"] + KT)
        ffn(1)

        dve.wait_ge(h_ready, H_BATCH["ffn1"] + KT)
        r = rstd_of(("embed", "norm"), SEQ)
        dve.wait_ge(p_hi_ready, 1)
        dve.tensor_tensor(p_lo[:, :, :], p_in[:, :, :], p_hi[:, :, :].bitcast(F32), ALU.subtract).then_inc(p_ready, 1)
        for k in range(KT):
            dve.scalar_tensor_tensor(wide[:, k, 0:SEQ], h[:, k, 0:SEQ], operand("g_embed")[:, k:k + 1], r, ALU.mult,
                                     ALU.mult).then_inc(full_ready, 1)
        rest_of_x("embed", SEQ)
        dve.wait_ge(pp_ready, KT)
        for m in range(KT):
            dve.wait_ge(tanh_ready, 8 * DEPTH + KT + m + 1)
            dve.scalar_tensor_tensor(prod[:, m % 2, 0:SEQ], th[:, m % 2, 0:SEQ], 1.0, pp[:, m], ALU.add,
                                     ALU.mult).then_inc(pg_used, 1)
            dve.wait_ge(pg_used, m + 1)
            dve.tensor_tensor(h[:, m, 0:SEQ], h[:, m, 0:SEQ], prod[:, m % 2, 0:SEQ], ALU.add).then_inc(h_ready, 1)
        dve.wait_ge(h_ready, H_BATCH["embed"] + KT)
        r = rstd_of(("final1", "norm"), SEQ)
        for k in range(KT):
            dve.scalar_tensor_tensor(wide[:, k, 0:SEQ], h[:, k, 0:SEQ], operand("g_final1")[:, k:k + 1], r, ALU.mult,
                                     ALU.mult).then_inc(out_ready, 1)

    @block.tensor
    def _(pe):
        def unit(u):
            pe.wait_ge(hi_cut, u + 1)
            pe.wait_ge(lo_cut, u + 1)
            return w_hi[:, u % CUT].rearrange("p (b c) -> p b c", c=P), \
                w_lo[:, u % CUT].rearrange("p (b c) -> p b c", c=P)

        def line_open(key):
            g = LINE[key]
            if g >= 2:
                name, count = LINE_READ[LINES[g - 2]]
                pe.wait_ge(signals[name], count)
            return line_bank[g % 2]

        def exact(out_, terms):
            for n, (stay_hi, stay_lo, move_hi, move_lo) in enumerate(terms):
                pe.matmul(out_, stay_hi, move_hi, start=n == 0, stop=False)
                pe.matmul(out_, stay_hi, move_lo, start=False, stop=False)
                ins = pe.matmul(out_, stay_lo, move_hi, start=False, stop=n == len(terms) - 1)
            return ins

        def line(key, at, n, depth=KT, src=None, first=0):
            hi, lo = unit(UNIT[key])
            src_hi, src_lo = src or (x_hi, x_lo)
            bank = line_open(key)
            exact(bank[:, 0:n], [(hi[:, at + k], lo[:, at + k], src_hi[:, first + k, 0:n], src_lo[:, first + k, 0:n])
                                 for k in range(depth)]).then_inc(line_done, 1)

        def by_token(key, at, chunks, tokens_of):
            hi, lo = unit(UNIT[key])
            bank = line_open(key)

            def moving(w, k):
                return w[:, at:at + KT * chunks].rearrange("p (m k) c -> p m k c", k=KT)[:, :, k]

            rows = tokens_of(x_hi, 0).shape[-1]
            exact(bank[0:rows, 0:P * chunks].rearrange("p (m c) -> p m c", c=P),
                  [(tokens_of(x_hi, k), tokens_of(x_lo, k), moving(hi, k), moving(lo, k))
                   for k in range(KT)]).then_inc(line_done, 1)

        def sums(key, tiles, mean):
            s = STAT[key]
            if s:
                pe.wait_ge(stat_read, s)
            for n, sq in enumerate(tiles):
                pe.wait_ge(squares_ready, SQUARES[key] + n + 1)
                ins = pe.matmul(stat_bank[:, 0:sq.shape[-1]], mean, sq, start=n == 0, stop=n == len(tiles) - 1)
            ins.then_inc(stat_done, 1)

        def result_open(key):
            r = RESULT[key]
            if r >= 2:
                name, count = RESULT_READ[RESULTS[r - 2]]
                pe.wait_ge(signals[name], count)
            return result_bank[r % 2]

        def score_open(key):
            s = SCORE[key]
            if s >= 2:
                name, count = SCORE_READ[SCORES[s - 2]]
                pe.wait_ge(signals[name], count)
            return score_bank[s % 2]

        ident = const("ident")

        def token_tile(x, k, t):
            if t < TILES:
                return x[:, k, t * P:(t + 1) * P]
            return x[:, k, SEQ:TOK]

        def layer(i):
            name = f"layer{i}"
            sums((name, "norm"), [wide[:, k, :] for k in range(KT)], mean_dm[:, :])
            pe.wait_ge(x_ready, X_BATCH[name] + KT)
            line((name, "ka"), 0, TOK)
            for t in range(3):
                by_token((name, "va", t), KT, 1, lambda x, k, t=t: token_tile(x, k, t))

            def head_sum(n):
                sums((name, "head", n), [th[:, n % 2, :]], const("head_mean"))

            def rot(n):
                src = ka[:, :] if n == 0 else qa[:, n - 1]
                bank = result_open((name, "rot", n))
                pe.wait_ge(normed, 5 * i + n + 1)
                pe.matmul(bank[:, 0:TOK], const("rot"), src, start=True, stop=True).then_inc(rot_done, 1)

            line((name, "qa", 0), 0, TOK)
            head_sum(0)
            for c in range(1, PAIRS):
                line((name, "qa", c), c % 2 * KT, TOK)
                rot(c - 1)
                head_sum(c)
            line((name, "kb", 0), 0, TOK)
            rot(PAIRS - 1)
            head_sum(PAIRS)
            line((name, "kb", 1), KT, TOK)
            rot(PAIRS)
            for c in range(2, PAIRS):
                line((name, "kb", c), c % 2 * KT, TOK)
            for c in range(PAIRS):
                line((name, "qb", c), c % 2 * KT, TOK)
            for half in range(2):
                for t in range(3):
                    by_token((name, "vb", half, t), 0, 2, lambda x, k, t=t: token_tile(x, k, t))

            def scores(job, n):
                key = (name, *job)
                s = score_open(key)
                if job[0] == "Bm":
                    for hd in [*range(0, HEADS, 2), *range(1, HEADS, 2)]:
                        if hd == 1:
                            ins.then_inc(even_scores, 1)
                            pe.wait_ge(even_scores, i + 1)
                        r = slice(hd % 2 * HD, hd % 2 * HD + HD)
                        ins = pe.matmul(s[0:META, hd * META:(hd + 1) * META], qb[r, hd // 2, SEQ:TOK],
                                        kb[r, hd // 2, SEQ:TOK], start=True, stop=True)
                elif job[0] == "Am":
                    r = slice(job[1] * HD, job[1] * HD + HD)
                    ins = pe.matmul(s[0:PAIRS * META, 0:TOK], q_meta[r, :], ka[r, :], start=True, stop=True)
                else:
                    kind, c, half, t = job
                    r = slice(half * HD, half * HD + HD)
                    q, k = (qa, ka[r, :]) if kind == "A" else (qb, kb[r, c])
                    ins = pe.matmul(s[:, 0:TOK], q[r, c, t * P:(t + 1) * P], k, start=True, stop=kind == "A")
                    if kind == "B":
                        m = PAIRS * i + c
                        pe.wait_ge(rel_ready, m + 1)
                        ins = pe.matmul(s[:, 0:SEQ], const("flip"), rel[:, m % 2, t, half], start=False, stop=True)
                ins.then_inc(score_done, 1)

            def turn(job, n):
                pe.wait_ge(probs_ready, n + 1)
                r = TURN[(name, *job)]
                if r:
                    pe.wait_ge(turned_most, r)
                    pe.wait_ge(turned_rest, r)
                if job[0] == "Bm":
                    for hd in range(HEADS):
                        at = slice(hd * META, (hd + 1) * META)
                        ins = pe.transpose(turn_bank[0:META, at], probs[0:META, n % 2, at], ident[0:META, 0:META])
                else:
                    m = PAIRS * META if job[0] == "Am" else P
                    for kt, w in key_tiles(TOK):
                        ins = pe.transpose(turn_bank[0:w, kt * P:kt * P + m], probs[0:m, n % 2, kt * P:kt * P + w],
                                           ident[0:m, 0:m])
                ins.then_inc(turn_done, 1)

            def values(job, n):
                pe.wait_ge(turned_most, TURN[(name, *job)] + 1)
                pe.wait_ge(turned_rest, TURN[(name, *job)] + 1)
                tn = turned[:, n % 2]
                if job[0] == "Bm":
                    bank = result_open((name, "Bm"))
                    for hd in range(HEADS):
                        r = slice(hd % 2 * HD, hd % 2 * HD + HD)
                        ins = pe.matmul(bank[r, hd // 2 * META:(hd // 2 + 1) * META],
                                        vb[0:META, 2, hd * HD:(hd + 1) * HD], tn[0:META, hd * META:(hd + 1) * META],
                                        start=True, stop=True)
                else:
                    if job[0] == "Am":
                        half, m, at, v = job[1], PAIRS * META, 0, va[:, :, job[1] * HD:(job[1] + 1) * HD]
                        bank = result_open((name, "Am")) if half == 0 else result_bank[RESULT[(name, "Am")] % 2]
                    else:
                        kind, c, half, t = job
                        head = half if kind == "A" else 2 * c + half
                        m, at, v = P, t * P, (va if kind == "A" else vb)[:, :, head * HD:(head + 1) * HD]
                        key = (name, kind, c)
                        bank = result_open(key) if (half, t) == (0, 0) else result_bank[RESULT[key] % 2]
                    r = slice(half * HD, half * HD + HD)
                    for kt, w in key_tiles(TOK):
                        ins = pe.matmul(bank[r, at:at + m], v[0:w, kt], tn[0:w, kt * P:kt * P + m], start=kt == 0,
                                        stop=kt == 2)
                ins.then_inc(valued, 1)

            pe.wait_ge(roped, 9 * i + 9)
            pe.wait_ge(kq_ready, 8 * i + 8)
            pe.wait_ge(v_ready, 9 * i + 9)
            for t in range(J + 2):
                if t < J:
                    scores(JOBS[t], J * i + t)
                if t < len(FILLERS):
                    f = FILLERS[t]
                    line((name, *f), f[1] % 2 * KT, TOK)
                if 1 <= t <= J:
                    turn(JOBS[t - 1], J * i + t - 1)
                if t >= 2:
                    values(JOBS[t - 2], J * i + t - 2)
            for m in range(KT):
                for n in range(2):
                    pe.wait_ge(y_ready, 2 * i + n + 1)
                    line((name, ("ya", "yb")[n], m), m % 2 * KT + n * PAIRS, TOK, PAIRS, (y_hi, y_lo), n * PAIRS)
            pe.wait_ge(x_ready, X_BATCH[f"mixed{i}"] + KT)
            for m in range(KT):
                line((name, "out", m), m % 2 * KT, TOK)

        pe.wait_ge(set_up, 2)
        pe.wait_ge(loaded, 64)
        for i in range(DEPTH):
            layer(i)
        sums(("final0", "norm"), [wide[:, k, 0:SEQ] for k in range(KT)], mean_dm[:, :])

        def norm_sums(name):
            sums((name, "norm"), [wide[:, k, 0:SEQ] for k in range(KT)], mean_dm[:, :])

        def ffn(f):
            name = f"ffn{f}"
            norm_sums(name)
            pe.wait_ge(x_ready, X_BATCH[name] + KT)
            for j in range(FT):
                line((name, "gate", j), 0, SEQ)
                line((name, "up", j), KT, SEQ)
            for m in range(KT):
                for half in range(2):
                    pe.wait_ge(act_ready, FT * f + FT // 2 * (1 + half))
                    line((name, "down", m, half), 0, SEQ, FT // 2, (act_hi, act_lo), half * FT // 2)

        ffn(0)

        norm_sums("mixer")
        pe.wait_ge(x_ready, X_BATCH["mixer"] + KT)
        line(("mixer", "low"), 0, SEQ)
        for t in range(TILES):
            key = ("mixer", "index_w", t)
            hi, lo = unit(UNIT[key])
            exact(line_open(key)[:, 0:SH], [(token_tile(x_hi, k, t), token_tile(x_lo, k, t), hi[:, k, 32:32 + SH],
                                             lo[:, k, 32:32 + SH]) for k in range(KT)]).then_inc(line_done, 1)
        line(("mixer", "ckv"), KT, SEQ)
        pe.wait_ge(loaded2, 48)
        pe.wait_ge(low_ready, 1)
        for i in range(GH // 2):
            bank = score_open(("mixer", "alpha", i))
            for g in range(2 * i, 2 * i + 2):
                ins = pe.matmul(bank[:, g % 2 * SEQ:(g % 2 + 1) * SEQ],
                                operand("alpha_w", LOWRANK)[:, g * GDK:(g + 1) * GDK], low[0:LOWRANK],
                                start=True, stop=True)
            ins.then_inc(score_done, 1)
        bank = result_open(("mixer", "rel"))
        pe.matmul(bank[0:SH, :], operand("rel", 32), const("bucket", 32), start=True, stop=True).then_inc(row_done, 1)
        line(("mixer", "gk", 0), 0, SEQ)
        line(("mixer", "gk", 1), KT, SEQ)
        pe.wait_ge(means_ready, 2)
        sums(("mixer", "ckv"), [th[:, 0, 0:SEQ]], mean_p[:, :])
        line(("mixer", "gk", 2), 0, SEQ)
        line(("mixer", "gk", 3), KT, SEQ)
        for c in range(GH):
            line(("mixer", "gq", c), c % 2 * KT, SEQ)
        pe.wait_ge(ckv_ready, 1)
        pe.wait_ge(turned_rest, TURN[("mixer", "ckv")])
        for t in range(TILES):
            ins = pe.transpose(turn_bank[:, t * P:(t + 1) * P], ckv[:, t * P:(t + 1) * P], ident)
        ins.then_inc(turn_done, 1)
        for n in range(len(HALVES) + 1):
            for f in LEVEL_FILLERS[2 * n:2 * n + 2]:
                if f[0] == "gv":
                    by_token(("mixer", *f), 0, 2, lambda x, k, t=f[2]: token_tile(x, k, t))
                else:
                    line(("mixer", *f), f[1] % 2 * KT, SEQ)
            last = n == len(HALVES)
            if not last:
                pe.wait_ge(level_ready, n + 1)
            for t in range(TILES):
                bank = score_open(("mixer", "level", n, t))
                for g in range(GH):
                    at = slice(g * SEQ + t * P, g * SEQ + (t + 1) * P)
                    keys, queries = (gk, gq[:, g, t * P:(t + 1) * P]) if last else (gate_k, gate_q[:, at])
                    ins = pe.matmul(bank[:, g * P:(g + 1) * P], keys[:, at], queries, start=True, stop=True)
                ins.then_inc(score_done, 1)
        pe.wait_ge(level_ready, len(HALVES) + 1)
        for t in range(TILES):
            bank = score_open(("mixer", "kdt", t))
            for g in range(GH):
                ins = pe.transpose(bank[:, g * P:(g + 1) * P], gate_k[:, g * SEQ + t * P:g * SEQ + (t + 1) * P], ident)
            ins.then_inc(score_done, 1)
        pe.wait_ge(gv_ready, 4 * TILES)
        for g in range(GH):
            line(("mixer", "gr", 2 * g), 0, SEQ)
            for c in range(3):
                pe.wait_ge(kdt_ready, c // 2 + 1)
                bank = score_open(("mixer", "state", g, c))
                rows = slice(c % 2 * CHUNK, (c % 2 + 1) * CHUNK)
                at = (c // 2 * GH + g) * P
                pe.matmul(bank[:, 0:GDV], fall[rows, at:at + P], gv[rows, c // 2, g * GDV:(g + 1) * GDV],
                          start=True, stop=True).then_inc(score_done, 1)
            line(("mixer", "gr", 2 * g + 1), KT, SEQ)
            for e in range(2):
                bank = result_open(("mixer", "gla", g, e))
                pe.wait_ge(level_used, TILES * (len(HALVES) + 1))
                out_rows = slice(g * GDV + e * P, g * GDV + (e + 1) * P)
                for t in range(TILES):
                    pe.matmul(bank[:, t * P:(t + 1) * P], gv[:, t, out_rows], pairs[:, t, g], start=t == 0, stop=False)
                pe.wait_ge(state_ready, 3 * g + 3)
                for c in range(1, SEQ // CHUNK):
                    at = slice(c * CHUNK, (c + 1) * CHUNK)
                    ins = pe.matmul(bank[:, at], states[:, c - 1, e * P:(e + 1) * P],
                                    gate_q[:, g * SEQ + c * CHUNK:g * SEQ + (c + 1) * CHUNK], start=False,
                                    stop=c == SEQ // CHUNK - 1)
                ins.then_inc(gla_done, 1)
            sums(("mixer", "gla", g), [th[:, e, 0:SEQ] for e in range(2)], mean_gdv[:, :])

        pe.wait_ge(index_q_ready, PAIRS)
        pe.wait_ge(low_ready, 3)
        for n, (t, hd) in enumerate((t, hd) for t in range(TILES) for hd in range(SH)):
            bank = score_open(("mixer", "dots", t, hd))
            rows = slice(hd % 2 * HD, (hd % 2 + 1) * HD)
            pe.matmul(bank[:, 0:(t + 1) * P], index_q[rows, hd // 2, t * P:(t + 1) * P], index_k[rows, 0:(t + 1) * P],
                      start=True, stop=True).then_inc(score_done, 1)
            if n % 2:
                line(("mixer", "dq", n // 2), n // 2 % 2 * KT, SEQ)

        def dsa_scores(i):
            hd, t = DSA_JOBS[i]
            bank = score_open(("mixer", "dsa", hd, t))
            pe.wait_ge(dq_ready, hd + 1)
            keys = (t + 1) * P
            pe.matmul(bank[:, 0:keys], dq[:, hd, t * P:(t + 1) * P], ckv[:, 0:keys], start=True, stop=False)
            pe.wait_ge(rbias_in[hd % 2], 16 * TILES * (hd // 2 + 1))
            pe.matmul(bank[:, 0:keys], const("flip"), rbias[:, hd % 2, t * P:t * P + keys], start=False,
                      stop=True).then_inc(score_done, 1)

        def dsa_turn(i):
            hd, t = DSA_JOBS[i]
            n = DEPTH * J + i
            pe.wait_ge(probs_ready, n + 1)
            pe.wait_ge(turned_most, TURN[("mixer", "dsa", hd, t)])
            for kt in range(t + 1):
                ins = pe.transpose(turn_bank[:, kt * P:(kt + 1) * P], probs[:, n % 2, kt * P:(kt + 1) * P], ident)
            ins.then_inc(turn_done, 1)

        def dsa_values(i):
            hd, t = DSA_JOBS[i]
            n, key = DEPTH * J + i, ("mixer", "dsa", hd)
            bank = result_open(key) if t == 0 else result_bank[RESULT[key] % 2]
            pe.wait_ge(turned_most, TURN[("mixer", "dsa", hd, t)] + 1)
            for kt in range(t + 1):
                ins = pe.matmul(bank[:, t * P:(t + 1) * P], ckv_t[:, kt], turned[:, n % 2, kt * P:(kt + 1) * P],
                                start=kt == 0, stop=kt == t)
            ins.then_inc(valued, 1)

        for i in range(len(DSA_JOBS) + 2):
            if i < len(DSA_JOBS):
                dsa_scores(i)
                line(("mixer", ("mg", "ms")[i // KT], i % KT), i % 2 * KT, SEQ)
            if 1 <= i <= len(DSA_JOBS):
                dsa_turn(i - 1)
            if i >= 2:
                dsa_values(i - 2)
        pe.wait_ge(gg_ready, KT)
        for m in range(KT):
            line(("mixer", "yg", m), 0, SEQ, KT, (gg_hi, gg_lo))
            if m == 0:
                pe.wait_ge(od_ready, SH)
            line(("mixer", "ys", m), KT, SEQ, KT, (od_hi, od_lo))
        pe.wait_ge(x_ready, X_BATCH["mixed2"] + KT)
        for m in range(KT):
            line(("mixer", "mix", m), m % 2 * KT, SEQ)

        ffn(1)
        norm_sums("embed")
        pe.wait_ge(p_ready, 1)
        for m in range(KT):
            line(("embed", "pp", m), 2 * m, SEQ, 2, (p_hi, p_lo))
        pe.wait_ge(x_ready, X_BATCH["embed"] + KT)
        for m in range(KT):
            line(("embed", "pg", m), m % 2 * KT, SEQ)
        norm_sums("final1")

    al.close()


def pair_heads(width=HD):
    return np.concatenate([np.r_[c * width:(c + 1) * width, (c + PAIRS) * width:(c + PAIRS + 1) * width]
                           for c in range(PAIRS)])


def blocks_of(w):
    k, n = w.shape
    return w.reshape(k // P, P, n // P, P).transpose(1, 2, 0, 3).reshape(P, -1)


def weight_stream(a):
    rows = []
    cols = np.cumsum([0, 512, 128, 128, 512, 512, 512, 512, 512, 1024, 1024])
    heads = pair_heads()
    for i in range(DEPTH):
        qa, ka, va, za, qb, kb, vb, zb, ga, gb = (a["w_in"][i][:, cols[j]:cols[j + 1]] for j in range(10))
        rows += [blocks_of(w) for w in (ka, va, qa[:, heads], kb, qb, vb, za[:, heads], zb, ga, gb)]
        rows += [blocks_of(np.concatenate([a["w_o_attn"][i][heads], a["w_o_na"][i]])), blocks_of(a["w_out"][i])]

    def ffn(w_in, w_out):
        both = np.stack([w_in[:, :DFF].reshape(DM, FT, P), w_in[:, DFF:].reshape(DM, FT, P)], 2)
        down = blocks_of(w_out).reshape(P, 2 * KT, FT // 2 * P)
        down = np.pad(down, ((0, 0), (0, 0), (0, (UB - FT // 2) * P)))
        return [blocks_of(both.reshape(DM, 2 * DFF)), down.reshape(P, -1)]

    rows += ffn(a["ffn1_w_in_2"][0], a["ffn1_w_out_2"][0])
    sizes = (GH * GDK, GH * GDK, GH * GDV, GH * GDV, LOWRANK, SH * P, P, SH * HD, HD, SH, 2 * DM)
    cols = np.cumsum((0,) + sizes)
    gq, gk, gv, gr, ga, dq, dkv, iq, ik, iw, gates = (a["mix_w_in_2"][0][:, cols[j]:cols[j + 1]] for j in range(11))
    low = np.zeros((DM, P), np.float32)
    low[:, :LOWRANK], low[:, 32:32 + SH], low[:, HD:] = ga, iw, ik
    rows += [blocks_of(w) for w in (low, dkv, gk, gq, gv, iq, gr, dq, gates)]
    outs = np.stack([a["gla_w_out_2"][0].reshape(DM, KT, P), a["dsa_w_out_2"][0].reshape(DM, KT, P)], 2)
    rows += [blocks_of(outs.reshape(DM, 2 * DM)), blocks_of(a["mix_w_out_2"][0])]
    rows += ffn(a["ffn2_w_in_2"][0], a["ffn2_w_out_2"][0])
    rows += [blocks_of(a["ple_w_proj_2"][0]), blocks_of(a["ple_w_gate_2"][0])]
    return np.ascontiguousarray(np.concatenate(rows, 1).reshape(P, len(UNITS), UB * P).transpose(1, 0, 2))


def by_feature(v):
    return v.reshape(-1, P).T


def small_operands(a):
    s, s2 = np.zeros((P, SMALL_W), np.float32), np.zeros((P, SMALL2_W), np.float32)

    def put(name, v):
        at, w = (SMALL.get(name) or SMALL2[name])
        (s if name in SMALL else s2)[:v.shape[0], at:at + w] = v

    gains = dict(layer0=a["norm_g"][0], layer1=a["norm_g"][1], final0=a["final_norm_g"], ffn0=a["ffn1_norm_2"][0],
                 mixer=a["mix_norm_2"][0], ffn1=a["ffn2_norm_2"][0], embed=a["ple_norm_2"][0], final1=a["final_norm_2"])
    for name, g in gains.items():
        put(f"g_{name}", by_feature(g))
    for i in range(DEPTH):
        put(f"q_gain{i}", np.tile(a["q_norm_g"][i], 2)[:, None])
        put(f"k_gain{i}", np.tile(a["k_norm_g"][i], 2)[:, None])
    put("gla_gain", by_feature(a["gla_out_norm_2"][0]))
    put("ckv_gain", by_feature(a["ckv_norm_2"][0]))
    put("alpha_b", by_feature(a["gla_alpha_b_2"][0]))
    put("alpha_w", a["gla_alpha_w_2"][0])
    put("rel", a["rel_bias_2"])
    return s, s2


def constants():
    c, c2 = np.zeros((P, CONST_W), np.float32), np.zeros((P, CONST2_W), np.float32)

    def put(name, v):
        at, w = (CONST.get(name) or CONST2[name])
        (c if name in CONST else c2)[:v.shape[0], at:at + w] = v

    p = np.arange(P)
    put("ident", np.eye(P))
    put("flip", np.eye(P)[::-1])
    put("head_mean", (p[:, None] // HD == p[None] // HD) / HD)
    quarter = HD // 4
    rot = np.zeros((P, P))
    for m in range(P):
        low = m % (2 * quarter) < quarter
        rot[m + quarter if low else m - quarter, m] = -1.0 if low else 1.0
    put("rot", rot)
    t = np.arange(SEQ)
    zeros = np.zeros(META)
    row = np.concatenate([t // GRID_W, zeros]).astype(np.float32)
    col = np.concatenate([t % GRID_W, zeros]).astype(np.float32)
    inv = np.float32(10000.0) ** (-np.arange(0, HD // 2, 2, dtype=np.float32) / np.float32(HD // 2))
    ang = np.concatenate([np.tile(row[:, None] * inv, 2), np.tile(col[:, None] * inv, 2)], 1).astype(np.float32)
    put("cos", np.tile(np.cos(ang).T, (2, 1)))
    put("sin", np.tile(np.sin(ang).T, (2, 1)))
    g = np.arange(GRID_W)
    start = np.clip(g - WIN // 2, 0, GRID_W - WIN)[:, None]
    put("window", np.tile(np.where((g[None] >= start) & (g[None] < start + WIN), 0.0, NEG)[::-1], (2, 1)))
    put("keep", np.tile((np.arange(GH * SEQ) % CHUNK != 0)[None], (P, 1)))
    put("later", np.where(p[None] <= p[:, None], 0.0, NEG))
    d = np.maximum(SEQ - 1 - np.arange(2 * SEQ), 0)
    half = 16
    ratio = np.maximum(d, 1).astype(np.float32) / np.float32(half)
    large = half + (np.log(ratio) / np.float32(np.log(128 / half)) * np.float32(half)).astype(np.int32)
    bucket = np.where(d < half, d, np.minimum(large, 31))
    put("bucket", np.arange(32)[:, None] == bucket[None])
    return c, c2


def level_masks():
    s, t = np.arange(P)[:, None], np.arange(P)[None]
    m = [(s // (2 * h) == t // (2 * h)) & (s // h % 2 == 0) & (t // h % 2 == 1) for h in HALVES] + [s == t]
    return np.ascontiguousarray(np.stack(m, 1).astype(np.uint32))


def kernel(**inputs):
    import concourse.bacc as bacc
    from concourse.bass_utils import run_bass_kernel_spmd

    a = {n: np.asarray(v) for n, v in inputs.items()}
    tokens = np.concatenate([a["x"][0], a["meta_tokens"]])
    arrays = {
        "weights": weight_stream(a),
        "tokens": np.ascontiguousarray(tokens.reshape(TOK, KT, P).transpose(2, 1, 0)),
        "embeds": np.ascontiguousarray(a["p_2"][0, 0].reshape(SEQ, -1, P).transpose(2, 1, 0)),
        "small": small_operands(a)[0],
        "small2": small_operands(a)[1],
        "rpb": np.ascontiguousarray(a["na_rpb"]),
        "consts": constants()[0],
        "consts2": constants()[1],
        "levels": level_masks(),
    }
    nc = bacc.Bacc("TRN2", target_bir_lowering=False, num_devices=1)
    arrays = {f"in_{n}": v for n, v in arrays.items()}
    args = [nc.dram_tensor(n, v.shape, mybir.dt.from_np(v.dtype), kind="ExternalInput").ap() for n, v in arrays.items()]
    out = nc.dram_tensor("out", (P, KT, SEQ), F32, kind="ExternalOutput").ap()
    hybrid_blocks_kernel(nc, *args, out)
    r = run_bass_kernel_spmd(nc, [arrays], core_ids=[0])
    y = r.results[0]["out"]
    return np.ascontiguousarray(y.transpose(2, 1, 0)).reshape(1, SEQ, DM)
```

```python
from contextlib import ExitStack

import numpy as np

import concourse.bass as bass
from concourse import mybir

P = 128
DM = 1024
KT = DM // P
EPS = 1e-6
F32 = mybir.dt.float32
F32R = mybir.dt.float32r
U32 = mybir.dt.uint32
ALU = mybir.AluOpType
ACT = mybir.ActivationFunctionType
AX = mybir.AxisListType

DEPTH = 2
SEQ = 256
META = 16
TOK = SEQ + META
HD = 64
HEADS = 8
PAIRS = HEADS // 2
GRID_W = 64
ROWS = SEQ // GRID_W
WIN = 16
RPB_R, RPB_C = 15, 31
NEG = -1.0e30
TILES = SEQ // P

DFF = 2816
FT = DFF // P
GH, GDK, GDV, CHUNK = 4, 128, 256, 64
LOWRANK, TAU = 16, 16.0
SH = 8
TOPK = min(256, SEQ // 4)
HALVES = (32, 16, 8, 4, 2, 1)
TAKEN = -3.0e38

RAW = 3
CUT = 3
UB = 16


def key_tiles(n):
    return [(i, min(P, n - i * P)) for i in range((n + P - 1) // P)]


def units_of_layer():
    u = [[("ka",), ("va",)]]
    for name in ("qa", "kb", "qb"):
        u += [[(name, 2 * i), (name, 2 * i + 1)] for i in range(2)]
    for name in ("vb", "za", "zb"):
        u += [[(name, 2 * i), (name, 2 * i + 1)] for i in range(2)]
    for name in ("ga", "gb"):
        u += [[(name, 2 * i), (name, 2 * i + 1)] for i in range(4)]
    u += [[(name, 4 * i + j) for j in range(4)] for name in ("ya", "yb") for i in range(2)]
    u += [[("out", 2 * i), ("out", 2 * i + 1)] for i in range(4)]
    return u


def units_of_ffn():
    return [[("gate", j), ("up", j)] for j in range(FT)] + [
        [("down", m, half)] for m in range(KT) for half in range(2)]


def units_of_mixer():
    u = [[("low",), ("ckv",)]]
    for name in ("gk", "gq"):
        u += [[(name, 2 * i), (name, 2 * i + 1)] for i in range(2)]
    for name, n in (("gv", 8), ("iq", 4), ("gr", 8), ("dq", 8), ("mg", 8), ("ms", 8), ("yg", 8), ("ys", 8),
                    ("mix", 8)):
        u += [[(name, 2 * i), (name, 2 * i + 1)] for i in range(n // 2)]
    return u


def units_of_embedding():
    return [[("pp", m) for m in range(KT)]] + [[("pg", 2 * i), ("pg", 2 * i + 1)] for i in range(4)]


def plan():
    stages = {}
    units = []
    for stage, u in ([(f"layer{i}", units_of_layer()) for i in range(DEPTH)]
                     + [("ffn0", units_of_ffn()), ("mixer", units_of_mixer()), ("ffn1", units_of_ffn()),
                        ("embed", units_of_embedding())]):
        stages[stage] = len(units)
        units += [[(stage, *g) for g in unit] for unit in u]
    blocks = [UB] * len(units)
    for s in ("ffn0", "ffn1"):
        for i in range(2 * KT):
            blocks[stages[s] + FT + i] = FT // 2
    return stages, units, blocks


STAGES, UNITS, BLOCKS = plan()
LINES = [g for unit in UNITS for g in unit]
LINE = {g: i for i, g in enumerate(LINES)}
UNIT = {g: u for u, unit in enumerate(UNITS) for g in unit}


def last_line(u):
    return LINE[UNITS[u][-1]]


def attention_jobs():
    a = [("A", c, half, t) for c in range(PAIRS) for half in range(2) for t in range(TILES)]
    b = [("B", c, half, t) for c in range(PAIRS) for half in range(2) for t in range(TILES)]
    return a[:4] + [("Am", 0), ("Am", 1)] + a[4:] + [("Bm",)] + b


JOBS = attention_jobs()


def tile_done(job):
    if job == ("Am", 1):
        return 0
    if len(job) == 4 and job[2:] == (1, TILES - 1) and job[:2] != ("A", 0):
        return PAIRS * (job[0] == "B") + job[1]
    return None


FILLERS = [(n, m) for n, k in (("za", 4), ("zb", 4), ("ga", 8), ("gb", 8), ("ya", 8)) for m in range(k)]
GATES = sum(f[0] != "ya" for f in FILLERS)

STATS = []
for _l in range(DEPTH):
    STATS += [(f"layer{_l}", "norm")] + [(f"layer{_l}", "head", i) for i in range(PAIRS + 1)]
STATS += [("ffn0", "norm"), ("final0", "norm"), ("mixer", "norm"), ("mixer", "ckv")]
STATS += [("mixer", "gla", h) for h in range(GH)] + [("ffn1", "norm"), ("embed", "norm"), ("final1", "norm")]
STAT = {k: i for i, k in enumerate(STATS)}
NORMS = ["layer0", "layer1", "final0", "ffn0", "mixer", "ffn1", "embed", "final1"]

SCORES = [(f"layer{_l}", *j) for _l in range(DEPTH) for j in JOBS]
SCORES += [("mixer", "alpha", i) for i in range(2)]
SCORES += [("mixer", "level", n, t) for n in range(len(HALVES) + 1) for t in range(TILES)]
SCORES += [("mixer", "kdt", t) for t in range(TILES)]
SCORES += [("mixer", "state", h, c) for h in range(GH) for c in range(3)]
SCORES += [("mixer", "dots", t, h) for t in range(TILES) for h in range(SH)]
SCORES += [("mixer", "dsa", h, t) for h in range(SH) for t in range(TILES)]
SCORE = {k: i for i, k in enumerate(SCORES)}

RESULTS = []
for _l in range(DEPTH):
    RESULTS += [(f"layer{_l}", "rot", i) for i in range(PAIRS + 1)]
    RESULTS += [(f"layer{_l}", "A", 0), (f"layer{_l}", "Am")] + [(f"layer{_l}", "A", c) for c in range(1, PAIRS)]
    RESULTS += [(f"layer{_l}", "Bm")] + [(f"layer{_l}", "B", c) for c in range(PAIRS)]
RESULTS += [("mixer", "index_w"), ("mixer", "rel")]
RESULTS += [("mixer", "gla", h, e) for h in range(GH) for e in range(2)]
RESULTS += [("mixer", "dsa", h) for h in range(SH)]
RESULT = {k: i for i, k in enumerate(RESULTS)}

TURNS = [(f"layer{_l}", *j) for _l in range(DEPTH) for j in JOBS]
TURNS += [("mixer", "ckv")] + [("mixer", "dsa", h, t) for h in range(SH) for t in range(TILES)]
TURN = {k: i for i, k in enumerate(TURNS)}



def columns(widths):
    at, places = 0, {}
    for name, w in widths:
        places[name] = (at, w)
        at += w
    return places, at


SMALL, SMALL_W = columns([(f"g_{n}", KT) for n in NORMS] + [(f"q_gain{i}", 1) for i in range(DEPTH)]
                         + [(f"k_gain{i}", 1) for i in range(DEPTH)])
SMALL2, SMALL2_W = columns([("gla_gain", KT), ("ckv_gain", 1), ("alpha_b", GH), ("alpha_w", GH * GDK), ("rel", SH)])
CONST, CONST_W = columns([("ident", P), ("flip", P), ("head_mean", P), ("rot", P), ("cos", TOK), ("sin", TOK), ("window", GRID_W)])
CONST2, CONST2_W = columns([("keep", GH * SEQ), ("later", P), ("bucket", 2 * SEQ)])


SQUARES, _n = {}, 0
for _k in STATS:
    SQUARES[_k] = _n
    _n += {"norm": KT, "head": 1, "ckv": 1, "gla": 2}[_k[1]]
SQUARES[("final0", "norm")] = SQUARES[("ffn0", "norm")]
X_BATCH = {k: KT * i for i, k in enumerate(["layer0", "mixed0", "layer1", "mixed1", "ffn0", "mixer", "mixed2", "ffn1",
                                            "embed"])}
FULL_BATCH = {k: KT * i for i, k in enumerate(["mixed0", "mixed1", "final0", "mixed2"])}
H_BATCH = {k: KT * i for i, k in enumerate(["layer0", "layer1", "final0", "ffn0", "mixer", "ffn1", "embed"])}
READS = {"layer1": "layer0", "final0": "layer1", "mixer": "ffn0", "ffn1": "mixer", "embed": "ffn1",
         "final1": "embed"}
SUMMED, _n = {}, 0
for _k in ("layer0", "layer1", "final0", "mixer", "ffn1", "embed", "final1"):
    SUMMED[_k] = _n
    _n += KT * (2 if _k == "final0" else 1)
J = len(JOBS)
TURN_OF_JOB = [i for i, k in enumerate(TURNS) if k != ("mixer", "ckv")]
NU = len(UNITS)


LINE_READ, SCORE_READ, RESULT_READ = {}, {}, {}
for _i in range(DEPTH):
    _l = f"layer{_i}"
    for _c in range(PAIRS + 1):
        LINE_READ[(_l, "qa", _c - 1) if _c else (_l, "ka")] = ("raw_head", 5 * _i + _c + 1)
        LINE_READ[(_l, "vb", _c - 1) if _c else (_l, "va")] = ("v_raw", 5 * _i + _c + 1)
        RESULT_READ[(_l, "rot", _c)] = ("rot_used", 5 * _i + _c + 1)
    for _n, _f in enumerate(FILLERS[:GATES]):
        LINE_READ[(_l, *_f)] = ("gate_raw", GATES * _i + _n + 1)
    for _c in range(PAIRS):
        for _n in range(2):
            LINE_READ[(_l, ("kb", "qb")[_n], _c)] = ("kq_ready", 8 * _i + 4 * _n + _c + 1)
            RESULT_READ[(_l, "AB"[_n], _c)] = ("pair_gated", 8 * _i + 4 * _n + _c + 1)
            RESULT_READ[(_l, "AB"[_n] + "m")] = ("gated", 2 * _i + _n + 1)
    for _m in range(KT):
        for _n in range(2):
            LINE_READ[(_l, ("ya", "yb")[_n], _m)] = ("y_used", 16 * _i + KT * _n + _m + 1)
        LINE_READ[(_l, "out", _m)] = ("h_ready", H_BATCH[_l] + _m + 1)
    for _n, _j in enumerate(JOBS):
        SCORE_READ[(_l, *_j)] = ("maxed" if _j[0] == "Bm" else "exped", J * _i + _n + 1)
for _f in range(2):
    for _n in range(FT):
        LINE_READ[(f"ffn{_f}", "gate", _n)] = ("act_raw", FT * _f + _n + 1)
        LINE_READ[(f"ffn{_f}", "up", _n)] = ("act_up", FT * _f + _n + 1)
    for _m in range(KT):
        LINE_READ[(f"ffn{_f}", "down", _m, 0)] = ("down_used", KT * _f + _m + 1)
        LINE_READ[(f"ffn{_f}", "down", _m, 1)] = ("h_ready", H_BATCH[f"ffn{_f}"] + _m + 1)
_m = "mixer"
LINE_READ[(_m, "low")] = ("low_ready", 1)
LINE_READ[(_m, "ckv")] = ("ckv_raw", 1)
RESULT_READ[(_m, "index_w")] = ("index_w_ready", 1)
RESULT_READ[(_m, "rel")] = ("row_ready", 1)
for _t in range(TILES):
    SCORE_READ[(_m, "alpha", _t)] = ("alpha_used", 2 * _t + 2)
    SCORE_READ[(_m, "kdt", _t)] = ("kdt_ready", _t + 1)
    for _n in range(len(HALVES) + 1):
        SCORE_READ[(_m, "level", _n, _t)] = ("level_used", TILES * _n + _t + 1)
    for _h in range(SH):
        SCORE_READ[(_m, "dots", _t, _h)] = ("relued", SH * _t + _h + 1)
        SCORE_READ[(_m, "dsa", _h, _t)] = ("exped", DEPTH * J + TILES * _h + _t + 1)
for _n in range(4):
    LINE_READ[(_m, "gk", _n)] = ("gla_in", _n + 1)
    LINE_READ[(_m, "gq", _n)] = ("gla_in", GH + _n + 1)
    LINE_READ[(_m, "iq", _n)] = ("index_q_ready", _n + 1)
    for _t in range(3):
        SCORE_READ[(_m, "state", _n, _t)] = ("state_ready", 3 * _n + _t + 1)
    for _t in range(2):
        RESULT_READ[(_m, "gla", _n, _t)] = ("squares_ready", SQUARES[(_m, "gla", _n)] + _t + 1)
for _n in range(KT):
    LINE_READ[(_m, "gv", _n)] = ("gv_raw", _n + 1)
    LINE_READ[(_m, "gr", _n)] = ("gr_raw", _n + 1)
    LINE_READ[(_m, "dq", _n)] = ("dq_ready", _n + 1)
    LINE_READ[(_m, "mg", _n)] = ("gate_raw", GATES * DEPTH + _n + 1)
    LINE_READ[(_m, "ms", _n)] = ("gate_raw", GATES * DEPTH + KT + _n + 1)
    LINE_READ[(_m, "yg", _n)] = ("y_used", 16 * DEPTH + _n + 1)
    LINE_READ[(_m, "ys", _n)] = ("y_used", 16 * DEPTH + KT + _n + 1)
    LINE_READ[(_m, "mix", _n)] = ("h_ready", H_BATCH[_m] + _n + 1)
    RESULT_READ[(_m, "dsa", _n)] = ("od_ready", _n + 1)
    LINE_READ[("embed", "pp", _n)] = ("pp_ready", _n + 1)
    LINE_READ[("embed", "pg", _n)] = ("pg_raw", _n + 1)
assert set(LINE_READ) == set(LINES) and set(SCORE_READ) == set(SCORES) and set(RESULT_READ) == set(RESULTS)

LEVEL_FILLERS = [("gv", n) for n in range(8)] + [("iq", c) for c in range(4)]
DSA_FILLERS = [("ms", n) for n in range(KT)] + [("yg", n) for n in range(KT)]
DSA_JOBS = [(h, t) for h in range(SH) for t in range(TILES)]


class Alloc:

    def __init__(self, nc):
        self.nc, self.stack = nc, ExitStack()

    def sb(self, name, shape, dt=F32):
        return self.stack.enter_context(self.nc.sbuf_tensor(name, [P, *shape], dt))

    def bank(self, name):
        return self.stack.enter_context(self.nc.psum_tensor(name, [P, 512], F32))

    def sem(self, name):
        return self.stack.enter_context(self.nc.semaphore(name))

    def close(self):
        self.stack.close()


def hybrid_blocks_kernel(nc, weights, tokens, embeds, small_in, small2_in, rpb, consts_in, consts2_in, levels_in,
                         out):
    al = Alloc(nc)
    sb, sem = al.sb, al.sem

    raw = sb("raw", [RAW, UB * P])
    w_hi = sb("w_hi", [CUT, UB * P], F32R)
    w_lo = sb("w_lo", [CUT, UB * P], F32R)
    h = sb("h", [KT, TOK])
    x_hi = sb("x_hi", [KT, TOK], F32R)
    x_lo = sb("x_lo", [KT, TOK], F32R)
    y_hi = sb("y_hi", [KT, TOK], F32R)
    y_lo = sb("y_lo", [KT, TOK], F32R)
    wide = sb("wide", [KT, TOK])
    scale = sb("scale", [TOK])
    root = sb("root", [2, TOK])
    rstd = sb("rstd", [2, TOK])
    consts = sb("consts", [CONST_W])
    small = sb("small", [SMALL_W])
    q_gain = sb("q_gain", [DEPTH])
    mean_dm = sb("mean_dm", [P])
    eps = sb("eps", [1])
    th = sb("th", [2, TOK])
    prod = sb("prod", [2, TOK])
    prod2 = sb("prod2", [2, TOK])
    probs = sb("probs", [2, TOK])
    turned = sb("turned", [2, 3 * P])
    top = sb("top", [2, 8])
    total = sb("total", [2, 8])
    share = sb("share", [2, 8])
    best = sb("best", [8])
    warm = sb("warm", [1])

    def const(name, rows=P):
        at, w = (CONST.get(name) or CONST2[name])
        return (consts if name in CONST else consts2)[0:rows, at:at + w]

    def operand(name, rows=P):
        at, w = (SMALL.get(name) or SMALL2[name])
        return (small if name in SMALL else small2)[0:rows, at:at + w]

    line_bank = [al.bank(f"line{i}") for i in range(2)]
    stat_bank = al.bank("stat")
    score_bank = [al.bank(f"score{i}") for i in range(2)]
    turn_bank = al.bank("turn")
    result_bank = [al.bank(f"result{i}") for i in range(2)]

    raw_in = [sem(f"raw_in{i}") for i in range(RAW)]
    hi_cut, lo_cut = sem("hi_cut"), sem("lo_cut")
    small_loaded, index_k_ready = sem("small_loaded"), sem("index_k_ready")
    tokens_in = [sem(f"tokens_in{i}") for i in range(2)]
    loaded, loaded2, masks_in = sem("loaded"), sem("loaded2"), sem("masks_in")
    embeds_in = sem("embeds_in")
    rel_in = [sem(f"rel_in{i}") for i in range(2)]
    rel_ready = sem("rel_ready")
    set_up = sem("set_up")
    gains_ready = sem("gains_ready")
    line_done = sem("line_done")
    squares_ready, stat_done, root_ready = sem("squares_ready"), sem("stat_done"), sem("root_ready")
    stat_read, summed, mean_ready, scaled = sem("stat_read"), sem("summed"), sem("mean_ready"), sem("scaled")
    full_ready, x_hi_ready, x_ready, h_ready = sem("full_ready"), sem("x_hi_ready"), sem("x_ready"), sem("h_ready")
    raw_head, normed, rot_done, roped = sem("raw_head"), sem("normed"), sem("rot_done"), sem("roped")
    kq_ready, v_raw, v_turned, v_ready = sem("kq_ready"), sem("v_raw"), sem("v_turned"), sem("v_ready")
    score_done = sem("score_done")
    maxed, exped, probs_ready = sem("maxed"), sem("exped"), sem("probs_ready")
    turn_done, turned_most, turned_rest = sem("turn_done"), sem("turned_most"), sem("turned_rest")
    valued, even_scores = sem("valued"), sem("even_scores")
    rot_used, pair_gated, y_used = sem("rot_used"), sem("pair_gated"), sem("y_used")
    act_raw, act_up, act_half, down_used = sem("act_raw"), sem("act_up"), sem("act_half"), sem("down_used")
    gate_raw, tanh_ready, gates_ready = sem("gate_raw"), sem("tanh_ready"), sem("gates_ready")
    gated, y_hi_ready, y_ready = sem("gated"), sem("y_hi_ready"), sem("y_ready")
    act_full, act_hi_ready, act_ready = sem("act_full"), sem("act_hi_ready"), sem("act_ready")
    dve_step = sem("dve_step")
    act_tanh, out_ready = sem("act_tanh"), sem("out_ready")
    low_ready, index_w_ready, index_q_ready = sem("low_ready"), sem("index_w_ready"), sem("index_q_ready")
    row_done = sem("row_done")
    row_ready, row_stored = sem("row_ready"), sem("row_stored")
    rbias_in = [sem(f"rbias_in{i}") for i in range(2)]
    ckv_raw, ckv_ready = sem("ckv_raw"), sem("ckv_ready")
    alpha_used, soft_in, soft_out = sem("alpha_used"), sem("soft_in"), sem("soft_out")
    soft_step = sem("soft_step")
    gla_in, gv_raw, gv_turned, gv_ready = sem("gla_in"), sem("gv_raw"), sem("gv_turned"), sem("gv_ready")
    fallen, risen, gr_raw, index_w_turned = sem("fallen"), sem("risen"), sem("gr_raw"), sem("index_w_turned")
    grown_ready, level_ready, level_used = sem("grown_ready"), sem("level_ready"), sem("level_used")
    kdt_ready, state_ready, gla_done, gla_raw = sem("kdt_ready"), sem("state_ready"), sem("gla_done"), sem("gla_raw")
    gla_full, gg_hi_ready, gg_ready = sem("gla_full"), sem("gg_hi_ready"), sem("gg_ready")
    dq_ready, relued, scored, selected = sem("dq_ready"), sem("relued"), sem("scored"), sem("selected")
    od_hi_ready, od_ready = sem("od_hi_ready"), sem("od_ready")
    p_hi_ready, p_ready, pp_ready = sem("p_hi_ready"), sem("p_ready"), sem("pp_ready")
    pg_raw, pg_used = sem("pg_raw"), sem("pg_used")
    means_ready = sem("means_ready")
    gate_ready = sem("gate_ready")
    stored = sem("stored")
    first, second = (x_hi, x_lo), (y_hi, y_lo)
    x_of = dict(layer0=first, mixed0=first, layer1=second, mixed1=second, ffn0=first, mixer=first, mixed2=first,
                ffn1=second, embed=first)
    y_of = dict(layer0=second, layer1=first)
    names = ("layer0", "layer1", "final0", "mixer", "ffn1", "embed", "final1")
    square_of = {n: th if n != "final1" else probs for n in names}
    sum_of = {n: (prod2[:, 0], prod2[:, 1]) for n in names} | {"final1": (root[:, 1 - STAT[("final1", "norm")] % 2],)}
    signals = dict(squares_ready=squares_ready, raw_head=raw_head, v_raw=v_raw, kq_ready=kq_ready, gate_raw=gate_raw,
                   y_used=y_used, h_ready=h_ready, act_raw=act_raw, act_up=act_up, down_used=down_used, exped=exped,
                   maxed=maxed, rot_used=rot_used, pair_gated=pair_gated, gated=gated, low_ready=low_ready,
                   ckv_raw=ckv_raw, row_ready=row_ready, index_w_ready=index_w_ready, alpha_used=alpha_used,
                   kdt_ready=kdt_ready, level_used=level_used, gv_raw=gv_raw, gr_raw=gr_raw, relued=relued,
                   gla_in=gla_in, index_q_ready=index_q_ready, state_ready=state_ready, dq_ready=dq_ready,
                   od_ready=od_ready, pp_ready=pp_ready, pg_raw=pg_raw)
    row_dram = nc.dram_tensor("bias_by_distance", (SH, 2 * SEQ), F32).ap()

    a1 = Alloc(nc)
    gate = {n: a1.sb(f"gate_{n}", [KT, TOK]) for n in "ab"}
    silu = {n: a1.sb(f"silu_{n}", [PAIRS, TOK]) for n in "ab"}
    qa = a1.sb("qa", [PAIRS, TOK])
    ka = a1.sb("ka", [TOK])
    q_meta = a1.sb("q_meta", [PAIRS * META])
    qb = a1.sb("qb", [PAIRS, TOK])
    kb = a1.sb("kb", [PAIRS, TOK])
    va = a1.sb("va", [3, P])
    vb = a1.sb("vb", [3, HEADS * HD])
    rel = a1.sb("rel", [2, TILES, 2, SEQ])
    a1.close()
    a2 = Alloc(nc)
    consts2 = a2.sb("consts2", [CONST2_W])
    small2 = a2.sb("small2", [SMALL2_W])
    gla_gain = a2.sb("gla_gain", [KT])
    mean_gdv = a2.sb("mean_gdv", [P])
    mean_p = a2.sb("mean_p", [P])
    levels = a2.sb("levels", [len(HALVES) + 1, P], U32)
    p_in = turned[:, :, 0:SEQ]
    p_hi = a2.sb("p_hi", [2, SEQ], F32R)
    p_lo = a2.sb("p_lo", [2, SEQ], F32R)
    pp = wide[:, :, 0:SEQ]
    a3 = Alloc(nc)
    act_hi = a3.sb("act_hi", [FT, SEQ], F32R)
    act_lo = a3.sb("act_lo", [FT, SEQ], F32R)
    a3.close()
    a3 = Alloc(nc)
    gg_hi, gg_lo = y_hi[:, :, 0:SEQ], y_lo[:, :, 0:SEQ]
    low = turned[:, 0, 0:SEQ]
    index_k = a3.sb("index_k", [SEQ])
    index_q = a3.sb("index_q", [PAIRS, SEQ])
    index_w = a3.sb("index_w", [TILES, SH])
    ckv = a3.sb("ckv", [SEQ])
    ckv_t = a3.sb("ckv_t", [TILES, P])
    a4 = Alloc(nc)
    gk_decay = a4.sb("gk_decay", [2, GH * SEQ])
    gk, decay = gk_decay[:, 0], gk_decay[:, 1]
    gr = gk_decay[:, :, :].rearrange("p a (k t) -> p (a k) t", t=SEQ)
    gq, grown = wide[:, 0:GH, 0:SEQ], wide[:, GH:2 * GH, 0:SEQ]
    fall = a4.sb("fall", [GH * SEQ])
    gate_q = a4.sb("gate_q", [GH * SEQ])
    gate_k = a4.sb("gate_k", [GH * SEQ])
    pairs = a4.sb("pairs", [TILES, GH, P])
    gv = a4.sb("gv", [TILES, GH * GDV])
    states = a4.sb("states", [3, GDV])
    a4.close()
    a4 = Alloc(nc)
    dq = wide[:, :, 0:SEQ]
    mgate = {n: a4.sb(f"mgate_{n}", [KT, SEQ]) for n in "gs"}
    od_hi = a4.sb("od_hi", [SH, SEQ], F32R)
    od_lo = a4.sb("od_lo", [SH, SEQ], F32R)
    rbias = a4.sb("rbias", [2, SEQ + P])
    score = root[:, :, 0:SEQ]
    work = prod2[:, :, 0:SEQ]
    a4.close()
    bias_row = turned[0:SH].rearrange("p a b -> p (a b)")[:, SEQ:3 * SEQ]
    a3.close()
    a2.close()

    block = al.stack.enter_context(nc.Block())

    @block.sync
    def _(sp):
        def load_unit(u):
            if u >= RAW:
                sp.wait_ge(lo_cut, u - RAW + 1)
            n = BLOCKS[u] * P
            sp.dma_start(raw[:, u % RAW, 0:n], weights[u, :, 0:n]).then_inc(raw_in[u % RAW], 16)

        def load_rel(i, c):
            n = PAIRS * i + c
            if n >= 2:
                sp.wait_ge(score_done, SCORE[(f"layer{(n - 2) // PAIRS}", "B", (n - 2) % PAIRS, 1, TILES - 1)] + 1)
            for half in range(2):
                for r in range(ROWS):
                    at = ((i * HEADS + 2 * c + half) * RPB_R + 7 - r) * RPB_C + WIN - GRID_W
                    src = bass.AP(rpb.tensor, at, [[1, GRID_W], [RPB_C, ROWS], [1, GRID_W]])
                    dst = rel[(1 - r % 2) * GRID_W:(2 - r % 2) * GRID_W, n % 2, r // 2, half]
                    sp.dma_start(dst.rearrange("p (r c) -> p r c", c=GRID_W), src).then_inc(rel_in[n % 2], 16)

        def load_rbias(hd):
            if hd >= 2:
                sp.wait_ge(score_done, SCORE[("mixer", "dsa", hd - 2, TILES - 1)] + 1)
            for t in range(TILES):
                at = hd * 2 * SEQ + SEQ - (t + 1) * P
                src = bass.AP(row_dram.tensor, at, [[1, P], [1, (t + 1) * P]])
                sp.dma_start(rbias[:, hd % 2, t * P:t * P + (t + 1) * P], src).then_inc(rbias_in[hd % 2], 16)

        sp.dma_start(small[:, :], small_in).then_inc(small_loaded, 16)
        load_unit(0)
        for half in range(2):
            k = slice(half * KT // 2, (half + 1) * KT // 2)
            sp.dma_start(h[:, k], tokens[:, k]).then_inc(tokens_in[half], 16)
        sp.dma_start(consts[:, :], consts_in).then_inc(loaded, 16)
        for u in range(1, NU):
            load_unit(u)
            for i in range(DEPTH):
                for c, behind in enumerate((5, 6, 22, 24)):
                    if u == STAGES[f"layer{i}"] + behind:
                        load_rel(i, c)
            if u == STAGES["ffn0"] + 4:
                sp.wait_ge(h_ready, H_BATCH["layer1"] + KT)
                sp.dma_start(consts2[:, :], consts2_in).then_inc(loaded2, 16)
                sp.dma_start(small2[:, :], small2_in).then_inc(loaded2, 16)
                sp.dma_start(levels[:, :, :], levels_in).then_inc(loaded2, 16)
            if u == STAGES["ffn1"] + 1:
                sp.wait_ge(valued, DEPTH * J + len(DSA_JOBS))
                sp.dma_start(p_in, embeds).then_inc(embeds_in, 16)
            if u == UNIT[("mixer", "gv", 7)]:
                sp.wait_ge(row_ready, 1)
                sp.dma_start(row_dram, bias_row).then_inc(row_stored, 16)
            if u == UNIT[("mixer", "mg", 0)]:
                sp.wait_ge(row_stored, 16)
                sp.wait_ge(gg_ready, KT)
                load_rbias(0)
                load_rbias(1)
            if 2 <= u - UNIT[("mixer", "ms", 0)] - 1 < SH:
                load_rbias(u - UNIT[("mixer", "ms", 0)] - 1)

        for k in range(0, KT, 2):
            sp.wait_ge(out_ready, k + 2)
            sp.dma_start(out[:, k:k + 2], wide[:, k:k + 2, 0:SEQ]).then_inc(stored, 16)
        sp.wait_ge(stored, 16 * KT // 2)

    @block.gpsimd
    def _(pool):
        pool.memset(mean_dm[:, :], 1.0 / DM).then_inc(set_up, 1)
        pool.memset(eps[:, :], EPS).then_inc(set_up, 1)
        for u in range(NU):
            n = BLOCKS[u] * P
            if u == STAGES["ffn0"] + CUT:
                pool.wait_ge(h_ready, H_BATCH["layer1"] + KT)
                pool.memset(mean_gdv[:, :], 1.0 / GDV).then_inc(means_ready, 1)
                pool.memset(mean_p[:, :], 1.0 / P).then_inc(means_ready, 1)
            pool.wait_ge(hi_cut, u + 1)
            pool.tensor_tensor(w_lo[:, u % CUT, 0:n], raw[:, u % RAW, 0:n], w_hi[:, u % CUT, 0:n].bitcast(F32),
                               ALU.subtract).then_inc(lo_cut, 1)

    @block.scalar
    def _(act):
        cut = [0]

        def cut_to(u):
            while cut[0] <= min(u, NU - 1):
                v = cut[0]
                n = BLOCKS[v] * P
                act.wait_ge(raw_in[v % RAW], 16 * (v // RAW + 1))
                if v >= CUT:
                    act.wait_ge(line_done, last_line(v - CUT) + 1)
                act.activation(w_hi[:, v % CUT, 0:n], raw[:, v % RAW, 0:n], ACT.Copy).then_inc(hi_cut, 1)
                cut[0] += 1

        def line_wait(key):
            cut_to(UNIT[key] + CUT - 1)
            act.wait_ge(line_done, LINE[key] + 1)
            return line_bank[LINE[key] % 2]

        def load_root_table(first):
            if first:
                act.wait_ge(set_up, 2)
            act.activation(warm[:, :], eps[:, :], ACT.Sqrt)

        def square(name, k, at, n):
            if at >= 2:
                act.wait_ge(summed, SUMMED[name] + at - 1)
            src = h if name != "final0" or at % 2 == 0 else wide
            act.activation(square_of[name][:, at % 2, 0:n], src[:, k, 0:n], ACT.Square).then_inc(squares_ready, 1)

        def round_h(name, n, before=None):
            x = x_of[name][0]
            load_root_table(name == "layer0")
            for k in range(KT):
                if before:
                    cut_to(UNIT[before(k)] + CUT - 1)
                if name == "layer0":
                    if k == 0:
                        cut_to(0)
                    act.wait_ge(tokens_in[k // (KT // 2)], 16)
                    if k == 0:
                        act.wait_ge(gains_ready, 1)
                else:
                    act.wait_ge(h_ready, H_BATCH[READS[name]] + k + 1)
                act.activation(x[:, k, 0:n], h[:, k, 0:n], ACT.Copy,
                               scale=operand(f"g_{name}")[:, k:k + 1]).then_inc(x_hi_ready, 1)
                square(name, k, k, n)

        def root_of(key, n):
            act.wait_ge(stat_done, STAT[key] + 1)
            act.activation(root[:, STAT[key] % 2, 0:n], stat_bank[:, 0:n], ACT.Sqrt,
                           bias=eps[:, :]).then_inc(root_ready, 1)

        def round_full(batch, k, n, x, gain=1.0):
            act.wait_ge(full_ready, FULL_BATCH[batch] + k + 1)
            act.activation(x[:, k, 0:n], wide[:, k, 0:n], ACT.Copy, scale=gain).then_inc(x_hi_ready, 1)

        def layer(i):
            name = f"layer{i}"
            round_h(name, TOK, (lambda k: (f"layer{i - 1}", "out", k)) if i else None)
            cut_to(STAGES[name] + CUT - 1)
            root_of((name, "norm"), TOK)

            def head_square(n):
                cut_to(UNIT[(name, "qa", n - 1) if n else (name, "ka")] + CUT - 1)
                act.wait_ge(raw_head, 5 * i + n + 1)
                if n >= 2:
                    act.wait_ge(stat_done, STAT[(name, "head", n - 2)] + 1)
                src = ka[:, :] if n == 0 else qa[:, n - 1]
                act.activation(th[:, n % 2, :], src, ACT.Square).then_inc(squares_ready, 1)

            def v_by_token(n):
                v = va[:, :, 0:P] if n == 0 else vb[:, :, (n - 1) * P:n * P]
                act.wait_ge(v_turned, 5 * i + n + 1)
                act.activation(v[:, 0:TILES], turn_bank[:, 0:TILES * P].rearrange("p (t c) -> p t c", c=P),
                               ACT.Copy).then_inc(v_ready, 1)
                act.activation(v[0:META, TILES], turn_bank[0:META, TILES * P:(TILES + 1) * P],
                               ACT.Copy).then_inc(v_ready, 1)

            head_square(0)
            head_square(1)
            for n in range(PAIRS + 1):
                if n >= PAIRS - 1:
                    cut_to(UNIT[(name, "kb", n - PAIRS + 1)] + CUT - 1)
                root_of((name, "head", n), TOK)
                if n == 0:
                    v_by_token(0)
                if n + 2 <= PAIRS:
                    head_square(n + 2)
            for n, c in (("kb", 3), ("qb", 1), ("qb", 3)):
                cut_to(UNIT[(name, n, c)] + CUT - 1)
            for c in range(PAIRS):
                cut_to(UNIT[(name, "vb", c)] + CUT - 1)
                if c:
                    v_by_token(c)
            v_by_token(PAIRS)

            def exps(job, n):
                s = SCORE[(name, *job)]
                act.wait_ge(maxed, n + 1)
                if n >= 2:
                    act.wait_ge(turn_done, TURN_OF_JOB[n - 2] + 1)
                if job[0] == "Bm":
                    at = probs[0:META, n % 2, 0:HEADS * META]
                    act.activation(at, at, ACT.Exp).then_inc(exped, 1)
                    return
                m = PAIRS * META if job[0] == "Am" else P
                act.activation(probs[0:m, n % 2, :], score_bank[s % 2][0:m, 0:TOK], ACT.Exp,
                               bias=top[0:m, n % 2, 0:1], accum_out=total[0:m, n % 2, 0:1]).then_inc(exped, 1)

            def turned_of(job, n):
                act.wait_ge(turn_done, TURN[(name, *job)] + 1)
                if n >= 2:
                    act.wait_ge(valued, n - 1)
                if job[0] == "Bm":
                    out_, in_ = turned[0:META, n % 2, 0:HD], turn_bank[0:META, 0:HD]
                else:
                    m = PAIRS * META if job[0] == "Am" else P
                    out_ = turned[:, n % 2, 0:2 * P].rearrange("p (b q) -> p b q", q=P)[:, :, 0:m]
                    in_ = turn_bank[:, 0:2 * P].rearrange("p (b q) -> p b q", q=P)[:, :, 0:m]
                act.activation(out_, in_, ACT.Copy).then_inc(turned_most, 1)

            def filler(m):
                kind, c = FILLERS[m]
                cut_to(UNIT[(name, kind, c)] + CUT - 1)
                if kind == "ya":
                    return
                act.wait_ge(gate_raw, GATES * i + m + 1)
                if kind in ("za", "zb"):
                    n = 8 * i + m
                    if n >= 2:
                        act.wait_ge(gates_ready, n - 1)
                    act.activation(th[:, m % 2, :], silu[kind[1]][:, c], ACT.Tanh, scale=0.5).then_inc(tanh_ready, 1)
                else:
                    g = gate[kind[1]][:, c]
                    act.activation(g, g, ACT.Tanh, scale=0.5).then_inc(gate_ready, 1)

            def round_y(job):
                n = tile_done(job)
                if n is not None:
                    if n == 0:
                        act.wait_ge(gated, 2 * i + 1)
                    act.wait_ge(pair_gated, KT * i + n + 1)
                    act.activation(y_of[name][0][:, n], wide[:, n], ACT.Copy).then_inc(y_hi_ready, 1)

            for t in range(J + 2):
                if t < J:
                    exps(JOBS[t], J * i + t)
                if t < len(FILLERS):
                    filler(t)
                if 1 <= t <= J:
                    turned_of(JOBS[t - 1], J * i + t - 1)
                if t >= 2:
                    round_y(JOBS[t - 2])
            for m in range(KT):
                cut_to(UNIT[(name, "yb", m)] + CUT - 1)
                round_full(f"mixed{i}", m, TOK, x_of[f"mixed{i}"][0])

        for i in range(DEPTH):
            layer(i)
        load_root_table(False)
        for k in range(KT):
            cut_to(UNIT[(f"layer{DEPTH - 1}", "out", k)] + CUT - 1)
            act.wait_ge(h_ready, H_BATCH["layer1"] + k + 1)
            square("final0", k, 2 * k, SEQ)
            round_full("final0", k, SEQ, x_of["ffn0"][0], operand("g_ffn0")[:, k:k + 1])
            square("final0", k, 2 * k + 1, SEQ)
        cut_to(STAGES["ffn0"] + CUT - 1)
        act.wait_ge(mean_ready, 1)
        act.activation(root[:, STAT[("ffn0", "norm")] % 2, 0:SEQ], prod[:, 0, 0:SEQ], ACT.Sqrt).then_inc(root_ready, 1)
        root_of(("final0", "norm"), SEQ)

        def ffn(f):
            name = f"ffn{f}"

            def round_act(j):
                act.wait_ge(act_full, FT * f + j + 1)
                act.activation(act_hi[:, j], prod2[:, j % 2, 0:SEQ], ACT.Copy).then_inc(act_hi_ready, 1)

            for j in range(FT):
                cut_to(UNIT[(name, "gate", j)] + CUT - 1)
                n = FT * f + j
                act.wait_ge(act_raw, n + 1)
                if j >= 2:
                    act.wait_ge(act_half, n - 1)
                act.activation(th[:, j % 2, 0:SEQ], prod[:, j % 2, 0:SEQ], ACT.Tanh, scale=0.5).then_inc(act_tanh, 1)
                if j:
                    round_act(j - 1)
            round_act(FT - 1)

        ffn(0)

        round_h("mixer", SEQ, lambda k: ("ffn0", "down", k, 1))
        cut_to(STAGES["mixer"] + CUT - 1)
        root_of(("mixer", "norm"), SEQ)
        act.wait_ge(low_ready, 1)
        for rows in (slice(HD, P), slice(0, HD)):
            act.activation(index_k[rows], low[HD:P], ACT.Copy).then_inc(index_k_ready, 1)
        act.wait_ge(ckv_raw, 1)
        act.activation(th[:, 0, 0:SEQ], ckv[:, :], ACT.Square).then_inc(squares_ready, 1)

        act.wait_ge(row_done, 1)
        act.activation(bias_row, result_bank[RESULT[("mixer", "rel")] % 2][0:SH, :], ACT.Copy).then_inc(row_ready, 1)
        cut_to(UNIT[("mixer", "gk", 0)] + CUT - 1)
        root_of(("mixer", "ckv"), SEQ)
        cut_to(UNIT[("mixer", "gk", 2)] + CUT - 1)
        act.wait_ge(soft_in, 1)
        act.activation(gate_k[:, :], gate_k[:, :], ACT.Exp).then_inc(soft_step, 1)
        act.wait_ge(soft_step, 1)
        act.activation(gate_k[:, :], gate_k[:, :], ACT.Ln, bias=1.0).then_inc(soft_out, 1)
        cut_to(UNIT[("mixer", "gq", 2)] + CUT - 1)
        act.wait_ge(turn_done, TURN[("mixer", "ckv")] + 1)
        act.activation(ckv_t[:, :, :], turn_bank[:, 0:TILES * P].rearrange("p (t c) -> p t c", c=P),
                       ACT.Copy).then_inc(turned_most, 1)

        def rise(n):
            act.wait_ge(fallen, n + 1)
            act.activation(fall[:, :], fall[:, :], ACT.Exp).then_inc(risen, 1)

        rise(0)
        act.activation(grown, decay.rearrange("p (g t) -> p g t", t=SEQ), ACT.Exp).then_inc(grown_ready, 1)
        for n in range(len(HALVES)):
            rise(n + 1)
            for f in LEVEL_FILLERS[2 * n:2 * n + 2]:
                cut_to(UNIT[("mixer", *f)] + CUT - 1)
                if f[0] == "gv":
                    act.wait_ge(gv_turned, f[1] + 1)
                    act.activation(gv[:, :, f[1] * P:(f[1] + 1) * P],
                                   turn_bank[:, 0:TILES * P].rearrange("p (t c) -> p t c", c=P),
                                   ACT.Copy).then_inc(gv_ready, 1)
        cut_to(UNIT[("mixer", "gr", 0)] + CUT - 2)
        for t in range(TILES):
            s = SCORE[("mixer", "kdt", t)]
            act.wait_ge(score_done, s + 1)
            act.activation(fall[:, t * GH * P:(t + 1) * GH * P], score_bank[s % 2][:, :], ACT.Copy).then_inc(kdt_ready, 1)

        def tanh_gr(m):
            cut_to(UNIT[("mixer", "gr", m)] + CUT - 1)
            act.wait_ge(gr_raw, m + 1)
            if m >= 2:
                act.wait_ge(gates_ready, 8 * DEPTH + m - 1)
            act.activation(probs[:, m % 2, 0:SEQ], gr[:, m], ACT.Tanh, scale=0.5).then_inc(tanh_ready, 1)

        def round_gg(m):
            act.wait_ge(gla_full, m + 1)
            act.activation(gg_hi[:, m], prod2[:, m % 2, 0:SEQ], ACT.Copy).then_inc(gg_hi_ready, 1)

        def head_out(g):
            if g:
                act.wait_ge(stat_done, STAT[("mixer", "gla", g - 1)] + 1)
                act.wait_ge(gla_full, 2 * g)
            for e in range(2):
                bank = result_bank[RESULT[("mixer", "gla", g, e)] % 2]
                act.wait_ge(gla_done, 2 * g + e + 1)
                act.activation(prod[:, e, 0:SEQ], bank[:, 0:SEQ], ACT.Copy).then_inc(gla_raw, 1)
                act.activation(th[:, e, 0:SEQ], bank[:, 0:SEQ], ACT.Square).then_inc(squares_ready, 1)

        for g in range(GH + 1):
            if g:
                root_of(("mixer", "gla", g - 1), SEQ)
            if g < GH:
                tanh_gr(2 * g)
                tanh_gr(2 * g + 1)
            if g:
                round_gg(2 * g - 2)
                round_gg(2 * g - 1)
            if g < GH:
                head_out(g)
            cut_to(UNIT[("mixer", "gr", min(2 * g + 2, 2 * GH - 1))] + CUT - 1)

        for n, (t, hd) in enumerate((t, hd) for t in range(TILES) for hd in range(SH)):
            s = SCORE[("mixer", "dots", t, hd)]
            keys = (t + 1) * P
            act.wait_ge(score_done, s + 1)
            if n >= 2:
                act.wait_ge(scored, n - 1)
            act.activation(th[:, n % 2, 0:keys], score_bank[s % 2][:, 0:keys], ACT.Relu).then_inc(relued, 1)
            if n % 2:
                cut_to(UNIT[("mixer", "dq", min(n // 2 + 2, SH - 1))] + CUT - 1)

        def tanh_gate(name, m):
            cut_to(UNIT[("mixer", name, m)] + CUT - 1)
            act.wait_ge(gate_raw, GATES * DEPTH + KT * (name == "ms") + m + 1)
            g = mgate[name[1]][:, m]
            act.activation(g, g, ACT.Tanh, scale=0.5).then_inc(gate_ready, 1)

        for m in range(KT):
            tanh_gate("mg", m)

        def dsa_exps(i):
            hd, t = DSA_JOBS[i]
            n, s, keys = DEPTH * J + i, SCORE[("mixer", "dsa", hd, t)], (t + 1) * P
            act.wait_ge(maxed, n + 1)
            act.wait_ge(turn_done, TURN_OF_JOB[n - 2] + 1)
            act.activation(probs[:, n % 2, 0:keys], score_bank[s % 2][:, 0:keys], ACT.Exp, bias=top[:, n % 2, 0:1],
                           accum_out=total[:, n % 2, 0:1]).then_inc(exped, 1)

        def dsa_turned(i):
            hd, t = DSA_JOBS[i]
            n, keys = DEPTH * J + i, (t + 1) * P
            act.wait_ge(turn_done, TURN[("mixer", "dsa", hd, t)] + 1)
            act.wait_ge(valued, n - 1)
            act.activation(turned[:, n % 2, 0:keys], turn_bank[:, 0:keys], ACT.Copy).then_inc(turned_most, 1)

        def round_od(i):
            hd, t = DSA_JOBS[i]
            if t == TILES - 1:
                act.wait_ge(valued, DEPTH * J + i + 1)
                act.activation(od_hi[:, hd], result_bank[RESULT[("mixer", "dsa", hd)] % 2][:, 0:SEQ],
                               ACT.Copy).then_inc(od_hi_ready, 1)

        for i in range(len(DSA_JOBS) + 2):
            if i < len(DSA_JOBS):
                dsa_exps(i)
                name, m = DSA_FILLERS[i]
                if name == "ms":
                    tanh_gate(name, m)
                else:
                    cut_to(UNIT[("mixer", name, m)] + CUT - 1)
            if 1 <= i <= len(DSA_JOBS):
                dsa_turned(i - 1)
            if i >= 2:
                round_od(i - 2)
        for m in range(KT):
            cut_to(UNIT[("mixer", "ys", m)] + CUT - 1)
            round_full("mixed2", m, SEQ, x_of["mixed2"][0])
        round_h("ffn1", SEQ, lambda k: ("mixer", "mix", k))
        cut_to(STAGES["ffn1"] + CUT - 1)
        root_of(("ffn1", "norm"), SEQ)
        act.wait_ge(embeds_in, 16)
        act.activation(p_hi[:, :, :], p_in, ACT.Copy).then_inc(p_hi_ready, 1)
        ffn(1)

        round_h("embed", SEQ, lambda k: ("ffn1", "down", k, 1))
        for m in range(KT):
            bank = line_wait(("embed", "pp", m))
            act.activation(pp[:, m], bank[:, 0:SEQ], ACT.Copy, scale=0.5).then_inc(pp_ready, 1)
        cut_to(STAGES["embed"] + CUT)
        root_of(("embed", "norm"), SEQ)

        def square_of_result(k):
            act.wait_ge(h_ready, H_BATCH["embed"] + k + 1)
            square("final1", k, k, SEQ)

        for m in range(KT):
            cut_to(UNIT[("embed", "pg", m)] + CUT - 1)
            act.wait_ge(pg_raw, m + 1)
            if m >= 2:
                act.wait_ge(pg_used, m - 1)
            act.activation(th[:, m % 2, 0:SEQ], prod2[:, m % 2, 0:SEQ], ACT.Tanh, scale=0.5).then_inc(tanh_ready, 1)
            if m:
                square_of_result(m - 1)
        square_of_result(KT - 1)
        root_of(("final1", "norm"), SEQ)

    @block.vector
    def _(dve):
        steps = [0]

        def link(ins):
            steps[0] += 1
            ins.then_inc(dve_step, 1)
            dve.wait_ge(dve_step, steps[0])

        def line_wait(key):
            dve.wait_ge(line_done, LINE[key] + 1)
            return line_bank[LINE[key] % 2]

        def newton(r, v, mean, out_=None):
            link(dve.reciprocal(r, v))
            mean(r)
            link(dve.tensor_tensor(v, v, r, ALU.mult))
            link(dve.scalar_tensor_tensor(r if out_ is None else out_, v, -3.0, r, ALU.add, ALU.mult))

        def rstd_of(key, n, out_=None):
            s = STAT[key] % 2
            r, v = rstd[:, s, 0:n], root[:, s, 0:n]
            dve.wait_ge(root_ready, STAT[key] + 1)

            def mean(r):
                dve.scalar_tensor_tensor(v, stat_bank[:, 0:n], EPS, r, ALU.add, ALU.mult).then_inc(stat_read, 1)
                dve.wait_ge(stat_read, STAT[key] + 1)

            newton(r, v, mean, out_)
            return r if out_ is None else out_

        def add_square(name, k, at, n):
            total_ = sum_of[name][at % 2 if name == "final0" else 0][:, 0:n]
            sq = square_of[name][:, at % 2, 0:n]
            dve.wait_ge(squares_ready, SQUARES[(name, "norm")] + at + 1)
            if k == 0:
                ins = dve.tensor_copy(total_, sq)
            else:
                dve.wait_ge(summed, SUMMED[name] + at - (name == "final0"))
                ins = dve.tensor_tensor(total_, total_, sq, ALU.add)
            ins.then_inc(summed, 1)

        def rest_of_h(name, k, n):
            x = x_of[name]
            dve.wait_ge(x_hi_ready, X_BATCH[name] + k + 1)
            dve.scalar_tensor_tensor(x[1][:, k, 0:n], h[:, k, 0:n], operand(f"g_{name}")[:, k:k + 1],
                                     x[0][:, k, 0:n].bitcast(F32), ALU.mult, ALU.subtract).then_inc(x_ready, 1)
            add_square(name, k, k, n)

        def rest_of_full(batch, k, n):
            x = x_of[batch]
            dve.wait_ge(x_hi_ready, X_BATCH[batch] + k + 1)
            dve.tensor_tensor(x[1][:, k, 0:n], wide[:, k, 0:n], x[0][:, k, 0:n].bitcast(F32),
                              ALU.subtract).then_inc(x_ready, 1)

        def scaled_line(key, dst, factor=None):
            bank = line_wait(key)[:, 0:dst.shape[-1]]
            by = scale[:, 0:dst.shape[-1]]
            if factor is None:
                return dve.tensor_tensor(dst, bank, by, ALU.mult)
            return dve.scalar_tensor_tensor(dst, bank, factor, by, ALU.mult, ALU.mult)

        def layer(i):
            name = f"layer{i}"
            rstd_of((name, "norm"), TOK, scale[:, :])

            def head_raw(n):
                key, dst = ((name, "qa", n - 1), qa[:, n - 1]) if n else ((name, "ka"), ka[:, :])
                scaled_line(key, dst).then_inc(raw_head, 1)

            def v_raw_of(n):
                if n >= 2:
                    dve.wait_ge(v_turned, 5 * i + n - 1)
                scaled_line((name, "vb", n - 1) if n else (name, "va"), prod2[:, n % 2, :]).then_inc(v_raw, 1)

            def head_norm(n):
                dst = ka[:, :] if n == 0 else qa[:, n - 1]
                g = operand(f"k_gain{i}") if n == 0 else q_gain[:, i:i + 1]
                r = rstd_of((name, "head", n), TOK)
                dve.scalar_tensor_tensor(dst, dst, g, r, ALU.mult, ALU.mult).then_inc(normed, 1)

            def rope(n):
                dst = ka[:, :] if n == 0 else qa[:, n - 1]
                key = (name, "rot", n)
                dve.wait_ge(normed, 5 * i + n + 1)
                dve.tensor_tensor(prod[:, 0, :], dst, const("cos"), ALU.mult)
                dve.wait_ge(rot_done, 5 * i + n + 1)
                dve.tensor_tensor(prod[:, 1, :], result_bank[RESULT[key] % 2][:, 0:TOK], const("sin"),
                                  ALU.mult).then_inc(rot_used, 1)
                dve.wait_ge(rot_used, 5 * i + n + 1)
                dve.tensor_tensor(dst, prod[:, 0, :], prod[:, 1, :], ALU.add).then_inc(roped, 1)
                if n:
                    dve.wait_ge(roped, 9 * i + 2 * n)
                    dve.tensor_copy(q_meta[:, (n - 1) * META:n * META], dst[:, SEQ:TOK]).then_inc(roped, 1)

            head_raw(0)
            v_raw_of(0)
            head_raw(1)
            head_raw(2)
            head_norm(0)
            for n in range(3, PAIRS + 1):
                head_raw(n)
                head_norm(n - 2)
                rope(n - 3)
            for c in range(PAIRS):
                scaled_line((name, "kb", c), kb[:, c]).then_inc(kq_ready, 1)
                if c < 2:
                    head_norm(PAIRS - 1 + c)
                if c < 3:
                    rope(PAIRS - 2 + c)
            for c in range(PAIRS):
                scaled_line((name, "qb", c), qb[:, c], HD ** -0.5).then_inc(kq_ready, 1)
            for c in range(PAIRS):
                v_raw_of(c + 1)

            def window_bias(c):
                n = PAIRS * i + c
                dve.wait_ge(rel_in[n % 2], 16 * 2 * ROWS * (n // 2 + 1))
                at = rel[:, n % 2].rearrange("p t h (r c) -> p (t h r) c", c=GRID_W)
                w = const("window").unsqueeze(1).to_broadcast([P, TILES * 2 * ROWS, GRID_W])
                dve.tensor_tensor(at, at, w, ALU.add).then_inc(rel_ready, 1)

            def maxes(job, n):
                s = SCORE[(name, *job)]
                bank = score_bank[s % 2]
                for c in range(PAIRS):
                    if n - J * i == JOBS.index(("B", c, 0, 0)) - 2:
                        window_bias(c)
                dve.wait_ge(score_done, s + 1)
                if job[0] == "Bm":
                    at = bank[0:META, 0:HEADS * META].rearrange("p (h k) -> p h k", k=META)
                    link(dve.tensor_reduce(top[0:META, n % 2, :], at, AX.X, ALU.max))
                    dve.tensor_tensor(probs[0:META, n % 2, 0:HEADS * META].rearrange("p (h k) -> p h k", k=META), at,
                                      top[0:META, n % 2, :].unsqueeze(2).to_broadcast([META, HEADS, META]),
                                      ALU.subtract).then_inc(maxed, 1)
                    return
                m = PAIRS * META if job[0] == "Am" else P
                dve.tensor_reduce(top[0:m, n % 2, 0:1], bank[0:m, 0:TOK], AX.X, ALU.max, negate=True).then_inc(maxed, 1)

            def shares(job, n):
                dve.wait_ge(exped, n + 1)
                if job[0] == "Bm":
                    at = probs[0:META, n % 2, 0:HEADS * META].rearrange("p (h k) -> p h k", k=META)
                    link(dve.tensor_reduce(total[0:META, n % 2, :], at, AX.X, ALU.add))
                    link(dve.reciprocal(share[0:META, n % 2, :], total[0:META, n % 2, :]))
                    dve.tensor_tensor(at, at, share[0:META, n % 2, :].unsqueeze(2).to_broadcast([META, HEADS, META]),
                                      ALU.mult).then_inc(probs_ready, 1)
                    return
                m = PAIRS * META if job[0] == "Am" else P
                link(dve.reciprocal(share[0:m, n % 2, 0:1], total[0:m, n % 2, 0:1]))
                dve.tensor_scalar(probs[0:m, n % 2, :], probs[0:m, n % 2, :], share[0:m, n % 2, 0:1], None,
                                  ALU.mult).then_inc(probs_ready, 1)

            def turned_of(job, n):
                dve.wait_ge(turned_most, TURN[(name, *job)] + 1)
                if job[0] == "Bm":
                    out_, in_ = turned[0:META, n % 2, HD:P], turn_bank[0:META, HD:P]
                else:
                    m = PAIRS * META if job[0] == "Am" else P
                    out_, in_ = turned[0:META, n % 2, 2 * P:2 * P + m], turn_bank[0:META, 2 * P:2 * P + m]
                dve.tensor_copy(out_, in_).then_inc(turned_rest, 1)

            def filler(m):
                kind, c = FILLERS[m]
                if kind == "ya":
                    dst = gate["a"][:, c]
                    dve.wait_ge(gate_ready, 16 * i + c + 1)
                    dve.scalar_tensor_tensor(dst, dst, 1.0, line_wait((name, kind, c))[:, 0:TOK], ALU.add,
                                             ALU.mult).then_inc(y_used, 1)
                    return
                dst = (silu if kind in ("za", "zb") else gate)[kind[1]][:, c]
                scaled_line((name, kind, c), dst).then_inc(gate_raw, 1)

            def silu_of(m):
                kind, c = FILLERS[m]
                if kind in ("za", "zb"):
                    n = 8 * i + m
                    dst = silu[kind[1]][:, c]
                    dve.wait_ge(tanh_ready, n + 1)
                    dve.scalar_tensor_tensor(dst, th[:, m % 2, :], 1.0, dst, ALU.add, ALU.mult).then_inc(gates_ready, 1)

            def result_of(job, n):
                kind = job[0][0]
                part = 0 if kind == "A" else PAIRS
                if job in (("Am", 1), ("Bm",)):
                    key = (name, kind + "m")
                    dve.wait_ge(valued, n + 1)
                    dve.tensor_tensor(wide[:, part:part + PAIRS, SEQ:TOK],
                                      result_bank[RESULT[key] % 2][:, 0:PAIRS * META].rearrange(
                                          "p (c q) -> p c q", q=META),
                                      silu[kind.lower()][:, :, SEQ:TOK], ALU.mult).then_inc(gated, 1)
                elif len(job) == 4 and job[2:] == (1, TILES - 1):
                    key = (name, kind, job[1])
                    dve.wait_ge(valued, n + 1)
                    dve.tensor_tensor(wide[:, part + job[1], 0:SEQ], result_bank[RESULT[key] % 2][:, 0:SEQ],
                                      silu[kind.lower()][:, job[1], 0:SEQ],
                                      ALU.mult).then_inc(pair_gated, 1)

            def rest_of_y(job):
                n, y = tile_done(job), y_of[name]
                if n is not None:
                    dve.wait_ge(y_hi_ready, KT * i + n + 1)
                    dve.tensor_tensor(y[1][:, n], wide[:, n], y[0][:, n].bitcast(F32), ALU.subtract).then_inc(y_ready, 1)

            for t in range(J + 2):
                if t < J:
                    maxes(JOBS[t], J * i + t)
                    shares(JOBS[t], J * i + t)
                if t < len(FILLERS):
                    filler(t)
                if 1 <= t <= J:
                    turned_of(JOBS[t - 1], J * i + t - 1)
                if 1 <= t <= len(FILLERS):
                    silu_of(t - 1)
                if t >= 2:
                    result_of(JOBS[t - 2], J * i + t - 2)
                if t >= 3:
                    rest_of_y(JOBS[t - 3])
            rest_of_y(JOBS[J - 1])

            for m in range(KT):
                dve.wait_ge(gate_ready, 16 * i + KT + m + 1)
                dve.scalar_tensor_tensor(prod[:, m % 2, :], gate["b"][:, m], 1.0, line_wait((name, "yb", m))[:, 0:TOK],
                                         ALU.add, ALU.mult).then_inc(y_used, 1)
                dve.wait_ge(y_used, 16 * i + KT + m + 1)
                dve.tensor_tensor(wide[:, m], prod[:, m % 2, :], gate["a"][:, m], ALU.add).then_inc(full_ready, 1)
                if m:
                    rest_of_full(f"mixed{i}", m - 1, TOK)
            rest_of_full(f"mixed{i}", KT - 1, TOK)
            for m in range(KT):
                key = (name, "out", m)
                dve.scalar_tensor_tensor(h[:, m], line_wait(key)[:, 0:TOK], 0.25, h[:, m], ALU.mult,
                                         ALU.add).then_inc(h_ready, 1)
                if i == 0:
                    dve.wait_ge(h_ready, H_BATCH[name] + m + 1)
                    rest_of_h("layer1", m, TOK)
                else:
                    dve.wait_ge(h_ready, H_BATCH[name] + m + 1)
                    dve.tensor_scalar(wide[:, m, 0:SEQ], h[:, m, 0:SEQ], operand("g_final0")[:, m:m + 1], None,
                                      ALU.mult).then_inc(full_ready, 1)
                    add_square("final0", m, 2 * m, SEQ)
                    dve.wait_ge(x_hi_ready, X_BATCH["ffn0"] + m + 1)
                    x = x_of["ffn0"]
                    dve.scalar_tensor_tensor(x[1][:, m, 0:SEQ], wide[:, m, 0:SEQ], operand("g_ffn0")[:, m:m + 1],
                                             x[0][:, m, 0:SEQ].bitcast(F32), ALU.mult, ALU.subtract).then_inc(x_ready, 1)
                    add_square("final0", m, 2 * m + 1, SEQ)

        dve.wait_ge(small_loaded, 16)
        dve.tensor_scalar(small[:, :], small[:, :], -0.5, None, ALU.mult).then_inc(gains_ready, 1)
        dve.wait_ge(gains_ready, 1)
        for i in range(DEPTH):
            link(dve.tensor_scalar(q_gain[:, i:i + 1], operand(f"q_gain{i}"), HD ** -0.5, None, ALU.mult))
        for k in range(KT):
            dve.wait_ge(tokens_in[k // (KT // 2)], 16)
            rest_of_h("layer0", k, TOK)
        dve.wait_ge(loaded, 16)
        for i in range(DEPTH):
            layer(i)

        key = ("ffn0", "norm")
        m2 = prod[:, 0, 0:SEQ]
        dve.wait_ge(stat_done, STAT[("final0", "norm")] + 1)
        link(dve.tensor_scalar(m2, stat_bank[:, 0:SEQ], EPS, EPS / 4, ALU.add, ALU.mult))
        dve.tensor_tensor(m2, m2, stat_bank[:, SEQ:2 * SEQ], ALU.add).then_inc(mean_ready, 1)
        dve.wait_ge(root_ready, STAT[key] + 1)
        r2, v2 = rstd[:, STAT[key] % 2, 0:SEQ], root[:, STAT[key] % 2, 0:SEQ]

        def mean(r):
            dve.tensor_tensor(v2, m2, r, ALU.mult).then_inc(stat_read, 1)
            dve.wait_ge(stat_read, STAT[key] + 1)

        newton(r2, v2, mean)
        link(dve.tensor_scalar(scale[:, 0:SEQ], r2, -1.0, None, ALU.mult))

        def last_norm():
            rstd_of(("final0", "norm"), SEQ)

        def first_result(k):
            dve.tensor_tensor(h[:, k, 0:SEQ], wide[:, k, 0:SEQ], rstd[:, STAT[("final0", "norm")] % 2, 0:SEQ],
                              ALU.mult).then_inc(h_ready, 1)

        def ffn(f):
            name = f"ffn{f}"

            def finish(j):
                n = FT * f + j
                dve.wait_ge(act_tanh, n + 1)
                dve.scalar_tensor_tensor(prod[:, j % 2, 0:SEQ], th[:, j % 2, 0:SEQ], 1.0, prod[:, j % 2, 0:SEQ],
                                         ALU.add, ALU.mult).then_inc(act_half, 1)
                dve.wait_ge(act_half, n + 1)
                dve.tensor_tensor(prod2[:, j % 2, 0:SEQ], prod[:, j % 2, 0:SEQ], prod2[:, j % 2, 0:SEQ],
                                  ALU.mult).then_inc(act_full, 1)

            def rest_of_act(j):
                dve.wait_ge(act_hi_ready, FT * f + j + 1)
                dve.tensor_tensor(act_lo[:, j], prod2[:, j % 2, 0:SEQ], act_hi[:, j].bitcast(F32),
                                  ALU.subtract).then_inc(act_ready, 1)

            for j in range(FT):
                scaled_line((name, "gate", j), prod[:, j % 2, 0:SEQ]).then_inc(act_raw, 1)
                if j:
                    rest_of_act(j - 1)
                if f == 0 and j == 1:
                    last_norm()
                if f == 0 and 2 <= j < KT + 2:
                    first_result(j - 2)
                scaled_line((name, "up", j), prod2[:, j % 2, 0:SEQ]).then_inc(act_up, 1)
                dve.wait_ge(act_up, FT * f + j + 1)
                finish(j)
            rest_of_act(FT - 1)
            for m in range(KT):
                dve.scalar_tensor_tensor(h[:, m, 0:SEQ], line_wait((name, "down", m, 0))[:, 0:SEQ], 0.25,
                                         h[:, m, 0:SEQ], ALU.mult, ALU.add).then_inc(down_used, 1)
                if m:
                    rest_of_h(("mixer", "embed")[f], m - 1, SEQ)
                dve.wait_ge(down_used, KT * f + m + 1)
                dve.scalar_tensor_tensor(h[:, m, 0:SEQ], line_wait((name, "down", m, 1))[:, 0:SEQ], 0.25,
                                         h[:, m, 0:SEQ], ALU.mult, ALU.add).then_inc(h_ready, 1)
            dve.wait_ge(h_ready, H_BATCH[name] + KT)
            rest_of_h(("mixer", "embed")[f], KT - 1, SEQ)

        ffn(0)

        rstd_of(("mixer", "norm"), SEQ, scale[:, 0:SEQ])
        scaled_line(("mixer", "low"), low).then_inc(low_ready, 1)
        scaled_line(("mixer", "ckv"), ckv[:, :]).then_inc(ckv_raw, 1)
        scaled_line(("mixer", "gk", 0), gk[:, 0:SEQ]).then_inc(gla_in, 1)
        dve.wait_ge(index_w_turned, 1)
        bank = result_bank[RESULT[("mixer", "index_w")] % 2]
        dve.tensor_scalar(index_w[:, :, :], bank[:, 0:TILES * SH].rearrange("p (t h) -> p t h", h=SH),
                          (HD * SH) ** -0.5, None, ALU.mult).then_inc(index_w_ready, 1)
        dve.wait_ge(loaded2, 48)
        link(dve.tensor_scalar(gla_gain[:, :], operand("gla_gain"), -0.25, None, ALU.mult))
        link(dve.tensor_scalar(operand("ckv_gain"), operand("ckv_gain"), -0.5, None, ALU.mult))
        dve.memset(pairs[:, :, :, :], 0.0)
        for g in range(GH):
            s = SCORE[("mixer", "alpha", g // 2)]
            dve.wait_ge(score_done, s + 1)
            dve.tensor_scalar(gate_q[:, g * SEQ:(g + 1) * SEQ], score_bank[s % 2][:, g % 2 * SEQ:(g % 2 + 1) * SEQ],
                              operand("alpha_b")[:, g:g + 1], None, ALU.add).then_inc(alpha_used, 1)
        scaled_line(("mixer", "gk", 1), gk[:, SEQ:2 * SEQ]).then_inc(gla_in, 1)
        dve.wait_ge(alpha_used, GH)
        dve.scalar_tensor_tensor(gate_k[:, :], gate_q[:, :], -1.0, gate_q[:, :], ALU.mult, ALU.min).then_inc(soft_in, 1)
        link(dve.tensor_scalar(gate_q[:, :], gate_q[:, :], 0.0, 1.0 / TAU, ALU.min, ALU.mult))
        r = rstd_of(("mixer", "ckv"), SEQ)
        dve.scalar_tensor_tensor(ckv[:, :], ckv[:, :], operand("ckv_gain"), r, ALU.mult, ALU.mult).then_inc(ckv_ready, 1)
        for c in range(2, GH):
            scaled_line(("mixer", "gk", c), gk[:, c * SEQ:(c + 1) * SEQ]).then_inc(gla_in, 1)
        dve.wait_ge(soft_out, 1)
        link(dve.scalar_tensor_tensor(fall[:, :], gate_k[:, :], -1.0 / TAU, gate_q[:, :], ALU.mult, ALU.add))
        link(dve.tensor_tensor_scan(decay, const("keep"), fall[:, :], 0.0, ALU.mult, ALU.add))

        def falls(n):
            if n == len(HALVES):
                d, f = (x.rearrange("p (b t) -> p b t", t=CHUNK) for x in (decay, fall[:, :]))
                dve.tensor_tensor(f, d[:, :, CHUNK - 1:CHUNK].to_broadcast([P, GH * SEQ // CHUNK, CHUNK]), d,
                                  ALU.subtract).then_inc(fallen, 1)
                return
            half = HALVES[n]
            d, f = (x.rearrange("p (b s t) -> p b s t", s=2, t=half) for x in (decay, fall[:, :]))
            ref = d[:, :, 0, half - 1:half].to_broadcast([P, GH * SEQ // (2 * half), half])
            link(dve.tensor_tensor(f[:, :, 0], ref, d[:, :, 0], ALU.subtract))
            dve.tensor_tensor(f[:, :, 1], d[:, :, 1], ref, ALU.subtract).then_inc(fallen, 1)

        def by_head(x):
            return x.rearrange("p (g t) -> p g t", t=SEQ)

        falls(0)
        for n in range(len(HALVES) + 1):
            if n == 0:
                for c in range(GH):
                    scaled_line(("mixer", "gq", c), gq[:, c], GDK ** -0.5).then_inc(gla_in, 1)
                dve.wait_ge(gla_in, 2 * GH)
            dve.wait_ge(risen, n + 1)
            if n < len(HALVES):
                dve.tensor_tensor(by_head(gate_q[:, :]), gq, by_head(fall[:, :]), ALU.mult)
            else:
                dve.wait_ge(grown_ready, 1)
                dve.tensor_tensor(by_head(gate_q[:, :]), gq, grown, ALU.mult)
            dve.tensor_tensor(gate_k[:, :], gk, fall[:, :], ALU.mult).then_inc(level_ready, 1)
            if n < len(HALVES):
                dve.wait_ge(level_ready, n + 1)
                falls(n + 1)
                for kind, c in LEVEL_FILLERS[2 * n:2 * n + 2]:
                    if kind == "gv":
                        if c >= 2:
                            dve.wait_ge(gv_turned, c - 1)
                        scaled_line(("mixer", kind, c), prod2[:, c % 2, 0:SEQ]).then_inc(gv_raw, 1)
                    else:
                        scaled_line(("mixer", kind, c), index_q[:, c]).then_inc(index_q_ready, 1)
            for t in range(TILES):
                s = SCORE[("mixer", "level", n, t)]
                dve.wait_ge(score_done, s + 1)
                mask = levels[:, n].unsqueeze(1).to_broadcast([P, GH, P])
                dve.copy_predicated(pairs[:, t], mask,
                                    score_bank[s % 2][:, :].rearrange("p (g t) -> p g t", t=P)).then_inc(level_used, 1)

        def gr_of(m):
            scaled_line(("mixer", "gr", m), gr[:, m]).then_inc(gr_raw, 1)

        def silu_gr(m):
            dve.wait_ge(tanh_ready, 8 * DEPTH + m + 1)
            dve.scalar_tensor_tensor(gr[:, m], probs[:, m % 2, 0:SEQ], 1.0, gr[:, m], ALU.add,
                                     ALU.mult).then_inc(gates_ready, 1)

        def head_states(g):
            if g:
                dve.wait_ge(gla_done, 2 * g)
            for c in range(3):
                s = SCORE[("mixer", "state", g, c)]
                dve.wait_ge(score_done, s + 1)
                bank = score_bank[s % 2][:, 0:GDV]
                if c == 0:
                    dve.tensor_copy(states[:, 0], bank).then_inc(state_ready, 1)
                else:
                    dve.wait_ge(state_ready, 3 * g + c)
                    end = c * CHUNK + CHUNK - 1
                    dve.scalar_tensor_tensor(states[:, c], states[:, c - 1], grown[:, g, end:end + 1], bank, ALU.mult,
                                             ALU.add).then_inc(state_ready, 1)

        def head_gated(g):
            r = rstd_of(("mixer", "gla", g), SEQ)
            dve.wait_ge(gla_raw, 2 * g + 2)
            for e in range(2):
                m = 2 * g + e
                link(dve.scalar_tensor_tensor(prod[:, e, 0:SEQ], prod[:, e, 0:SEQ], gla_gain[:, m:m + 1], r, ALU.mult,
                                              ALU.mult))
                dve.tensor_tensor(prod2[:, e, 0:SEQ], prod[:, e, 0:SEQ], gr[:, m], ALU.mult).then_inc(gla_full, 1)
            for e in range(2):
                m = 2 * g + e
                dve.wait_ge(gg_hi_ready, m + 1)
                dve.tensor_tensor(gg_lo[:, m], prod2[:, e, 0:SEQ], gg_hi[:, m].bitcast(F32),
                                  ALU.subtract).then_inc(gg_ready, 1)

        def dq_of(m):
            scaled_line(("mixer", "dq", m), dq[:, m], P ** -0.5).then_inc(dq_ready, 1)

        for g in range(GH):
            gr_of(2 * g)
            gr_of(2 * g + 1)
            head_states(g)
            silu_gr(2 * g)
            silu_gr(2 * g + 1)
            if g:
                head_gated(g - 1)
        dq_of(0)
        head_gated(GH - 1)
        dq_of(1)

        def gate_of(name, m):
            scaled_line(("mixer", name, m), mgate[name[1]][:, m]).then_inc(gate_raw, 1)

        def choose(t):
            keys = (t + 1) * P
            own = score[:, t, t * P:keys]
            link(dve.tensor_tensor(own, own, const("later"), ALU.add))
            for r in range(TOPK // 8):
                src = work[:, t, 0:keys] if r else score[:, t, 0:keys]
                link(dve.max(best[:, :], src))
                link(dve.match_replace(work[:, t, 0:keys], best[:, :], src, TAKEN))
                if r % 2:
                    gate_of("mg", TOPK // 16 * t + r // 2)
            link(dve.tensor_scalar(score[:, t, 0:keys], work[:, t, 0:keys], TAKEN / 2, NEG, ALU.is_gt, ALU.mult))
            link(dve.tensor_tensor(own, own, const("later"), ALU.add))

        for n, (t, hd) in enumerate((t, hd) for t in range(TILES) for hd in range(SH)):
            keys = (t + 1) * P
            dve.wait_ge(relued, n + 1)
            w = index_w[:, t, hd:hd + 1]
            if hd == 0:
                dve.tensor_scalar(score[:, t, 0:keys], th[:, n % 2, 0:keys], w, None, ALU.mult).then_inc(scored, 1)
            else:
                dve.wait_ge(scored, n)
                dve.scalar_tensor_tensor(score[:, t, 0:keys], th[:, n % 2, 0:keys], w, score[:, t, 0:keys], ALU.mult,
                                         ALU.add).then_inc(scored, 1)
            if n % 2 and n // 2 + 2 < SH:
                dq_of(n // 2 + 2)
        dve.wait_ge(scored, TILES * SH)
        for t in range(TILES):
            choose(t)

        def dsa_maxes(i):
            hd, t = DSA_JOBS[i]
            n, s, keys = DEPTH * J + i, SCORE[("mixer", "dsa", hd, t)], (t + 1) * P
            bank = score_bank[s % 2][:, 0:keys]
            dve.wait_ge(score_done, s + 1)
            link(dve.tensor_tensor(bank, bank, score[:, t, 0:keys], ALU.add))
            dve.tensor_reduce(top[:, n % 2, 0:1], bank, AX.X, ALU.max, negate=True).then_inc(maxed, 1)

        def dsa_shares(i):
            hd, t = DSA_JOBS[i]
            n, keys = DEPTH * J + i, (t + 1) * P
            dve.wait_ge(exped, n + 1)
            link(dve.reciprocal(share[:, n % 2, 0:1], total[:, n % 2, 0:1]))
            dve.tensor_scalar(probs[:, n % 2, 0:keys], probs[:, n % 2, 0:keys], share[:, n % 2, 0:1], None,
                              ALU.mult).then_inc(probs_ready, 1)

        def rest_of_od(i):
            hd, t = DSA_JOBS[i]
            if t == TILES - 1:
                dve.wait_ge(od_hi_ready, hd + 1)
                dve.tensor_tensor(od_lo[:, hd], result_bank[RESULT[("mixer", "dsa", hd)] % 2][:, 0:SEQ],
                                  od_hi[:, hd].bitcast(F32), ALU.subtract).then_inc(od_ready, 1)

        def filled(i):
            name, m = DSA_FILLERS[i]
            if name == "ms":
                gate_of(name, m)
                return
            dve.wait_ge(gate_ready, 16 * DEPTH + m + 1)
            dst = mgate["g"][:, m]
            dve.scalar_tensor_tensor(dst, dst, 1.0, line_wait(("mixer", name, m))[:, 0:SEQ], ALU.add,
                                     ALU.mult).then_inc(y_used, 1)

        for i in range(len(DSA_JOBS) + 2):
            if i < len(DSA_JOBS):
                dsa_maxes(i)
                dsa_shares(i)
                filled(i)
            if i >= 2:
                rest_of_od(i - 2)

        dve.wait_ge(gate_ready, 16 * DEPTH + 2 * KT)
        for m in range(KT):
            bank = line_wait(("mixer", "ys", m))
            dve.scalar_tensor_tensor(prod[:, m % 2, 0:SEQ], mgate["s"][:, m], 1.0, bank[:, 0:SEQ], ALU.add,
                                     ALU.mult).then_inc(y_used, 1)
            dve.wait_ge(y_used, 16 * DEPTH + KT + m + 1)
            dve.tensor_tensor(wide[:, m, 0:SEQ], prod[:, m % 2, 0:SEQ], mgate["g"][:, m],
                              ALU.add).then_inc(full_ready, 1)
            if m:
                rest_of_full("mixed2", m - 1, SEQ)
        rest_of_full("mixed2", KT - 1, SEQ)
        for m in range(KT):
            dve.scalar_tensor_tensor(h[:, m, 0:SEQ], line_wait(("mixer", "mix", m))[:, 0:SEQ], 0.5, h[:, m, 0:SEQ],
                                     ALU.mult, ALU.add).then_inc(h_ready, 1)
            dve.wait_ge(h_ready, H_BATCH["mixer"] + m + 1)
            rest_of_h("ffn1", m, SEQ)
        rstd_of(("ffn1", "norm"), SEQ, scale[:, 0:SEQ])
        dve.wait_ge(p_hi_ready, 1)
        dve.tensor_tensor(p_lo[:, :, :], p_in, p_hi[:, :, :].bitcast(F32), ALU.subtract).then_inc(p_ready, 1)
        ffn(1)

        rstd_of(("embed", "norm"), SEQ, scale[:, 0:SEQ])

        def embedded(m):
            dve.wait_ge(tanh_ready, 8 * DEPTH + KT + m + 1)
            dve.wait_ge(pp_ready, m + 1)
            dve.scalar_tensor_tensor(prod[:, m % 2, 0:SEQ], th[:, m % 2, 0:SEQ], 1.0, pp[:, m], ALU.add,
                                     ALU.mult).then_inc(pg_used, 1)
            dve.wait_ge(pg_used, m + 1)
            dve.tensor_tensor(h[:, m, 0:SEQ], h[:, m, 0:SEQ], prod[:, m % 2, 0:SEQ], ALU.add).then_inc(h_ready, 1)

        for m in range(KT):
            scaled_line(("embed", "pg", m), prod2[:, m % 2, 0:SEQ]).then_inc(pg_raw, 1)
            if m:
                embedded(m - 1)
            if m >= 2:
                add_square("final1", m - 2, m - 2, SEQ)
        embedded(KT - 1)
        add_square("final1", KT - 2, KT - 2, SEQ)
        add_square("final1", KT - 1, KT - 1, SEQ)
        dve.wait_ge(h_ready, H_BATCH["embed"] + KT)
        r = rstd_of(("final1", "norm"), SEQ)
        for k in range(KT):
            dve.scalar_tensor_tensor(wide[:, k, 0:SEQ], h[:, k, 0:SEQ], operand("g_final1")[:, k:k + 1], r, ALU.mult,
                                     ALU.mult).then_inc(out_ready, 1)

    @block.tensor
    def _(pe):
        def unit(u):
            pe.wait_ge(hi_cut, u + 1)
            pe.wait_ge(lo_cut, u + 1)
            return w_hi[:, u % CUT].rearrange("p (b c) -> p b c", c=P), \
                w_lo[:, u % CUT].rearrange("p (b c) -> p b c", c=P)

        def line_open(key):
            g = LINE[key]
            if g >= 2:
                name, count = LINE_READ[LINES[g - 2]]
                pe.wait_ge(signals[name], count)
            return line_bank[g % 2]

        def line(key, n, src=None, depth=KT, first=0, at=None, ready=None, last=None):
            if at is None:
                at = key[-1] % 2 * KT
            hi, lo = unit(UNIT[key])
            src_hi, src_lo = src or x_of[key[0]]
            bank = line_open(key)
            for k in range(depth):
                if last and k == depth - 1:
                    last()
                if ready:
                    ready(k)
                here = [(hi[:, at + k], src_hi), (hi[:, at + k], src_lo), (lo[:, at + k], src_hi)]
                for m, (stay, move) in enumerate(here):
                    ins = pe.matmul(bank[:, 0:n], stay, move[:, first + k, 0:n], start=(k, m) == (0, 0),
                                    stop=(k, m) == (depth - 1, 2))
            ins.then_inc(line_done, 1)

        def x_tile(batch):
            return lambda k: pe.wait_ge(x_ready, X_BATCH[batch] + k + 1)

        def stat_open(key):
            s = STAT[key]
            if s:
                pe.wait_ge(stat_read, s)

        def sums(key, tiles, mean):
            stat_open(key)
            for n, sq in enumerate(tiles):
                pe.wait_ge(squares_ready, SQUARES[key] + n + 1)
                ins = pe.matmul(stat_bank[:, 0:sq.shape[-1]], mean, sq, start=n == 0, stop=n == len(tiles) - 1)
            ins.then_inc(stat_done, 1)

        def norm_sum(name, n):
            stat_open((name, "norm"))
            pe.wait_ge(summed, SUMMED[name] + KT)
            pe.matmul(stat_bank[:, 0:n], mean_dm[:, :], sum_of[name][0][:, 0:n], start=True,
                      stop=True).then_inc(stat_done, 1)

        def result_open(key):
            r = RESULT[key]
            if r >= 2:
                name, count = RESULT_READ[RESULTS[r - 2]]
                pe.wait_ge(signals[name], count)
            return result_bank[r % 2]

        def score_open(key):
            s = SCORE[key]
            if s >= 2:
                name, count = SCORE_READ[SCORES[s - 2]]
                pe.wait_ge(signals[name], count)
            return score_bank[s % 2]

        ident = const("ident")

        def layer(i):
            name = f"layer{i}"
            line((name, "ka"), TOK, at=0, ready=x_tile(name), last=lambda: norm_sum(name, TOK))
            line((name, "va"), TOK, at=KT)

            def turn_v(n):
                pe.wait_ge(v_raw, 5 * i + n + 1)
                if n:
                    pe.wait_ge(v_ready, 2 * (5 * i + n))
                for t, w in key_tiles(TOK):
                    ins = pe.transpose(turn_bank[0:w, t * P:(t + 1) * P], prod2[:, n % 2, t * P:t * P + w], ident)
                ins.then_inc(v_turned, 1)

            def head_sum(n):
                sums((name, "head", n), [th[:, n % 2, :]], const("head_mean"))

            def rot(n):
                src = ka[:, :] if n == 0 else qa[:, n - 1]
                bank = result_open((name, "rot", n))
                pe.wait_ge(normed, 5 * i + n + 1)
                pe.matmul(bank[:, 0:TOK], const("rot"), src, start=True, stop=True).then_inc(rot_done, 1)

            if i == 0:
                pe.wait_ge(loaded, 16)
            for n, key in enumerate([("qa", c) for c in range(PAIRS)] + [("kb", c) for c in range(PAIRS)]):
                line((name, *key), TOK)
                if n >= 3:
                    rot(n - 3)
                if 1 <= n <= PAIRS + 1:
                    head_sum(n - 1)
                if n == 1:
                    turn_v(0)
            for c in range(PAIRS):
                line((name, "qb", c), TOK)
            for c in range(PAIRS):
                line((name, "vb", c), TOK)
                if c:
                    turn_v(c)
            turn_v(PAIRS)

            def scores(job, n):
                key = (name, *job)
                s = score_open(key)
                if job[0] == "Bm":
                    for hd in [*range(0, HEADS, 2), *range(1, HEADS, 2)]:
                        if hd == 1:
                            ins.then_inc(even_scores, 1)
                            pe.wait_ge(even_scores, i + 1)
                        r = slice(hd % 2 * HD, hd % 2 * HD + HD)
                        ins = pe.matmul(s[0:META, hd * META:(hd + 1) * META], qb[r, hd // 2, SEQ:TOK],
                                        kb[r, hd // 2, SEQ:TOK], start=True, stop=True)
                elif job[0] == "Am":
                    r = slice(job[1] * HD, job[1] * HD + HD)
                    ins = pe.matmul(s[0:PAIRS * META, 0:TOK], q_meta[r, :], ka[r, :], start=True, stop=True)
                else:
                    kind, c, half, t = job
                    r = slice(half * HD, half * HD + HD)
                    q, k = (qa, ka[r, :]) if kind == "A" else (qb, kb[r, c])
                    ins = pe.matmul(s[:, 0:TOK], q[r, c, t * P:(t + 1) * P], k, start=True, stop=kind == "A")
                    if kind == "B":
                        m = PAIRS * i + c
                        pe.wait_ge(rel_ready, m + 1)
                        ins = pe.matmul(s[:, 0:SEQ], const("flip"), rel[:, m % 2, t, half], start=False, stop=True)
                ins.then_inc(score_done, 1)

            def turn(job, n):
                pe.wait_ge(probs_ready, n + 1)
                r = TURN[(name, *job)]
                if r:
                    pe.wait_ge(turned_most, r)
                    pe.wait_ge(turned_rest, r)
                if job[0] == "Bm":
                    for hd in range(HEADS):
                        at = slice(hd * META, (hd + 1) * META)
                        ins = pe.transpose(turn_bank[0:META, at], probs[0:META, n % 2, at], ident[0:META, 0:META])
                else:
                    m = PAIRS * META if job[0] == "Am" else P
                    for kt, w in key_tiles(TOK):
                        ins = pe.transpose(turn_bank[0:w, kt * P:kt * P + m], probs[0:m, n % 2, kt * P:kt * P + w],
                                           ident[0:m, 0:m])
                ins.then_inc(turn_done, 1)

            def values(job, n):
                pe.wait_ge(turned_most, TURN[(name, *job)] + 1)
                pe.wait_ge(turned_rest, TURN[(name, *job)] + 1)
                tn = turned[:, n % 2]
                if job[0] == "Bm":
                    bank = result_open((name, "Bm"))
                    for hd in range(HEADS):
                        r = slice(hd % 2 * HD, hd % 2 * HD + HD)
                        ins = pe.matmul(bank[r, hd // 2 * META:(hd // 2 + 1) * META],
                                        vb[0:META, 2, hd * HD:(hd + 1) * HD], tn[0:META, hd * META:(hd + 1) * META],
                                        start=True, stop=True)
                else:
                    if job[0] == "Am":
                        half, m, at, v = job[1], PAIRS * META, 0, va[:, :, job[1] * HD:(job[1] + 1) * HD]
                        bank = result_open((name, "Am")) if half == 0 else result_bank[RESULT[(name, "Am")] % 2]
                    else:
                        kind, c, half, t = job
                        head = half if kind == "A" else 2 * c + half
                        m, at, v = P, t * P, (va if kind == "A" else vb)[:, :, head * HD:(head + 1) * HD]
                        key = (name, kind, c)
                        bank = result_open(key) if (half, t) == (0, 0) else result_bank[RESULT[key] % 2]
                    r = slice(half * HD, half * HD + HD)
                    for kt, w in key_tiles(TOK):
                        ins = pe.matmul(bank[r, at:at + m], v[0:w, kt], tn[0:w, kt * P:kt * P + m], start=kt == 0,
                                        stop=kt == 2)
                ins.then_inc(valued, 1)

            pe.wait_ge(roped, 9 * i + 9)
            pe.wait_ge(kq_ready, 8 * i + 8)
            pe.wait_ge(v_ready, 10 * i + 10)
            for t in range(J + 2):
                if t < J:
                    scores(JOBS[t], J * i + t)
                if t < len(FILLERS):
                    kind, m = FILLERS[t]
                    if kind == "ya":
                        pe.wait_ge(y_ready, KT * i + PAIRS)
                        line((name, kind, m), TOK, y_of[name], PAIRS, 0, m % 4 * PAIRS)
                    else:
                        line((name, kind, m), TOK)
                if 1 <= t <= J:
                    turn(JOBS[t - 1], J * i + t - 1)
                if t >= 2:
                    values(JOBS[t - 2], J * i + t - 2)
            for m in range(KT):
                line((name, "yb", m), TOK, y_of[name], PAIRS, PAIRS, m % 4 * PAIRS,
                     ready=(lambda k: pe.wait_ge(y_ready, KT * i + PAIRS + k + 1)) if m == 0 else None)
            for m in range(KT):
                line((name, "out", m), TOK, x_of[f"mixed{i}"], ready=x_tile(f"mixed{i}") if m == 0 else None)

        pe.wait_ge(set_up, 2)
        for i in range(DEPTH):
            layer(i)

        def two_norm_sums():
            stat_open(("ffn0", "norm"))
            pe.wait_ge(summed, SUMMED["final0"] + 2 * KT)
            for n in range(2):
                pe.matmul(stat_bank[:, n * SEQ:(n + 1) * SEQ], mean_dm[:, :], sum_of["final0"][n][:, 0:SEQ],
                          start=True, stop=True).then_inc(stat_done, 1)

        def ffn(f):
            name = f"ffn{f}"
            for j in range(FT):
                if j == 0:
                    line((name, "gate", j), SEQ, at=0, ready=x_tile(name),
                         last=(two_norm_sums, lambda: norm_sum(name, SEQ))[f])
                else:
                    line((name, "gate", j), SEQ, at=0)
                line((name, "up", j), SEQ, at=KT)
            for m in range(KT):
                for half in range(2):
                    first = half * FT // 2
                    line((name, "down", m, half), SEQ, (act_hi, act_lo), FT // 2, first, 0,
                         ready=(lambda k: pe.wait_ge(act_ready, FT * f + first + k + 1)) if m == 0 else None)

        ffn(0)

        line(("mixer", "low"), SEQ, at=0, ready=x_tile("mixer"), last=lambda: norm_sum("mixer", SEQ))
        line(("mixer", "ckv"), SEQ, at=KT)
        line(("mixer", "gk", 0), SEQ)
        bank = result_open(("mixer", "index_w"))
        pe.wait_ge(low_ready, 1)
        for t in range(TILES):
            ins = pe.transpose(bank[:, t * SH:(t + 1) * SH], low[32:32 + SH, t * P:(t + 1) * P],
                               ident[32:32 + SH, 32:32 + SH])
        ins.then_inc(index_w_turned, 1)
        pe.wait_ge(loaded2, 48)
        for i in range(GH // 2):
            bank = score_open(("mixer", "alpha", i))
            for g in range(2 * i, 2 * i + 2):
                ins = pe.matmul(bank[:, g % 2 * SEQ:(g % 2 + 1) * SEQ],
                                operand("alpha_w", LOWRANK)[:, g * GDK:(g + 1) * GDK], low[0:LOWRANK],
                                start=True, stop=True)
            ins.then_inc(score_done, 1)
        bank = result_open(("mixer", "rel"))
        pe.matmul(bank[0:SH, :], operand("rel", 32), const("bucket", 32), start=True, stop=True).then_inc(row_done, 1)
        line(("mixer", "gk", 1), SEQ)
        pe.wait_ge(means_ready, 2)
        sums(("mixer", "ckv"), [th[:, 0, 0:SEQ]], mean_p[:, :])
        line(("mixer", "gk", 2), SEQ)
        line(("mixer", "gk", 3), SEQ)
        for c in range(GH):
            line(("mixer", "gq", c), SEQ)
        pe.wait_ge(ckv_ready, 1)
        pe.wait_ge(turned_rest, TURN[("mixer", "ckv")])
        for t in range(TILES):
            ins = pe.transpose(turn_bank[:, t * P:(t + 1) * P], ckv[:, t * P:(t + 1) * P], ident)
        ins.then_inc(turn_done, 1)

        def turn_gv(c):
            pe.wait_ge(gv_raw, c + 1)
            if c:
                pe.wait_ge(gv_ready, c)
            else:
                pe.wait_ge(turned_most, TURN[("mixer", "ckv")] + 1)
            for t in range(TILES):
                ins = pe.transpose(turn_bank[:, t * P:(t + 1) * P], prod2[:, c % 2, t * P:(t + 1) * P], ident)
            ins.then_inc(gv_turned, 1)

        for n in range(len(HALVES) + 1):
            for kind, c in LEVEL_FILLERS[2 * n:2 * n + 2]:
                line(("mixer", kind, c), SEQ)
            last = n == len(HALVES)
            if n:
                for kind, c in LEVEL_FILLERS[2 * n - 2:2 * n]:
                    if kind == "gv":
                        turn_gv(c)
            if not last:
                pe.wait_ge(level_ready, n + 1)
            for t in range(TILES):
                bank = score_open(("mixer", "level", n, t))
                for g in range(GH):
                    at = slice(g * SEQ + t * P, g * SEQ + (t + 1) * P)
                    keys, queries = (gk, gq[:, g, t * P:(t + 1) * P]) if last else (gate_k, gate_q[:, at])
                    ins = pe.matmul(bank[:, g * P:(g + 1) * P], keys[:, at], queries, start=True, stop=True)
                ins.then_inc(score_done, 1)
        pe.wait_ge(level_ready, len(HALVES) + 1)
        for t in range(TILES):
            bank = score_open(("mixer", "kdt", t))
            for g in range(GH):
                ins = pe.transpose(bank[:, g * P:(g + 1) * P], gate_k[:, g * SEQ + t * P:g * SEQ + (t + 1) * P], ident)
            ins.then_inc(score_done, 1)
        pe.wait_ge(gv_ready, 2 * GH)

        def head_mean_gla(g):
            sums(("mixer", "gla", g), [th[:, e, 0:SEQ] for e in range(2)], mean_gdv[:, :])

        for g in range(GH):
            line(("mixer", "gr", 2 * g), SEQ)
            if g:
                head_mean_gla(g - 1)
            line(("mixer", "gr", 2 * g + 1), SEQ)
            for c in range(3):
                pe.wait_ge(kdt_ready, c // 2 + 1)
                bank = score_open(("mixer", "state", g, c))
                rows = slice(c % 2 * CHUNK, (c % 2 + 1) * CHUNK)
                at = (c // 2 * GH + g) * P
                pe.matmul(bank[:, 0:GDV], fall[rows, at:at + P], gv[rows, c // 2, g * GDV:(g + 1) * GDV],
                          start=True, stop=True).then_inc(score_done, 1)
            for e in range(2):
                bank = result_open(("mixer", "gla", g, e))
                pe.wait_ge(level_used, TILES * (len(HALVES) + 1))
                out_rows = slice(g * GDV + e * P, g * GDV + (e + 1) * P)
                for t in range(TILES):
                    pe.matmul(bank[:, t * P:(t + 1) * P], gv[:, t, out_rows], pairs[:, t, g], start=t == 0, stop=False)
                pe.wait_ge(state_ready, 3 * g + 3)
                for c in range(1, SEQ // CHUNK):
                    at = slice(c * CHUNK, (c + 1) * CHUNK)
                    ins = pe.matmul(bank[:, at], states[:, c - 1, e * P:(e + 1) * P],
                                    gate_q[:, g * SEQ + c * CHUNK:g * SEQ + (c + 1) * CHUNK], start=False,
                                    stop=c == SEQ // CHUNK - 1)
                ins.then_inc(gla_done, 1)

        line(("mixer", "dq", 0), SEQ)
        head_mean_gla(GH - 1)
        line(("mixer", "dq", 1), SEQ)
        pe.wait_ge(index_q_ready, PAIRS)
        pe.wait_ge(index_k_ready, 2)
        for n, (t, hd) in enumerate((t, hd) for t in range(TILES) for hd in range(SH)):
            bank = score_open(("mixer", "dots", t, hd))
            rows = slice(hd % 2 * HD, (hd % 2 + 1) * HD)
            pe.matmul(bank[:, 0:(t + 1) * P], index_q[rows, hd // 2, t * P:(t + 1) * P], index_k[rows, 0:(t + 1) * P],
                      start=True, stop=True).then_inc(score_done, 1)
            if n % 2 and n // 2 + 2 < SH:
                line(("mixer", "dq", n // 2 + 2), SEQ)
        for m in range(KT):
            line(("mixer", "mg", m), SEQ)

        def dsa_scores(i):
            hd, t = DSA_JOBS[i]
            bank = score_open(("mixer", "dsa", hd, t))
            pe.wait_ge(dq_ready, hd + 1)
            keys = (t + 1) * P
            pe.matmul(bank[:, 0:keys], dq[:, hd, t * P:(t + 1) * P], ckv[:, 0:keys], start=True, stop=False)
            pe.wait_ge(rbias_in[hd % 2], 16 * TILES * (hd // 2 + 1))
            pe.matmul(bank[:, 0:keys], const("flip"), rbias[:, hd % 2, t * P:t * P + keys], start=False,
                      stop=True).then_inc(score_done, 1)

        def dsa_turn(i):
            hd, t = DSA_JOBS[i]
            n = DEPTH * J + i
            pe.wait_ge(probs_ready, n + 1)
            pe.wait_ge(turned_most, TURN[("mixer", "dsa", hd, t)])
            for kt in range(t + 1):
                ins = pe.transpose(turn_bank[:, kt * P:(kt + 1) * P], probs[:, n % 2, kt * P:(kt + 1) * P], ident)
            ins.then_inc(turn_done, 1)

        def dsa_values(i):
            hd, t = DSA_JOBS[i]
            n, key = DEPTH * J + i, ("mixer", "dsa", hd)
            bank = result_open(key) if t == 0 else result_bank[RESULT[key] % 2]
            pe.wait_ge(turned_most, TURN[("mixer", "dsa", hd, t)] + 1)
            for kt in range(t + 1):
                ins = pe.matmul(bank[:, t * P:(t + 1) * P], ckv_t[:, kt], turned[:, n % 2, kt * P:(kt + 1) * P],
                                start=kt == 0, stop=kt == t)
            ins.then_inc(valued, 1)

        for i in range(len(DSA_JOBS) + 2):
            if i < len(DSA_JOBS):
                dsa_scores(i)
                if i == KT:
                    pe.wait_ge(gg_ready, KT)
                name, m = DSA_FILLERS[i]
                line(("mixer", name, m), SEQ, (gg_hi, gg_lo) if name == "yg" else None)
            if 1 <= i <= len(DSA_JOBS):
                dsa_turn(i - 1)
            if i >= 2:
                dsa_values(i - 2)
        for m in range(KT):
            line(("mixer", "ys", m), SEQ, (od_hi, od_lo),
                 ready=(lambda k: pe.wait_ge(od_ready, k + 1)) if m == 0 else None)
        for m in range(KT):
            line(("mixer", "mix", m), SEQ, x_of["mixed2"], ready=x_tile("mixed2") if m == 0 else None)

        ffn(1)
        pe.wait_ge(p_ready, 1)
        for m in range(KT):
            line(("embed", "pp", m), SEQ, (p_hi, p_lo), 2, 0, 2 * m)
        for m in range(KT):
            if m == 0:
                line(("embed", "pg", m), SEQ, ready=x_tile("embed"), last=lambda: norm_sum("embed", SEQ))
            else:
                line(("embed", "pg", m), SEQ)
        norm_sum("final1", SEQ)

    al.close()


def pair_heads(width=HD):
    return np.concatenate([np.r_[c * width:(c + 1) * width, (c + PAIRS) * width:(c + PAIRS + 1) * width]
                           for c in range(PAIRS)])


def blocks_of(w):
    k, n = w.shape
    return w.reshape(k // P, P, n // P, P).transpose(1, 2, 0, 3).reshape(P, -1)


def weight_stream(a):
    rows = []
    cols = np.cumsum([0, 512, 128, 128, 512, 512, 512, 512, 512, 1024, 1024])
    heads = pair_heads()
    for i in range(DEPTH):
        qa, ka, va, za, qb, kb, vb, zb, ga, gb = (a["w_in"][i][:, cols[j]:cols[j + 1]] for j in range(10))
        rows += [blocks_of(w) for w in (ka, va, qa[:, heads], kb, qb, vb, za[:, heads], zb, ga, gb)]
        rows += [blocks_of(w) for w in (a["w_o_attn"][i][heads], a["w_o_na"][i], a["w_out"][i])]

    def ffn(w_in, w_out):
        both = np.stack([w_in[:, :DFF].reshape(DM, FT, P), w_in[:, DFF:].reshape(DM, FT, P)], 2)
        down = blocks_of(w_out).reshape(P, 2 * KT, FT // 2 * P)
        down = np.pad(down, ((0, 0), (0, 0), (0, (UB - FT // 2) * P)))
        return [blocks_of(both.reshape(DM, 2 * DFF)), down.reshape(P, -1)]

    rows += ffn(a["ffn1_w_in_2"][0], a["ffn1_w_out_2"][0])
    sizes = (GH * GDK, GH * GDK, GH * GDV, GH * GDV, LOWRANK, SH * P, P, SH * HD, HD, SH, 2 * DM)
    cols = np.cumsum((0,) + sizes)
    gq, gk, gv, gr, ga, dq, dkv, iq, ik, iw, gates = (a["mix_w_in_2"][0][:, cols[j]:cols[j + 1]] for j in range(11))
    low = np.zeros((DM, P), np.float32)
    low[:, :LOWRANK], low[:, 32:32 + SH], low[:, HD:] = ga, iw, ik
    rows += [blocks_of(w) for w in (low, dkv, gk, gq, gv, iq, gr, dq, gates)]
    rows += [blocks_of(a[n][0]) for n in ("gla_w_out_2", "dsa_w_out_2", "mix_w_out_2")]
    rows += ffn(a["ffn2_w_in_2"][0], a["ffn2_w_out_2"][0])
    rows += [blocks_of(a["ple_w_proj_2"][0]), blocks_of(a["ple_w_gate_2"][0])]
    return np.ascontiguousarray(np.concatenate(rows, 1).reshape(P, len(UNITS), UB * P).transpose(1, 0, 2))


def by_feature(v):
    return v.reshape(-1, P).T


def small_operands(a):
    s, s2 = np.zeros((P, SMALL_W), np.float32), np.zeros((P, SMALL2_W), np.float32)

    def put(name, v):
        at, w = (SMALL.get(name) or SMALL2[name])
        (s if name in SMALL else s2)[:v.shape[0], at:at + w] = v

    gains = dict(layer0=a["norm_g"][0], layer1=a["norm_g"][1], final0=a["final_norm_g"], ffn0=a["ffn1_norm_2"][0],
                 mixer=a["mix_norm_2"][0], ffn1=a["ffn2_norm_2"][0], embed=a["ple_norm_2"][0], final1=a["final_norm_2"])
    for name, g in gains.items():
        put(f"g_{name}", by_feature(g))
    for i in range(DEPTH):
        put(f"q_gain{i}", np.tile(a["q_norm_g"][i], 2)[:, None])
        put(f"k_gain{i}", np.tile(a["k_norm_g"][i], 2)[:, None])
    put("gla_gain", by_feature(a["gla_out_norm_2"][0]))
    put("ckv_gain", by_feature(a["ckv_norm_2"][0]))
    put("alpha_b", by_feature(a["gla_alpha_b_2"][0]))
    put("alpha_w", a["gla_alpha_w_2"][0])
    put("rel", a["rel_bias_2"])
    return s, s2


def constants():
    c, c2 = np.zeros((P, CONST_W), np.float32), np.zeros((P, CONST2_W), np.float32)

    def put(name, v):
        at, w = (CONST.get(name) or CONST2[name])
        (c if name in CONST else c2)[:v.shape[0], at:at + w] = v

    p = np.arange(P)
    put("ident", np.eye(P))
    put("flip", np.eye(P)[::-1])
    put("head_mean", (p[:, None] // HD == p[None] // HD) / HD)
    quarter = HD // 4
    rot = np.zeros((P, P))
    for m in range(P):
        low = m % (2 * quarter) < quarter
        rot[m + quarter if low else m - quarter, m] = -1.0 if low else 1.0
    put("rot", rot)
    t = np.arange(SEQ)
    zeros = np.zeros(META)
    row = np.concatenate([t // GRID_W, zeros]).astype(np.float32)
    col = np.concatenate([t % GRID_W, zeros]).astype(np.float32)
    inv = np.float32(10000.0) ** (-np.arange(0, HD // 2, 2, dtype=np.float32) / np.float32(HD // 2))
    ang = np.concatenate([np.tile(row[:, None] * inv, 2), np.tile(col[:, None] * inv, 2)], 1).astype(np.float32)
    put("cos", np.tile(np.cos(ang).T, (2, 1)))
    put("sin", np.tile(np.sin(ang).T, (2, 1)))
    g = np.arange(GRID_W)
    start = np.clip(g - WIN // 2, 0, GRID_W - WIN)[:, None]
    put("window", np.tile(np.where((g[None] >= start) & (g[None] < start + WIN), 0.0, NEG)[::-1], (2, 1)))
    put("keep", np.tile((np.arange(GH * SEQ) % CHUNK != 0)[None], (P, 1)))
    put("later", np.where(p[None] <= p[:, None], 0.0, NEG))
    d = np.maximum(SEQ - 1 - np.arange(2 * SEQ), 0)
    half = 16
    ratio = np.maximum(d, 1).astype(np.float32) / np.float32(half)
    large = half + (np.log(ratio) / np.float32(np.log(128 / half)) * np.float32(half)).astype(np.int32)
    bucket = np.where(d < half, d, np.minimum(large, 31))
    put("bucket", np.arange(32)[:, None] == bucket[None])
    return c, c2


def level_masks():
    s, t = np.arange(P)[:, None], np.arange(P)[None]
    m = [(s // (2 * h) == t // (2 * h)) & (s // h % 2 == 0) & (t // h % 2 == 1) for h in HALVES] + [s == t]
    return np.ascontiguousarray(np.stack(m, 1).astype(np.uint32))


def kernel(**inputs):
    import concourse.bacc as bacc
    from concourse.bass_utils import run_bass_kernel_spmd

    a = {n: np.asarray(v) for n, v in inputs.items()}
    tokens = np.concatenate([a["x"][0], a["meta_tokens"]])
    arrays = {
        "weights": weight_stream(a),
        "tokens": np.ascontiguousarray(tokens.reshape(TOK, KT, P).transpose(2, 1, 0)),
        "embeds": np.ascontiguousarray(a["p_2"][0, 0].reshape(SEQ, -1, P).transpose(2, 1, 0)),
        "small": small_operands(a)[0],
        "small2": small_operands(a)[1],
        "rpb": np.ascontiguousarray(a["na_rpb"]),
        "consts": constants()[0],
        "consts2": constants()[1],
        "levels": level_masks(),
    }
    nc = bacc.Bacc("TRN2", target_bir_lowering=False, num_devices=1)
    arrays = {f"in_{n}": v for n, v in arrays.items()}
    args = [nc.dram_tensor(n, v.shape, mybir.dt.from_np(v.dtype), kind="ExternalInput").ap() for n, v in arrays.items()]
    out = nc.dram_tensor("out", (P, KT, SEQ), F32, kind="ExternalOutput").ap()
    hybrid_blocks_kernel(nc, *args, out)
    r = run_bass_kernel_spmd(nc, [arrays], core_ids=[0])
    y = r.results[0]["out"]
    return np.ascontiguousarray(y.transpose(2, 1, 0)).reshape(1, SEQ, DM)
```

```python
from contextlib import ExitStack

import numpy as np

import concourse.bass as bass
from concourse import mybir

P = 128
DM = 1024
KT = DM // P
EPS = 1e-6
F32 = mybir.dt.float32
F32R = mybir.dt.float32r
U32 = mybir.dt.uint32
ALU = mybir.AluOpType
ACT = mybir.ActivationFunctionType
AX = mybir.AxisListType

DEPTH = 2
SEQ = 256
META = 16
TOK = SEQ + META
HD = 64
HEADS = 8
PAIRS = HEADS // 2
GRID_W = 64
ROWS = SEQ // GRID_W
WIN = 16
RPB_R, RPB_C = 15, 31
NEG = -1.0e30
TILES = SEQ // P

DFF = 2816
FT = DFF // P
GH, GDK, GDV, CHUNK = 4, 128, 256, 64
LOWRANK, TAU = 16, 16.0
SH = 8
TOPK = min(256, SEQ // 4)
HALVES = (32, 16, 8, 4, 2, 1)
TAKEN = -3.0e38

RAW = 3
CUT = 3
UB = 16


def key_tiles(n):
    return [(i, min(P, n - i * P)) for i in range((n + P - 1) // P)]


def units_of_layer():
    u = [[("ka",), ("va",)]]
    for name in ("qa", "kb", "qb"):
        u += [[(name, 2 * i), (name, 2 * i + 1)] for i in range(2)]
    for name in ("vb", "za", "zb"):
        u += [[(name, 2 * i), (name, 2 * i + 1)] for i in range(2)]
    for name in ("ga", "gb"):
        u += [[(name, 2 * i), (name, 2 * i + 1)] for i in range(4)]
    u += [[(name, 4 * i + j) for j in range(4)] for name in ("ya", "yb") for i in range(2)]
    u += [[("out", 2 * i), ("out", 2 * i + 1)] for i in range(4)]
    return u


def units_of_ffn():
    return [[("gate", j), ("up", j)] for j in range(FT)] + [
        [("down", m, half)] for m in range(KT) for half in range(2)]


def units_of_mixer():
    u = [[("low",), ("ckv",)]]
    for name in ("gk", "gq"):
        u += [[(name, 2 * i), (name, 2 * i + 1)] for i in range(2)]
    for name, first, end in (("gv", 0, 8), ("iq", 0, 4), ("gr", 0, 8), ("dq", 0, 2), ("mg", 0, 2), ("dq", 2, 8),
                             ("mg", 2, 8), ("ms", 0, 8), ("yg", 0, 8), ("ys", 0, 8), ("mix", 0, 8)):
        u += [[(name, i), (name, i + 1)] for i in range(first, end, 2)]
    return u


def units_of_embedding():
    return [[("pp", m) for m in range(KT)]] + [[("pg", 2 * i), ("pg", 2 * i + 1)] for i in range(4)]


def plan():
    stages = {}
    units = []
    for stage, u in ([(f"layer{i}", units_of_layer()) for i in range(DEPTH)]
                     + [("ffn0", units_of_ffn()), ("mixer", units_of_mixer()), ("ffn1", units_of_ffn()),
                        ("embed", units_of_embedding())]):
        stages[stage] = len(units)
        units += [[(stage, *g) for g in unit] for unit in u]
    blocks = [UB] * len(units)
    for s in ("ffn0", "ffn1"):
        for i in range(2 * KT):
            blocks[stages[s] + FT + i] = FT // 2
    return stages, units, blocks


STAGES, UNITS, BLOCKS = plan()
LINES = [g for unit in UNITS for g in unit]
LINE = {g: i for i, g in enumerate(LINES)}
UNIT = {g: u for u, unit in enumerate(UNITS) for g in unit}


HEAD_LINES = [(name, c) for name in ("qa", "kb", "qb", "vb") for c in range(PAIRS)]


def cuts(u):
    return u + 2


def last_line(u):
    return LINE[UNITS[u][-1]]


def attention_jobs(meta):
    a = [("A", c, half, t) for c in range(PAIRS) for half in range(2) for t in range(TILES)]
    b = [("B", c, half, t) for c in range(PAIRS) for half in range(2) for t in range(TILES)]
    if not meta:
        return a + b
    return a[:4] + [("Am", 0), ("Am", 1)] + a[4:] + [("Bm",)] + b


JOBS = [attention_jobs(i < DEPTH - 1) for i in range(DEPTH)]
WIDTH = [TOK if i < DEPTH - 1 else SEQ for i in range(DEPTH)]
JOB = [sum(map(len, JOBS[:i])) for i in range(DEPTH + 1)]


def tile_done(i, job):
    if job == ("Am", 1):
        return 0
    if len(job) == 4 and job[2:] == (1, TILES - 1) and (job[:2] != ("A", 0) or i == DEPTH - 1):
        return PAIRS * (job[0] == "B") + job[1]
    return None


FILLERS = [(n, m) for n, k in (("za", 4), ("zb", 4), ("ga", 8), ("gb", 8), ("ya", 8)) for m in range(k)]
GATES = sum(f[0] != "ya" for f in FILLERS)

STATS = []
for _l in range(DEPTH):
    STATS += [(f"layer{_l}", "norm")] + [(f"layer{_l}", "head", i) for i in range(PAIRS + 1)]
STATS += [("ffn0", "norm"), ("final0", "norm"), ("mixer", "norm"), ("mixer", "ckv")]
STATS += [("mixer", "gla", h) for h in range(GH)] + [("ffn1", "norm"), ("embed", "norm"), ("final1", "norm")]
STAT = {k: i for i, k in enumerate(STATS)}
NORMS = ["layer0", "layer1", "final0", "ffn0", "mixer", "ffn1", "embed", "final1"]

SCORES = [(f"layer{_l}", *j) for _l in range(DEPTH) for j in JOBS[_l]]
SCORES += [("mixer", "alpha", i) for i in range(2)]
SCORES += [("mixer", "level", n, t) for n in range(len(HALVES) + 1) for t in range(TILES)]
SCORES += [("mixer", "kdt", t) for t in range(TILES)]
SCORES += [("mixer", "state", h, c) for h in range(GH) for c in range(3)]
SCORES += [("mixer", "dots", t, h) for t in range(TILES) for h in range(SH)]
SCORES += [("mixer", "dsa", h, t) for h in range(SH) for t in range(TILES)]
SCORE = {k: i for i, k in enumerate(SCORES)}

RESULTS = []
for _l in range(DEPTH):
    RESULTS += [(f"layer{_l}", "rot", i) for i in range(PAIRS + 1)]
    for _j in JOBS[_l]:
        _k = (f"layer{_l}", *_j[:2 if len(_j) == 4 else 1])
        if _k not in RESULTS:
            RESULTS.append(_k)
RESULTS += [("mixer", "index_w"), ("mixer", "rel")]
RESULTS += [("mixer", "gla", h, e) for h in range(GH) for e in range(2)]
RESULTS += [("mixer", "dsa", h) for h in range(SH)]
RESULT = {k: i for i, k in enumerate(RESULTS)}

TURNS = [(f"layer{_l}", *j) for _l in range(DEPTH) for j in JOBS[_l]]
TURNS += [("mixer", "ckv")] + [("mixer", "dsa", h, t) for h in range(SH) for t in range(TILES)]
TURN = {k: i for i, k in enumerate(TURNS)}



def columns(widths):
    at, places = 0, {}
    for name, w in widths:
        places[name] = (at, w)
        at += w
    return places, at


SMALL, SMALL_W = columns([(f"g_{n}", KT) for n in NORMS] + [(f"q_gain{i}", 1) for i in range(DEPTH)]
                         + [(f"k_gain{i}", 1) for i in range(DEPTH)])
SMALL2, SMALL2_W = columns([("gla_gain", KT), ("ckv_gain", 1), ("alpha_b", GH), ("alpha_w", GH * GDK), ("rel", SH)])
CONST, CONST_W = columns([("ident", P), ("flip", P), ("head_mean", P),
                          ("rot", P), ("cos", TOK), ("sin", TOK), ("window", GRID_W)])
CONST2, CONST2_W = columns([("keep", GH * SEQ), ("later", P), ("bucket", 2 * SEQ)])


SQUARES, _n = {}, 0
for _k in STATS:
    SQUARES[_k] = _n
    _n += {"norm": KT, "head": 1, "ckv": 1, "gla": 2}[_k[1]]
SQUARES[("final0", "norm")] = SQUARES[("ffn0", "norm")]
X_BATCH = {k: KT * i for i, k in enumerate(["layer0", "mixed0", "layer1", "mixed1", "ffn0", "mixer", "mixed2", "ffn1",
                                            "embed"])}
FULL_BATCH = {k: KT * i for i, k in enumerate(["mixed0", "mixed1", "final0", "mixed2"])}
H_BATCH = {k: KT * i for i, k in enumerate(["layer0", "layer1", "final0", "ffn0", "mixer", "ffn1", "embed"])}
READS = {"layer1": "layer0", "final0": "layer1", "mixer": "ffn0", "ffn1": "mixer", "embed": "ffn1",
         "final1": "embed"}
SUMMED, _n = {}, 0
for _k in ("layer0", "layer1", "final0", "mixer", "ffn1", "embed", "final1"):
    SUMMED[_k] = _n
    _n += KT * (2 if _k == "final0" else 1)
TURN_OF_JOB = [i for i, k in enumerate(TURNS) if k != ("mixer", "ckv")]
NU = len(UNITS)


LINE_READ, SCORE_READ, RESULT_READ = {}, {}, {}
for _i in range(DEPTH):
    _l = f"layer{_i}"
    for _c in range(PAIRS + 1):
        LINE_READ[(_l, "qa", _c - 1) if _c else (_l, "ka")] = ("raw_head", 5 * _i + _c + 1)
        LINE_READ[(_l, "vb", _c - 1) if _c else (_l, "va")] = ("v_raw", 5 * _i + _c + 1)
        RESULT_READ[(_l, "rot", _c)] = ("rot_used", 5 * _i + _c + 1)
    for _n, _f in enumerate(FILLERS[:GATES]):
        LINE_READ[(_l, *_f)] = ("gate_raw", GATES * _i + _n + 1)
    for _c in range(PAIRS):
        for _n in range(2):
            LINE_READ[(_l, ("kb", "qb")[_n], _c)] = ("kq_ready", 8 * _i + 4 * _n + _c + 1)
            RESULT_READ[(_l, "AB"[_n], _c)] = ("pair_gated", 8 * _i + 4 * _n + _c + 1)
            if (_l, "AB"[_n] + "m") in RESULT:
                RESULT_READ[(_l, "AB"[_n] + "m")] = ("gated", 2 * _i + _n + 1)
    for _m in range(KT):
        for _n in range(2):
            LINE_READ[(_l, ("ya", "yb")[_n], _m)] = ("y_used", 16 * _i + KT * _n + _m + 1)
        LINE_READ[(_l, "out", _m)] = ("h_ready", H_BATCH[_l] + _m + 1)
    for _n, _j in enumerate(JOBS[_i]):
        SCORE_READ[(_l, *_j)] = ("maxed" if _j[0] == "Bm" else "exped", JOB[_i] + _n + 1)
for _f in range(2):
    for _n in range(FT):
        LINE_READ[(f"ffn{_f}", "gate", _n)] = ("act_raw", FT * _f + _n + 1)
        LINE_READ[(f"ffn{_f}", "up", _n)] = ("act_up", FT * _f + _n + 1)
    for _m in range(KT):
        LINE_READ[(f"ffn{_f}", "down", _m, 0)] = ("down_used", KT * _f + _m + 1)
        LINE_READ[(f"ffn{_f}", "down", _m, 1)] = ("h_ready", H_BATCH[f"ffn{_f}"] + _m + 1)
_m = "mixer"
LINE_READ[(_m, "low")] = ("low_ready", 1)
LINE_READ[(_m, "ckv")] = ("ckv_raw", 1)
RESULT_READ[(_m, "index_w")] = ("index_w_ready", 1)
RESULT_READ[(_m, "rel")] = ("row_ready", 1)
for _t in range(TILES):
    SCORE_READ[(_m, "alpha", _t)] = ("alpha_used", 2 * _t + 2)
    SCORE_READ[(_m, "kdt", _t)] = ("kdt_ready", _t + 1)
    for _n in range(len(HALVES) + 1):
        SCORE_READ[(_m, "level", _n, _t)] = ("level_used", TILES * _n + _t + 1)
    for _h in range(SH):
        SCORE_READ[(_m, "dots", _t, _h)] = ("relued", SH * _t + _h + 1)
        SCORE_READ[(_m, "dsa", _h, _t)] = ("exped", JOB[DEPTH] + TILES * _h + _t + 1)
for _n in range(4):
    LINE_READ[(_m, "gk", _n)] = ("gla_in", _n + 1)
    LINE_READ[(_m, "gq", _n)] = ("gla_in", GH + _n + 1)
    LINE_READ[(_m, "iq", _n)] = ("index_q_ready", _n + 1)
    for _t in range(3):
        SCORE_READ[(_m, "state", _n, _t)] = ("state_ready", 3 * _n + _t + 1)
    for _t in range(2):
        RESULT_READ[(_m, "gla", _n, _t)] = ("squares_ready", SQUARES[(_m, "gla", _n)] + _t + 1)
for _n in range(KT):
    LINE_READ[(_m, "gv", _n)] = ("gv_raw", _n + 1)
    LINE_READ[(_m, "gr", _n)] = ("gr_raw", _n + 1)
    LINE_READ[(_m, "dq", _n)] = ("dq_ready", _n + 1)
    LINE_READ[(_m, "mg", _n)] = ("gate_raw", GATES * DEPTH + _n + 1)
    LINE_READ[(_m, "ms", _n)] = ("gate_raw", GATES * DEPTH + KT + _n + 1)
    LINE_READ[(_m, "yg", _n)] = ("y_used", 16 * DEPTH + _n + 1)
    LINE_READ[(_m, "ys", _n)] = ("y_used", 16 * DEPTH + KT + _n + 1)
    LINE_READ[(_m, "mix", _n)] = ("h_ready", H_BATCH[_m] + _n + 1)
    RESULT_READ[(_m, "dsa", _n)] = ("od_ready", _n + 1)
    LINE_READ[("embed", "pp", _n)] = ("pp_ready", _n + 1)
    LINE_READ[("embed", "pg", _n)] = ("pg_raw", _n + 1)
assert set(LINE_READ) == set(LINES) and set(SCORE_READ) == set(SCORES) and set(RESULT_READ) == set(RESULTS)

LINE_BANK, LINE_BEFORE, _last = [], [], {}
for _g, _k in enumerate(LINES):
    if _k[0] in STAGES and UNITS[STAGES[_k[0]]][0] == _k and _k[0] != "embed":
        for _r in [_r for _r in RESULTS if STAGES[_r[0]] < STAGES[_k[0]]][-2:]:
            if STAGES[_r[0]] >= STAGES[_k[0]] - len(units_of_ffn()) - len(units_of_mixer()) and _k[0] != "mixer":
                _last[2 + RESULT[_r] % 2] = RESULT_READ[_r]
    if _k[0] in ("ffn0", "ffn1", "embed"):
        LINE_BANK.append(_g % 4)
    elif _k[1:] in (("qa", 0), ("qa", 1)):
        LINE_BANK.append(2 + _k[2])
    elif _k == ("mixer", "gk", 0):
        LINE_BANK.append(2 + RESULT[("mixer", "rel")] % 2)
    else:
        LINE_BANK.append(_g % 2)
    LINE_BEFORE.append(_last.get(LINE_BANK[-1]))
    _last[LINE_BANK[-1]] = LINE_READ[_k]

LEVEL_FILLERS = [("gv", n) for n in range(8)] + [("iq", c) for c in range(4)]
DSA_FILLERS = [("ms", n) for n in range(KT)] + [("yg", n) for n in range(KT)]
DSA_JOBS = [(h, t) for h in range(SH) for t in range(TILES)]


class Alloc:

    def __init__(self, nc):
        self.nc, self.stack = nc, ExitStack()

    def sb(self, name, shape, dt=F32):
        return self.stack.enter_context(self.nc.sbuf_tensor(name, [P, *shape], dt))

    def bank(self, name):
        return self.stack.enter_context(self.nc.psum_tensor(name, [P, 512], F32))

    def sem(self, name):
        return self.stack.enter_context(self.nc.semaphore(name))

    def close(self):
        self.stack.close()


def hybrid_blocks_kernel(nc, weights, tokens, embeds, small_in, small2_in, rpb, consts_in, consts2_in, levels_in,
                         out):
    al = Alloc(nc)
    sb, sem = al.sb, al.sem

    raw = sb("raw", [RAW, UB * P])
    w_hi = sb("w_hi", [CUT, UB * P], F32R)
    w_lo = sb("w_lo", [CUT, UB * P], F32R)
    h = sb("h", [KT, TOK])
    x_hi = sb("x_hi", [KT, TOK], F32R)
    x_lo = sb("x_lo", [KT, TOK], F32R)
    y_hi = sb("y_hi", [KT, TOK], F32R)
    y_lo = sb("y_lo", [KT, TOK], F32R)
    wide = sb("wide", [KT, TOK])
    scale = sb("scale", [TOK])
    root = sb("root", [2, TOK])
    rstd = sb("rstd", [2, TOK])
    consts = sb("consts", [CONST_W])
    small = sb("small", [SMALL_W])
    q_gain = sb("q_gain", [DEPTH])
    mean_dm = sb("mean_dm", [P])
    eps = sb("eps", [1])
    th = sb("th", [2, TOK])
    prod = sb("prod", [2, TOK])
    prod2 = sb("prod2", [2, TOK])
    probs = sb("probs", [2, TOK])
    turned = sb("turned", [2, 3 * P])
    top = sb("top", [2, 8])
    total = sb("total", [2, 8])
    share = sb("share", [2, 8])
    best = sb("best", [8])
    warm = sb("warm", [1])

    def const(name, rows=P):
        at, w = (CONST.get(name) or CONST2[name])
        return (consts if name in CONST else consts2)[0:rows, at:at + w]

    def operand(name, rows=P):
        at, w = (SMALL.get(name) or SMALL2[name])
        return (small if name in SMALL else small2)[0:rows, at:at + w]

    line_bank = [al.bank(f"line{i}") for i in range(2)]
    stat_bank = al.bank("stat")
    score_bank = [al.bank(f"score{i}") for i in range(2)]
    turn_bank = al.bank("turn")
    result_bank = [al.bank(f"result{i}") for i in range(2)]
    product_bank = line_bank + result_bank

    raw_in = [sem(f"raw_in{i}") for i in range(RAW)]
    first_in = sem("first_in")
    hi_cut, lo_cut = sem("hi_cut"), sem("lo_cut")
    small_loaded, index_k_ready = sem("small_loaded"), sem("index_k_ready")
    tokens_in = [sem(f"tokens_in{i}") for i in range(2)]
    loaded, loaded2 = sem("loaded"), sem("loaded2")
    embeds_in = sem("embeds_in")
    rel_in = [sem(f"rel_in{i}") for i in range(2)]
    rel_ready = sem("rel_ready")
    set_up = sem("set_up")
    gains_ready = sem("gains_ready")
    line_done = sem("line_done")
    squares_ready, stat_done, root_ready = sem("squares_ready"), sem("stat_done"), sem("root_ready")
    log_ready = sem("log_ready")
    stat_read, summed, mean_ready = sem("stat_read"), sem("summed"), sem("mean_ready")
    full_ready, x_hi_ready, x_ready, h_ready = sem("full_ready"), sem("x_hi_ready"), sem("x_ready"), sem("h_ready")
    raw_head, normed, rot_done, roped = sem("raw_head"), sem("normed"), sem("rot_done"), sem("roped")
    kq_ready, v_raw, v_turned, v_ready = sem("kq_ready"), sem("v_raw"), sem("v_turned"), sem("v_ready")
    score_done = sem("score_done")
    maxed, exped, probs_ready = sem("maxed"), sem("exped"), sem("probs_ready")
    turn_done, turned_most, turned_rest = sem("turn_done"), sem("turned_most"), sem("turned_rest")
    valued, even_scores = sem("valued"), sem("even_scores")
    rot_used, pair_gated, y_used = sem("rot_used"), sem("pair_gated"), sem("y_used")
    act_raw, act_up, act_half, down_used = sem("act_raw"), sem("act_up"), sem("act_half"), sem("down_used")
    gate_raw, tanh_ready, gates_ready = sem("gate_raw"), sem("tanh_ready"), sem("gates_ready")
    gated, y_hi_ready, y_ready = sem("gated"), sem("y_hi_ready"), sem("y_ready")
    act_full, act_hi_ready, act_ready = sem("act_full"), sem("act_hi_ready"), sem("act_ready")
    dve_step = sem("dve_step")
    act_tanh, out_ready = sem("act_tanh"), sem("out_ready")
    low_ready, index_w_ready, index_q_ready = sem("low_ready"), sem("index_w_ready"), sem("index_q_ready")
    row_done = sem("row_done")
    row_ready, row_stored = sem("row_ready"), sem("row_stored")
    rbias_in = [sem(f"rbias_in{i}") for i in range(2)]
    ckv_raw, ckv_ready = sem("ckv_raw"), sem("ckv_ready")
    alpha_used, soft_in, soft_out = sem("alpha_used"), sem("soft_in"), sem("soft_out")
    soft_step = sem("soft_step")
    gla_in, gv_raw, gv_turned, gv_ready = sem("gla_in"), sem("gv_raw"), sem("gv_turned"), sem("gv_ready")
    fallen, risen, gr_raw, index_w_turned = sem("fallen"), sem("risen"), sem("gr_raw"), sem("index_w_turned")
    grown_ready, level_ready, level_used = sem("grown_ready"), sem("level_ready"), sem("level_used")
    kdt_ready, state_ready, gla_done, gla_raw = sem("kdt_ready"), sem("state_ready"), sem("gla_done"), sem("gla_raw")
    gla_full, gg_hi_ready, gg_ready = sem("gla_full"), sem("gg_hi_ready"), sem("gg_ready")
    dq_ready, relued, scored = sem("dq_ready"), sem("relued"), sem("scored")
    od_hi_ready, od_ready = sem("od_hi_ready"), sem("od_ready")
    p_hi_ready, p_ready, pp_ready = sem("p_hi_ready"), sem("p_ready"), sem("pp_ready")
    pg_raw, pg_used = sem("pg_raw"), sem("pg_used")
    means_ready = sem("means_ready")
    gate_ready = sem("gate_ready")
    stored = sem("stored")
    first, second = (x_hi, x_lo), (y_hi, y_lo)
    x_of = dict(layer0=first, mixed0=first, layer1=second, mixed1=second, ffn0=first, mixer=first, mixed2=first,
                ffn1=second, embed=first)
    y_of = dict(layer0=second, layer1=first)
    names = ("layer0", "layer1", "final0", "mixer", "ffn1", "embed", "final1")
    square_of = {n: th if n != "final1" else probs for n in names}
    sum_of = {n: (prod2[:, 0], prod2[:, 1]) for n in names} | {"final1": (root[:, 1 - STAT[("final1", "norm")] % 2],)}
    signals = dict(squares_ready=squares_ready, raw_head=raw_head, v_raw=v_raw, kq_ready=kq_ready, gate_raw=gate_raw,
                   y_used=y_used, h_ready=h_ready, act_raw=act_raw, act_up=act_up, down_used=down_used, exped=exped,
                   maxed=maxed, rot_used=rot_used, pair_gated=pair_gated, gated=gated, low_ready=low_ready,
                   ckv_raw=ckv_raw, row_ready=row_ready, index_w_ready=index_w_ready, alpha_used=alpha_used,
                   kdt_ready=kdt_ready, level_used=level_used, gv_raw=gv_raw, gr_raw=gr_raw, relued=relued,
                   gla_in=gla_in, index_q_ready=index_q_ready, state_ready=state_ready, dq_ready=dq_ready,
                   od_ready=od_ready, pp_ready=pp_ready, pg_raw=pg_raw)
    row_dram = nc.dram_tensor("bias_by_distance", (SH, 2 * SEQ), F32).ap()

    a1 = Alloc(nc)
    gate = {n: a1.sb(f"gate_{n}", [KT, TOK]) for n in "ab"}
    silu = {n: a1.sb(f"silu_{n}", [PAIRS, TOK]) for n in "ab"}
    qa = a1.sb("qa", [PAIRS, TOK])
    ka = a1.sb("ka", [TOK])
    q_meta = a1.sb("q_meta", [PAIRS * META])
    qb = a1.sb("qb", [PAIRS, TOK])
    kb = a1.sb("kb", [PAIRS, TOK])
    va = a1.sb("va", [3, P])
    vb = a1.sb("vb", [3, HEADS * HD])
    rel = a1.sb("rel", [2, TILES, 2, SEQ])
    a1.close()
    a2 = Alloc(nc)
    consts2 = a2.sb("consts2", [CONST2_W])
    small2 = a2.sb("small2", [SMALL2_W])
    gla_gain = a2.sb("gla_gain", [KT])
    mean_gdv = a2.sb("mean_gdv", [P])
    mean_p = a2.sb("mean_p", [P])
    levels = a2.sb("levels", [len(HALVES) + 1, P], U32)
    p_in = turned[:, :, 0:SEQ]
    p_hi = a2.sb("p_hi", [2, SEQ], F32R)
    p_lo = a2.sb("p_lo", [2, SEQ], F32R)
    pp = wide[:, :, 0:SEQ]
    a3 = Alloc(nc)
    act_hi = a3.sb("act_hi", [FT, SEQ], F32R)
    act_lo = a3.sb("act_lo", [FT, SEQ], F32R)
    a3.close()
    a3 = Alloc(nc)
    gg_hi, gg_lo = y_hi[:, :, 0:SEQ], y_lo[:, :, 0:SEQ]
    low = turned[:, 0, 0:SEQ]
    index_k = a3.sb("index_k", [SEQ])
    index_q = a3.sb("index_q", [PAIRS, SEQ])
    index_w = a3.sb("index_w", [TILES, SH])
    ckv = a3.sb("ckv", [SEQ])
    ckv_t = a3.sb("ckv_t", [TILES, P])
    a4 = Alloc(nc)
    gk_decay = a4.sb("gk_decay", [2, GH * SEQ])
    gk, decay = gk_decay[:, 0], gk_decay[:, 1]
    gr = gk_decay[:, :, :].rearrange("p a (k t) -> p (a k) t", t=SEQ)
    gq, grown = wide[:, 0:GH, 0:SEQ], wide[:, GH:2 * GH, 0:SEQ]
    fall = a4.sb("fall", [GH * SEQ])
    gate_q = a4.sb("gate_q", [GH * SEQ])
    gate_k = a4.sb("gate_k", [GH * SEQ])
    pairs = a4.sb("pairs", [TILES, GH, P])
    gv = a4.sb("gv", [TILES, GH * GDV])
    states = a4.sb("states", [3, GDV])
    a4.close()
    a4 = Alloc(nc)
    dq = wide[:, :, 0:SEQ]
    mgate = {n: a4.sb(f"mgate_{n}", [KT, SEQ]) for n in "gs"}
    od_hi = a4.sb("od_hi", [SH, SEQ], F32R)
    od_lo = a4.sb("od_lo", [SH, SEQ], F32R)
    rbias = a4.sb("rbias", [2, SEQ + P])
    score = root[:, :, 0:SEQ]
    work = prod2[:, :, 0:SEQ]
    a4.close()
    bias_row = turned[0:SH].rearrange("p a b -> p (a b)")[:, SEQ:3 * SEQ]
    a3.close()
    a2.close()

    block = al.stack.enter_context(nc.Block())

    @block.sync
    def _(sp):
        def load_unit(u):
            if u >= RAW:
                sp.wait_ge(lo_cut, cuts(u - RAW))
            n = BLOCKS[u] * P
            sp.dma_start(raw[:, u % RAW, 0:n], weights[u, :, 0:n]).then_inc(raw_in[u % RAW], 16)

        def load_rel(i, c):
            n = PAIRS * i + c
            if n >= 2:
                sp.wait_ge(score_done, SCORE[(f"layer{(n - 2) // PAIRS}", "B", (n - 2) % PAIRS, 1, TILES - 1)] + 1)
            for half in range(2):
                for r in range(ROWS):
                    at = ((i * HEADS + 2 * c + half) * RPB_R + 7 - r) * RPB_C + WIN - GRID_W
                    src = bass.AP(rpb.tensor, at, [[1, GRID_W], [RPB_C, ROWS], [1, GRID_W]])
                    dst = rel[(1 - r % 2) * GRID_W:(2 - r % 2) * GRID_W, n % 2, r // 2, half]
                    sp.dma_start(dst.rearrange("p (r c) -> p r c", c=GRID_W), src).then_inc(rel_in[n % 2], 16)

        def load_rbias(hd):
            if hd >= 2:
                sp.wait_ge(score_done, SCORE[("mixer", "dsa", hd - 2, TILES - 1)] + 1)
            for t in range(TILES):
                at = hd * 2 * SEQ + SEQ - (t + 1) * P
                src = bass.AP(row_dram.tensor, at, [[1, P], [1, (t + 1) * P]])
                sp.dma_start(rbias[:, hd % 2, t * P:t * P + (t + 1) * P], src).then_inc(rbias_in[hd % 2], 16)

        sp.dma_start(small[:, :], small_in).then_inc(small_loaded, 16)
        sp.dma_start(raw[:, 0, 0:KT * P], weights[0, :, 0:KT * P]).then_inc(first_in, 16)
        for half in range(2):
            k = slice(half * KT // 2, (half + 1) * KT // 2)
            sp.dma_start(h[:, k], tokens[:, k]).then_inc(tokens_in[half], 16)
        sp.dma_start(raw[:, 0, KT * P:UB * P], weights[0, :, KT * P:UB * P]).then_inc(raw_in[0], 16)
        for u in range(1, NU):
            load_unit(u)
            if u == 1:
                sp.dma_start(consts[:, :], consts_in).then_inc(loaded, 16)
            for i in range(DEPTH):
                for c, behind in enumerate((5, 6, 22, 24)):
                    if u == STAGES[f"layer{i}"] + behind:
                        load_rel(i, c)
            if u == STAGES["ffn0"] + 4:
                sp.wait_ge(h_ready, H_BATCH["layer1"] + KT)
                sp.dma_start(consts2[:, :], consts2_in).then_inc(loaded2, 16)
                sp.dma_start(small2[:, :], small2_in).then_inc(loaded2, 16)
                sp.dma_start(levels[:, :, :], levels_in).then_inc(loaded2, 16)
            if u == STAGES["ffn1"] + 1:
                sp.wait_ge(valued, JOB[DEPTH] + len(DSA_JOBS))
                sp.dma_start(p_in, embeds).then_inc(embeds_in, 16)
            if u == UNIT[("mixer", "gv", 7)]:
                sp.wait_ge(row_ready, 1)
                sp.dma_start(row_dram, bias_row).then_inc(row_stored, 16)
            if u == UNIT[("mixer", "mg", 2)]:
                sp.wait_ge(row_stored, 16)
                sp.wait_ge(gg_ready, KT)
                load_rbias(0)
                load_rbias(1)
            if 2 <= u - UNIT[("mixer", "ms", 0)] - 1 < SH:
                load_rbias(u - UNIT[("mixer", "ms", 0)] - 1)

        for k in range(0, KT, 2):
            sp.wait_ge(out_ready, k + 2)
            sp.dma_start(out[:, k:k + 2], wide[:, k:k + 2, 0:SEQ]).then_inc(stored, 16)
        sp.wait_ge(stored, 16 * KT // 2)

    @block.gpsimd
    def _(pool):
        pool.memset(mean_dm[:, :], 1.0 / DM).then_inc(set_up, 1)
        pool.memset(eps[:, :], EPS).then_inc(set_up, 1)
        for u in range(NU):
            n = BLOCKS[u] * P
            if u == STAGES["ffn0"] + CUT:
                pool.wait_ge(h_ready, H_BATCH["layer1"] + KT)
                pool.memset(mean_gdv[:, :], 1.0 / GDV).then_inc(means_ready, 1)
                pool.memset(mean_p[:, :], 1.0 / P).then_inc(means_ready, 1)
            first = 0
            if u == 0:
                first = KT * P
                pool.wait_ge(hi_cut, 1)
                pool.tensor_tensor(w_lo[:, 0, 0:first], raw[:, 0, 0:first], w_hi[:, 0, 0:first].bitcast(F32),
                                   ALU.subtract).then_inc(lo_cut, 1)
            pool.wait_ge(hi_cut, cuts(u))
            pool.tensor_tensor(w_lo[:, u % CUT, first:n], raw[:, u % RAW, first:n],
                               w_hi[:, u % CUT, first:n].bitcast(F32), ALU.subtract).then_inc(lo_cut, 1)

    @block.scalar
    def _(act):
        cut = [0]

        def cut_to(u):
            while cut[0] <= min(u, NU - 1):
                v = cut[0]
                n = BLOCKS[v] * P
                act.wait_ge(raw_in[v % RAW], 16 * (v // RAW + 1))
                if v >= CUT:
                    act.wait_ge(line_done, last_line(v - CUT) + 1)
                first = 0 if v else KT * P
                act.activation(w_hi[:, v % CUT, first:n], raw[:, v % RAW, first:n], ACT.Copy).then_inc(hi_cut, 1)
                cut[0] += 1

        def line_wait(key):
            cut_to(UNIT[key] + CUT - 1)
            act.wait_ge(line_done, LINE[key] + 1)
            return product_bank[LINE_BANK[LINE[key]]]

        def load_log_table(first):
            if first:
                act.wait_ge(set_up, 2)
            act.activation(warm[:, :], eps[:, :], ACT.Ln)

        def square(name, k, at, n):
            if at >= 2:
                act.wait_ge(summed, SUMMED[name] + at - 1)
            src = h if name != "final0" or at % 2 == 0 else wide
            act.activation(square_of[name][:, at % 2, 0:n], src[:, k, 0:n], ACT.Square).then_inc(squares_ready, 1)

        def round_h(name, n, before=None):
            x = x_of[name][0]
            load_log_table(name == "layer0")
            for k in range(KT):
                if before:
                    cut_to(UNIT[before(k)] + CUT - 1)
                if name == "layer0":
                    if k == 0:
                        act.wait_ge(first_in, 16)
                        act.activation(w_hi[:, 0, 0:KT * P], raw[:, 0, 0:KT * P], ACT.Copy).then_inc(hi_cut, 1)
                        act.wait_ge(gains_ready, 1)
                    act.wait_ge(tokens_in[k // (KT // 2)], 16)
                else:
                    act.wait_ge(h_ready, H_BATCH[READS[name]] + k + 1)
                act.activation(x[:, k, 0:n], h[:, k, 0:n], ACT.Copy,
                               scale=operand(f"g_{name}")[:, k:k + 1]).then_inc(x_hi_ready, 1)
                if name != "layer0":
                    square(name, k, k, n)
            if name == "layer0":
                cut_to(1)
                for k in range(KT):
                    square(name, k, k, n)

        def root_of(key, n, mean=None):
            s = STAT[key] % 2
            log, r = root[:, s, 0:n], rstd[:, s, 0:n]
            if mean is None:
                act.wait_ge(stat_done, STAT[key] + 1)
                act.activation(log, stat_bank[:, 0:n], ACT.Ln, bias=eps[:, :]).then_inc(log_ready, 1)
            else:
                act.activation(log, mean, ACT.Ln).then_inc(log_ready, 1)
            act.wait_ge(log_ready, STAT[key] + 1)
            act.activation(r, log, ACT.Exp, scale=-0.5).then_inc(root_ready, 1)

        def round_full(batch, k, n, x, gain=1.0):
            act.wait_ge(full_ready, FULL_BATCH[batch] + k + 1)
            act.activation(x[:, k, 0:n], wide[:, k, 0:n], ACT.Copy, scale=gain).then_inc(x_hi_ready, 1)

        def layer(i):
            name, W = f"layer{i}", WIDTH[i]
            round_h(name, TOK, (lambda k: (f"layer{i - 1}", "out", k)) if i else None)
            cut_to(STAGES[name] + CUT - 1)
            root_of((name, "norm"), TOK)

            def head_square(n):
                cut_to(UNIT[(name, "qa", n - 1) if n else (name, "ka")] + CUT - 1)
                act.wait_ge(raw_head, 5 * i + n + 1)
                if n >= 2:
                    act.wait_ge(stat_done, STAT[(name, "head", n - 2)] + 1)
                src = ka[:, :] if n == 0 else qa[:, n - 1]
                w = W if n else TOK
                act.activation(th[:, n % 2, 0:w], src[:, 0:w], ACT.Square).then_inc(squares_ready, 1)

            def v_by_token(n):
                v = va[:, :, 0:P] if n == 0 else vb[:, :, (n - 1) * P:n * P]
                act.wait_ge(v_turned, 5 * i + n + 1)
                act.activation(v[:, 0:TILES], turn_bank[:, 0:TILES * P].rearrange("p (t c) -> p t c", c=P),
                               ACT.Copy).then_inc(v_ready, 1)
                act.activation(v[0:META, TILES], turn_bank[0:META, TILES * P:(TILES + 1) * P],
                               ACT.Copy).then_inc(v_ready, 1)

            head_square(0)
            for at, key in enumerate(HEAD_LINES):
                cut_to(UNIT[(name, *key)] + CUT - 1)
                n = at // 2
                if at == 0:
                    head_square(1)
                elif at % 2 and n <= PAIRS:
                    root_of((name, "head", n), W if n else TOK)
                    if n + 2 <= PAIRS:
                        head_square(n + 2)
                if at == 1:
                    v_by_token(0)
                if key[0] == "vb" and key[1]:
                    v_by_token(key[1])
            v_by_token(PAIRS)

            def exps(job, n):
                s = SCORE[(name, *job)]
                act.wait_ge(maxed, n + 1)
                if n >= 2:
                    act.wait_ge(turn_done, TURN_OF_JOB[n - 2] + 1)
                if job[0] == "Bm":
                    at = probs[0:META, n % 2, 0:HEADS * META]
                    act.activation(at, at, ACT.Exp).then_inc(exped, 1)
                    return
                m = PAIRS * META if job[0] == "Am" else P
                act.activation(probs[0:m, n % 2, :], score_bank[s % 2][0:m, 0:TOK], ACT.Exp,
                               bias=top[0:m, n % 2, 0:1], accum_out=total[0:m, n % 2, 0:1]).then_inc(exped, 1)

            def turned_of(job, n):
                act.wait_ge(turn_done, TURN[(name, *job)] + 1)
                if n >= 2:
                    act.wait_ge(valued, n - 1)
                if job[0] == "Bm":
                    out_, in_ = turned[0:META, n % 2, 0:HD], turn_bank[0:META, 0:HD]
                else:
                    m = PAIRS * META if job[0] == "Am" else P
                    out_ = turned[:, n % 2, 0:2 * P].rearrange("p (b q) -> p b q", q=P)[:, :, 0:m]
                    in_ = turn_bank[:, 0:2 * P].rearrange("p (b q) -> p b q", q=P)[:, :, 0:m]
                act.activation(out_, in_, ACT.Copy).then_inc(turned_most, 1)

            def filler(m):
                kind, c = FILLERS[m]
                cut_to(UNIT[(name, kind, c)] + CUT - 1)
                if kind == "ya":
                    return
                act.wait_ge(gate_raw, GATES * i + m + 1)
                if kind in ("za", "zb"):
                    n = 8 * i + m
                    if n >= 2:
                        act.wait_ge(gates_ready, n - 1)
                    act.activation(th[:, m % 2, 0:W], silu[kind[1]][:, c, 0:W], ACT.Tanh,
                                   scale=0.5).then_inc(tanh_ready, 1)
                else:
                    g = gate[kind[1]][:, c, 0:W]
                    act.activation(g, g, ACT.Tanh, scale=0.5).then_inc(gate_ready, 1)

            def round_y(job):
                n = tile_done(i, job)
                if n is not None:
                    if n == 0:
                        if i < DEPTH - 1:
                            act.wait_ge(gated, 2 * i + 1)
                    act.wait_ge(pair_gated, KT * i + n + 1)
                    act.activation(y_of[name][0][:, n, 0:W], wide[:, n, 0:W], ACT.Copy).then_inc(y_hi_ready, 1)

            J, jobs = len(JOBS[i]), JOBS[i]
            for t in range(J + 2):
                if t < J:
                    exps(jobs[t], JOB[i] + t)
                if t < len(FILLERS):
                    filler(t)
                if 1 <= t <= J:
                    turned_of(jobs[t - 1], JOB[i] + t - 1)
                if t >= 2:
                    round_y(jobs[t - 2])
            for m in range(KT):
                cut_to(UNIT[(name, "yb", m)] + CUT - 1)
                round_full(f"mixed{i}", m, W, x_of[f"mixed{i}"][0])

        for i in range(DEPTH):
            layer(i)
        load_log_table(False)
        for k in range(KT):
            cut_to(UNIT[(f"layer{DEPTH - 1}", "out", k)] + CUT - 1)
            act.wait_ge(h_ready, H_BATCH["layer1"] + k + 1)
            square("final0", k, 2 * k, SEQ)
            round_full("final0", k, SEQ, x_of["ffn0"][0], operand("g_ffn0")[:, k:k + 1])
            square("final0", k, 2 * k + 1, SEQ)
        cut_to(STAGES["ffn0"] + CUT - 1)
        act.wait_ge(mean_ready, 1)
        root_of(("ffn0", "norm"), SEQ, prod[:, 0, 0:SEQ])
        root_of(("final0", "norm"), SEQ)

        def ffn(f):
            name = f"ffn{f}"

            def round_act(j):
                act.wait_ge(act_full, FT * f + j + 1)
                act.activation(act_hi[:, j], prod2[:, j % 2, 0:SEQ], ACT.Copy).then_inc(act_hi_ready, 1)

            for j in range(FT):
                cut_to(UNIT[(name, "gate", j)] + CUT - 1)
                n = FT * f + j
                act.wait_ge(act_raw, n + 1)
                if j >= 2:
                    act.wait_ge(act_half, n - 1)
                act.activation(th[:, j % 2, 0:SEQ], prod[:, j % 2, 0:SEQ], ACT.Tanh, scale=0.5).then_inc(act_tanh, 1)
                if j:
                    round_act(j - 1)
            round_act(FT - 1)

        ffn(0)

        round_h("mixer", SEQ, lambda k: ("ffn0", "down", k, 1))
        cut_to(STAGES["mixer"] + CUT - 1)
        root_of(("mixer", "norm"), SEQ)
        act.wait_ge(low_ready, 1)
        for rows in (slice(HD, P), slice(0, HD)):
            act.activation(index_k[rows], low[HD:P], ACT.Copy).then_inc(index_k_ready, 1)
        act.wait_ge(ckv_raw, 1)
        act.activation(th[:, 0, 0:SEQ], ckv[:, :], ACT.Square).then_inc(squares_ready, 1)

        act.wait_ge(row_done, 1)
        act.activation(bias_row, result_bank[RESULT[("mixer", "rel")] % 2][0:SH, :], ACT.Copy).then_inc(row_ready, 1)
        cut_to(UNIT[("mixer", "gk", 0)] + CUT - 1)
        root_of(("mixer", "ckv"), SEQ)
        cut_to(UNIT[("mixer", "gk", 2)] + CUT - 1)
        act.wait_ge(soft_in, 1)
        act.activation(gate_k[:, :], gate_k[:, :], ACT.Exp).then_inc(soft_step, 1)
        act.wait_ge(soft_step, 1)
        act.activation(gate_k[:, :], gate_k[:, :], ACT.Ln, bias=1.0).then_inc(soft_out, 1)
        cut_to(UNIT[("mixer", "gq", 2)] + CUT - 1)
        act.wait_ge(turn_done, TURN[("mixer", "ckv")] + 1)
        act.activation(ckv_t[:, :, :], turn_bank[:, 0:TILES * P].rearrange("p (t c) -> p t c", c=P),
                       ACT.Copy).then_inc(turned_most, 1)

        def rise(n):
            act.wait_ge(fallen, n + 1)
            act.activation(fall[:, :], fall[:, :], ACT.Exp).then_inc(risen, 1)

        rise(0)
        act.activation(grown, decay.rearrange("p (g t) -> p g t", t=SEQ), ACT.Exp).then_inc(grown_ready, 1)
        for n in range(len(HALVES)):
            rise(n + 1)
            for f in LEVEL_FILLERS[2 * n:2 * n + 2]:
                cut_to(UNIT[("mixer", *f)] + CUT - 1)
                if f[0] == "gv":
                    act.wait_ge(gv_turned, f[1] + 1)
                    act.activation(gv[:, :, f[1] * P:(f[1] + 1) * P],
                                   turn_bank[:, 0:TILES * P].rearrange("p (t c) -> p t c", c=P),
                                   ACT.Copy).then_inc(gv_ready, 1)
        cut_to(UNIT[("mixer", "gr", 0)] + CUT - 2)
        for t in range(TILES):
            s = SCORE[("mixer", "kdt", t)]
            act.wait_ge(score_done, s + 1)
            act.activation(fall[:, t * GH * P:(t + 1) * GH * P], score_bank[s % 2][:, :],
                           ACT.Copy).then_inc(kdt_ready, 1)

        def tanh_gr(m):
            cut_to(UNIT[("mixer", "gr", m)] + CUT - 1)
            act.wait_ge(gr_raw, m + 1)
            if m >= 2:
                act.wait_ge(gates_ready, 8 * DEPTH + m - 1)
            act.activation(probs[:, m % 2, 0:SEQ], gr[:, m], ACT.Tanh, scale=0.5).then_inc(tanh_ready, 1)

        def round_gg(m):
            act.wait_ge(gla_full, m + 1)
            act.activation(gg_hi[:, m], prod2[:, m % 2, 0:SEQ], ACT.Copy).then_inc(gg_hi_ready, 1)

        def head_out(g):
            if g:
                act.wait_ge(stat_done, STAT[("mixer", "gla", g - 1)] + 1)
                act.wait_ge(gla_full, 2 * g)
            for e in range(2):
                bank = result_bank[RESULT[("mixer", "gla", g, e)] % 2]
                act.wait_ge(gla_done, 2 * g + e + 1)
                act.activation(prod[:, e, 0:SEQ], bank[:, 0:SEQ], ACT.Copy).then_inc(gla_raw, 1)
                act.activation(th[:, e, 0:SEQ], bank[:, 0:SEQ], ACT.Square).then_inc(squares_ready, 1)

        for g in range(GH + 1):
            if g < GH:
                tanh_gr(2 * g)
                tanh_gr(2 * g + 1)
            if g == GH:
                cut_to(UNIT[("mixer", "dq", 0)] + CUT - 1)
            if g:
                root_of(("mixer", "gla", g - 1), SEQ)
                round_gg(2 * g - 2)
                round_gg(2 * g - 1)
            if g < GH:
                head_out(g)
            cut_to(UNIT[("mixer", "gr", min(2 * g + 2, 2 * GH - 1))] + CUT - 1)

        def tanh_gate(name, m):
            cut_to(UNIT[("mixer", name, m)] + CUT - 1)
            act.wait_ge(gate_raw, GATES * DEPTH + KT * (name == "ms") + m + 1)
            g = mgate[name[1]][:, m]
            act.activation(g, g, ACT.Tanh, scale=0.5).then_inc(gate_ready, 1)

        tanh_gate("mg", 0)
        tanh_gate("mg", 1)
        for n, (t, hd) in enumerate((t, hd) for t in range(TILES) for hd in range(SH)):
            s = SCORE[("mixer", "dots", t, hd)]
            keys = (t + 1) * P
            act.wait_ge(score_done, s + 1)
            if n >= 2:
                act.wait_ge(scored, n - 1)
            act.activation(th[:, n % 2, 0:keys], score_bank[s % 2][:, 0:keys], ACT.Relu).then_inc(relued, 1)
            if n % 2:
                cut_to(UNIT[("mixer", "dq", min(n // 2 + 2, SH - 1))] + CUT - 1)

        for m in range(2, KT):
            tanh_gate("mg", m)

        def dsa_exps(i):
            hd, t = DSA_JOBS[i]
            n, s, keys = JOB[DEPTH] + i, SCORE[("mixer", "dsa", hd, t)], (t + 1) * P
            act.wait_ge(maxed, n + 1)
            act.wait_ge(turn_done, TURN_OF_JOB[n - 2] + 1)
            act.activation(probs[:, n % 2, 0:keys], score_bank[s % 2][:, 0:keys], ACT.Exp, bias=top[:, n % 2, 0:1],
                           accum_out=total[:, n % 2, 0:1]).then_inc(exped, 1)

        def dsa_turned(i):
            hd, t = DSA_JOBS[i]
            n, keys = JOB[DEPTH] + i, (t + 1) * P
            act.wait_ge(turn_done, TURN[("mixer", "dsa", hd, t)] + 1)
            act.wait_ge(valued, n - 1)
            act.activation(turned[:, n % 2, 0:keys], turn_bank[:, 0:keys], ACT.Copy).then_inc(turned_most, 1)

        def round_od(i):
            hd, t = DSA_JOBS[i]
            if t == TILES - 1:
                act.wait_ge(valued, JOB[DEPTH] + i + 1)
                act.activation(od_hi[:, hd], result_bank[RESULT[("mixer", "dsa", hd)] % 2][:, 0:SEQ],
                               ACT.Copy).then_inc(od_hi_ready, 1)

        for i in range(len(DSA_JOBS) + 2):
            if i < len(DSA_JOBS):
                dsa_exps(i)
                name, m = DSA_FILLERS[i]
                if name == "ms":
                    tanh_gate(name, m)
                else:
                    cut_to(UNIT[("mixer", name, m)] + CUT - 1)
            if 1 <= i <= len(DSA_JOBS):
                dsa_turned(i - 1)
            if i >= 2:
                round_od(i - 2)
        for m in range(KT):
            cut_to(UNIT[("mixer", "ys", m)] + CUT - 1)
            round_full("mixed2", m, SEQ, x_of["mixed2"][0])
        round_h("ffn1", SEQ, lambda k: ("mixer", "mix", k))
        cut_to(STAGES["ffn1"] + CUT - 1)
        root_of(("ffn1", "norm"), SEQ)
        act.wait_ge(embeds_in, 16)
        act.activation(p_hi[:, :, :], p_in, ACT.Copy).then_inc(p_hi_ready, 1)
        ffn(1)

        round_h("embed", SEQ, lambda k: ("ffn1", "down", k, 1))
        for m in range(KT):
            bank = line_wait(("embed", "pp", m))
            act.activation(pp[:, m], bank[:, 0:SEQ], ACT.Copy, scale=0.5).then_inc(pp_ready, 1)
        cut_to(STAGES["embed"] + CUT)
        root_of(("embed", "norm"), SEQ)

        def square_of_result(k):
            act.wait_ge(h_ready, H_BATCH["embed"] + k + 1)
            square("final1", k, k, SEQ)

        for m in range(KT):
            cut_to(UNIT[("embed", "pg", m)] + CUT - 1)
            act.wait_ge(pg_raw, m + 1)
            if m >= 2:
                act.wait_ge(pg_used, m - 1)
            act.activation(th[:, m % 2, 0:SEQ], prod2[:, m % 2, 0:SEQ], ACT.Tanh, scale=0.5).then_inc(tanh_ready, 1)
            if m:
                square_of_result(m - 1)
        load_log_table(False)
        square_of_result(KT - 1)
        root_of(("final1", "norm"), SEQ)

    @block.vector
    def _(dve):
        steps = [0]

        def link(ins):
            steps[0] += 1
            ins.then_inc(dve_step, 1)
            dve.wait_ge(dve_step, steps[0])

        def line_wait(key):
            dve.wait_ge(line_done, LINE[key] + 1)
            return product_bank[LINE_BANK[LINE[key]]]

        def newton(r, v, mean, out_=None):
            mean(r)
            link(dve.tensor_tensor(v, v, r, ALU.mult))
            link(dve.scalar_tensor_tensor(r if out_ is None else out_, v, -3.0, r, ALU.add, ALU.mult))

        def rstd_of(key, n, out_=None):
            s = STAT[key] % 2
            r, v = rstd[:, s, 0:n], root[:, s, 0:n]
            dve.wait_ge(root_ready, STAT[key] + 1)

            def mean(r):
                dve.scalar_tensor_tensor(v, stat_bank[:, 0:n], EPS, r, ALU.add, ALU.mult).then_inc(stat_read, 1)
                dve.wait_ge(stat_read, STAT[key] + 1)

            newton(r, v, mean, out_)
            return r if out_ is None else out_

        def add_square(name, k, at, n):
            total_ = sum_of[name][at % 2 if name == "final0" else 0][:, 0:n]
            sq = square_of[name][:, at % 2, 0:n]
            dve.wait_ge(squares_ready, SQUARES[(name, "norm")] + at + 1)
            if k == 0:
                ins = dve.tensor_copy(total_, sq)
            else:
                dve.wait_ge(summed, SUMMED[name] + at - (name == "final0"))
                ins = dve.tensor_tensor(total_, total_, sq, ALU.add)
            ins.then_inc(summed, 1)

        def rest_of_h(name, k, n):
            x = x_of[name]
            dve.wait_ge(x_hi_ready, X_BATCH[name] + k + 1)
            dve.scalar_tensor_tensor(x[1][:, k, 0:n], h[:, k, 0:n], operand(f"g_{name}")[:, k:k + 1],
                                     x[0][:, k, 0:n].bitcast(F32), ALU.mult, ALU.subtract).then_inc(x_ready, 1)
            if name != "layer0":
                add_square(name, k, k, n)

        def rest_of_full(batch, k, n):
            x = x_of[batch]
            dve.wait_ge(x_hi_ready, X_BATCH[batch] + k + 1)
            dve.tensor_tensor(x[1][:, k, 0:n], wide[:, k, 0:n], x[0][:, k, 0:n].bitcast(F32),
                              ALU.subtract).then_inc(x_ready, 1)

        def scaled_line(key, dst, factor=None):
            bank = line_wait(key)[:, 0:dst.shape[-1]]
            by = scale[:, 0:dst.shape[-1]]
            if factor is None:
                return dve.tensor_tensor(dst, bank, by, ALU.mult)
            return dve.scalar_tensor_tensor(dst, bank, factor, by, ALU.mult, ALU.mult)

        def layer(i):
            name, W = f"layer{i}", WIDTH[i]
            rstd_of((name, "norm"), TOK, scale[:, :])

            def head_raw(n):
                key, dst = ((name, "qa", n - 1), qa[:, n - 1, 0:W]) if n else ((name, "ka"), ka[:, :])
                scaled_line(key, dst).then_inc(raw_head, 1)

            def v_raw_of(n):
                if n >= 2:
                    dve.wait_ge(v_turned, 5 * i + n - 1)
                scaled_line((name, "vb", n - 1) if n else (name, "va"), prod2[:, n % 2, :]).then_inc(v_raw, 1)

            def head_norm(n):
                dst = ka[:, :] if n == 0 else qa[:, n - 1, 0:W]
                g = operand(f"k_gain{i}") if n == 0 else q_gain[:, i:i + 1]
                r = rstd_of((name, "head", n), W if n else TOK)
                dve.scalar_tensor_tensor(dst, dst, g, r, ALU.mult, ALU.mult).then_inc(normed, 1)

            def rope(n):
                w = W if n else TOK
                dst = ka[:, :] if n == 0 else qa[:, n - 1, 0:w]
                key = (name, "rot", n)
                if n and w < TOK:
                    dve.wait_ge(roped, 9 * i + n)
                dve.wait_ge(normed, 5 * i + n + 1)
                dve.tensor_tensor(prod[:, 0, 0:w], dst, const("cos")[:, 0:w], ALU.mult)
                dve.wait_ge(rot_done, 5 * i + n + 1)
                dve.tensor_tensor(prod[:, 1, 0:w], result_bank[RESULT[key] % 2][:, 0:w], const("sin")[:, 0:w],
                                  ALU.mult).then_inc(rot_used, 1)
                dve.wait_ge(rot_used, 5 * i + n + 1)
                dve.tensor_tensor(dst, prod[:, 0, 0:w], prod[:, 1, 0:w], ALU.add).then_inc(roped, 1)
                if n and w == TOK:
                    dve.wait_ge(roped, 9 * i + 2 * n)
                    dve.tensor_copy(q_meta[:, (n - 1) * META:n * META], dst[:, SEQ:TOK]).then_inc(roped, 1)

            head_raw(0)
            v_raw_of(0)
            for at, (kind, c) in enumerate(HEAD_LINES):
                if kind == "qa":
                    head_raw(c + 1)
                elif kind == "kb":
                    scaled_line((name, kind, c), kb[:, c]).then_inc(kq_ready, 1)
                elif kind == "qb":
                    scaled_line((name, kind, c), qb[:, c, 0:W], HD ** -0.5).then_inc(kq_ready, 1)
                else:
                    v_raw_of(c + 1)
                if at % 2 == 0 and 1 <= at // 2 <= PAIRS + 1:
                    head_norm(at // 2 - 1)
                if at % 2 == 0 and 2 <= at // 2 <= PAIRS + 2:
                    rope(at // 2 - 2)

            def window_bias(c):
                n = PAIRS * i + c
                dve.wait_ge(rel_in[n % 2], 16 * 2 * ROWS * (n // 2 + 1))
                at = rel[:, n % 2].rearrange("p t h (r c) -> p (t h r) c", c=GRID_W)
                w = const("window").unsqueeze(1).to_broadcast([P, TILES * 2 * ROWS, GRID_W])
                dve.tensor_tensor(at, at, w, ALU.add).then_inc(rel_ready, 1)

            def maxes(job, n):
                s = SCORE[(name, *job)]
                bank = score_bank[s % 2]
                for c in range(PAIRS):
                    if n - JOB[i] == JOBS[i].index(("B", c, 0, 0)) - 2:
                        window_bias(c)
                dve.wait_ge(score_done, s + 1)
                if job[0] == "Bm":
                    at = bank[0:META, 0:HEADS * META].rearrange("p (h k) -> p h k", k=META)
                    link(dve.tensor_reduce(top[0:META, n % 2, :], at, AX.X, ALU.max))
                    dve.tensor_tensor(probs[0:META, n % 2, 0:HEADS * META].rearrange("p (h k) -> p h k", k=META), at,
                                      top[0:META, n % 2, :].unsqueeze(2).to_broadcast([META, HEADS, META]),
                                      ALU.subtract).then_inc(maxed, 1)
                    return
                m = PAIRS * META if job[0] == "Am" else P
                dve.tensor_reduce(top[0:m, n % 2, 0:1], bank[0:m, 0:TOK], AX.X, ALU.max, negate=True).then_inc(maxed, 1)

            def shares(job, n):
                dve.wait_ge(exped, n + 1)
                if job[0] == "Bm":
                    at = probs[0:META, n % 2, 0:HEADS * META].rearrange("p (h k) -> p h k", k=META)
                    link(dve.tensor_reduce(total[0:META, n % 2, :], at, AX.X, ALU.add))
                    link(dve.reciprocal(share[0:META, n % 2, :], total[0:META, n % 2, :]))
                    dve.tensor_tensor(at, at, share[0:META, n % 2, :].unsqueeze(2).to_broadcast([META, HEADS, META]),
                                      ALU.mult).then_inc(probs_ready, 1)
                    return
                m = PAIRS * META if job[0] == "Am" else P
                link(dve.reciprocal(share[0:m, n % 2, 0:1], total[0:m, n % 2, 0:1]))
                dve.tensor_scalar(probs[0:m, n % 2, :], probs[0:m, n % 2, :], share[0:m, n % 2, 0:1], None,
                                  ALU.mult).then_inc(probs_ready, 1)

            def turned_of(job, n):
                dve.wait_ge(turned_most, TURN[(name, *job)] + 1)
                if job[0] == "Bm":
                    out_, in_ = turned[0:META, n % 2, HD:P], turn_bank[0:META, HD:P]
                else:
                    m = PAIRS * META if job[0] == "Am" else P
                    out_, in_ = turned[0:META, n % 2, 2 * P:2 * P + m], turn_bank[0:META, 2 * P:2 * P + m]
                dve.tensor_copy(out_, in_).then_inc(turned_rest, 1)

            def filler(m):
                kind, c = FILLERS[m]
                if kind == "ya":
                    dst = gate["a"][:, c, 0:W]
                    dve.wait_ge(gate_ready, 16 * i + c + 1)
                    dve.scalar_tensor_tensor(dst, dst, 1.0, line_wait((name, kind, c))[:, 0:W], ALU.add,
                                             ALU.mult).then_inc(y_used, 1)
                    return
                dst = (silu if kind in ("za", "zb") else gate)[kind[1]][:, c, 0:W]
                scaled_line((name, kind, c), dst).then_inc(gate_raw, 1)

            def silu_of(m):
                kind, c = FILLERS[m]
                if kind in ("za", "zb"):
                    n = 8 * i + m
                    dst = silu[kind[1]][:, c, 0:W]
                    dve.wait_ge(tanh_ready, n + 1)
                    dve.scalar_tensor_tensor(dst, th[:, m % 2, 0:W], 1.0, dst, ALU.add,
                                             ALU.mult).then_inc(gates_ready, 1)

            def result_of(job, n):
                kind = job[0][0]
                part = 0 if kind == "A" else PAIRS
                if job in (("Am", 1), ("Bm",)):
                    key = (name, kind + "m")
                    dve.wait_ge(valued, n + 1)
                    dve.tensor_tensor(wide[:, part:part + PAIRS, SEQ:TOK],
                                      result_bank[RESULT[key] % 2][:, 0:PAIRS * META].rearrange(
                                          "p (c q) -> p c q", q=META),
                                      silu[kind.lower()][:, :, SEQ:TOK], ALU.mult).then_inc(gated, 1)
                elif len(job) == 4 and job[2:] == (1, TILES - 1):
                    key = (name, kind, job[1])
                    dve.wait_ge(valued, n + 1)
                    dve.tensor_tensor(wide[:, part + job[1], 0:SEQ], result_bank[RESULT[key] % 2][:, 0:SEQ],
                                      silu[kind.lower()][:, job[1], 0:SEQ],
                                      ALU.mult).then_inc(pair_gated, 1)

            def rest_of_y(job):
                n, y = tile_done(i, job), y_of[name]
                if n is not None:
                    dve.wait_ge(y_hi_ready, KT * i + n + 1)
                    dve.tensor_tensor(y[1][:, n, 0:W], wide[:, n, 0:W], y[0][:, n, 0:W].bitcast(F32),
                                      ALU.subtract).then_inc(y_ready, 1)

            J, jobs = len(JOBS[i]), JOBS[i]
            for t in range(J + 2):
                if t < J:
                    maxes(jobs[t], JOB[i] + t)
                    shares(jobs[t], JOB[i] + t)
                if t < len(FILLERS):
                    filler(t)
                if 1 <= t <= J:
                    turned_of(jobs[t - 1], JOB[i] + t - 1)
                if 1 <= t <= len(FILLERS):
                    silu_of(t - 1)
                if t >= 2:
                    result_of(jobs[t - 2], JOB[i] + t - 2)
                if t >= 3:
                    rest_of_y(jobs[t - 3])
            rest_of_y(jobs[J - 1])

            for m in range(KT):
                dve.wait_ge(gate_ready, 16 * i + KT + m + 1)
                dve.scalar_tensor_tensor(prod[:, m % 2, 0:W], gate["b"][:, m, 0:W], 1.0,
                                         line_wait((name, "yb", m))[:, 0:W], ALU.add, ALU.mult).then_inc(y_used, 1)
                dve.wait_ge(y_used, 16 * i + KT + m + 1)
                dve.tensor_tensor(wide[:, m, 0:W], prod[:, m % 2, 0:W], gate["a"][:, m, 0:W],
                                  ALU.add).then_inc(full_ready, 1)
                if m:
                    rest_of_full(f"mixed{i}", m - 1, W)
            rest_of_full(f"mixed{i}", KT - 1, W)
            for m in range(KT):
                key = (name, "out", m)
                dve.scalar_tensor_tensor(h[:, m, 0:W], line_wait(key)[:, 0:W], 0.25, h[:, m, 0:W], ALU.mult,
                                         ALU.add).then_inc(h_ready, 1)
                if i == 0:
                    dve.wait_ge(h_ready, H_BATCH[name] + m + 1)
                    rest_of_h("layer1", m, TOK)
                else:
                    dve.wait_ge(h_ready, H_BATCH[name] + m + 1)
                    dve.tensor_scalar(wide[:, m, 0:SEQ], h[:, m, 0:SEQ], operand("g_final0")[:, m:m + 1], None,
                                      ALU.mult).then_inc(full_ready, 1)
                    add_square("final0", m, 2 * m, SEQ)
                    dve.wait_ge(x_hi_ready, X_BATCH["ffn0"] + m + 1)
                    x = x_of["ffn0"]
                    dve.scalar_tensor_tensor(x[1][:, m, 0:SEQ], wide[:, m, 0:SEQ], operand("g_ffn0")[:, m:m + 1],
                                             x[0][:, m, 0:SEQ].bitcast(F32), ALU.mult,
                                             ALU.subtract).then_inc(x_ready, 1)
                    add_square("final0", m, 2 * m + 1, SEQ)

        dve.wait_ge(small_loaded, 16)
        dve.tensor_scalar(small[:, :], small[:, :], -0.5, None, ALU.mult).then_inc(gains_ready, 1)
        dve.wait_ge(gains_ready, 1)
        for i in range(DEPTH):
            link(dve.tensor_scalar(q_gain[:, i:i + 1], operand(f"q_gain{i}"), HD ** -0.5, None, ALU.mult))
        for k in range(KT):
            dve.wait_ge(tokens_in[k // (KT // 2)], 16)
            rest_of_h("layer0", k, TOK)
        for k in range(KT):
            add_square("layer0", k, k, TOK)
        dve.wait_ge(loaded, 16)
        for i in range(DEPTH):
            layer(i)

        key = ("ffn0", "norm")
        m2 = prod[:, 0, 0:SEQ]
        dve.wait_ge(stat_done, STAT[("final0", "norm")] + 1)
        link(dve.tensor_scalar(m2, stat_bank[:, 0:SEQ], EPS, EPS / 4, ALU.add, ALU.mult))
        dve.tensor_tensor(m2, m2, stat_bank[:, SEQ:2 * SEQ], ALU.add).then_inc(mean_ready, 1)
        dve.wait_ge(root_ready, STAT[key] + 1)
        r2, v2 = rstd[:, STAT[key] % 2, 0:SEQ], root[:, STAT[key] % 2, 0:SEQ]

        def mean(r):
            dve.tensor_tensor(v2, m2, r, ALU.mult).then_inc(stat_read, 1)
            dve.wait_ge(stat_read, STAT[key] + 1)

        newton(r2, v2, mean)
        link(dve.tensor_scalar(scale[:, 0:SEQ], r2, -1.0, None, ALU.mult))

        def last_norm():
            rstd_of(("final0", "norm"), SEQ)

        def first_result(k):
            dve.tensor_tensor(h[:, k, 0:SEQ], wide[:, k, 0:SEQ], rstd[:, STAT[("final0", "norm")] % 2, 0:SEQ],
                              ALU.mult).then_inc(h_ready, 1)

        def ffn(f):
            name = f"ffn{f}"

            def finish(j):
                n = FT * f + j
                dve.wait_ge(act_tanh, n + 1)
                dve.scalar_tensor_tensor(prod[:, j % 2, 0:SEQ], th[:, j % 2, 0:SEQ], 1.0, prod[:, j % 2, 0:SEQ],
                                         ALU.add, ALU.mult).then_inc(act_half, 1)
                dve.wait_ge(act_half, n + 1)
                dve.tensor_tensor(prod2[:, j % 2, 0:SEQ], prod[:, j % 2, 0:SEQ], prod2[:, j % 2, 0:SEQ],
                                  ALU.mult).then_inc(act_full, 1)

            def rest_of_act(j):
                dve.wait_ge(act_hi_ready, FT * f + j + 1)
                dve.tensor_tensor(act_lo[:, j], prod2[:, j % 2, 0:SEQ], act_hi[:, j].bitcast(F32),
                                  ALU.subtract).then_inc(act_ready, 1)

            for j in range(FT):
                scaled_line((name, "gate", j), prod[:, j % 2, 0:SEQ]).then_inc(act_raw, 1)
                if j:
                    rest_of_act(j - 1)
                if f == 0 and j == 1:
                    last_norm()
                if f == 0 and 2 <= j < KT + 2:
                    first_result(j - 2)
                scaled_line((name, "up", j), prod2[:, j % 2, 0:SEQ]).then_inc(act_up, 1)
                dve.wait_ge(act_up, FT * f + j + 1)
                finish(j)
            rest_of_act(FT - 1)
            for m in range(KT):
                dve.scalar_tensor_tensor(h[:, m, 0:SEQ], line_wait((name, "down", m, 0))[:, 0:SEQ], 0.25,
                                         h[:, m, 0:SEQ], ALU.mult, ALU.add).then_inc(down_used, 1)
                if m:
                    rest_of_h(("mixer", "embed")[f], m - 1, SEQ)
                dve.wait_ge(down_used, KT * f + m + 1)
                dve.scalar_tensor_tensor(h[:, m, 0:SEQ], line_wait((name, "down", m, 1))[:, 0:SEQ], 0.25,
                                         h[:, m, 0:SEQ], ALU.mult, ALU.add).then_inc(h_ready, 1)
            dve.wait_ge(h_ready, H_BATCH[name] + KT)
            rest_of_h(("mixer", "embed")[f], KT - 1, SEQ)

        ffn(0)

        rstd_of(("mixer", "norm"), SEQ, scale[:, 0:SEQ])
        scaled_line(("mixer", "low"), low).then_inc(low_ready, 1)
        scaled_line(("mixer", "ckv"), ckv[:, :]).then_inc(ckv_raw, 1)
        scaled_line(("mixer", "gk", 0), gk[:, 0:SEQ]).then_inc(gla_in, 1)
        dve.wait_ge(index_w_turned, 1)
        bank = result_bank[RESULT[("mixer", "index_w")] % 2]
        dve.tensor_scalar(index_w[:, :, :], bank[:, 0:TILES * SH].rearrange("p (t h) -> p t h", h=SH),
                          (HD * SH) ** -0.5, None, ALU.mult).then_inc(index_w_ready, 1)
        dve.wait_ge(loaded2, 48)
        link(dve.tensor_scalar(gla_gain[:, :], operand("gla_gain"), -0.25, None, ALU.mult))
        link(dve.tensor_scalar(operand("ckv_gain"), operand("ckv_gain"), -0.5, None, ALU.mult))
        dve.memset(pairs[:, :, :, :], 0.0)
        for g in range(GH):
            s = SCORE[("mixer", "alpha", g // 2)]
            dve.wait_ge(score_done, s + 1)
            dve.tensor_scalar(gate_q[:, g * SEQ:(g + 1) * SEQ], score_bank[s % 2][:, g % 2 * SEQ:(g % 2 + 1) * SEQ],
                              operand("alpha_b")[:, g:g + 1], None, ALU.add).then_inc(alpha_used, 1)
        scaled_line(("mixer", "gk", 1), gk[:, SEQ:2 * SEQ]).then_inc(gla_in, 1)
        dve.wait_ge(alpha_used, GH)
        dve.scalar_tensor_tensor(gate_k[:, :], gate_q[:, :], -1.0, gate_q[:, :], ALU.mult, ALU.min).then_inc(soft_in, 1)
        link(dve.tensor_scalar(gate_q[:, :], gate_q[:, :], 0.0, 1.0 / TAU, ALU.min, ALU.mult))
        r = rstd_of(("mixer", "ckv"), SEQ)
        dve.scalar_tensor_tensor(ckv[:, :], ckv[:, :], operand("ckv_gain"), r, ALU.mult,
                                 ALU.mult).then_inc(ckv_ready, 1)
        for c in range(2, GH):
            scaled_line(("mixer", "gk", c), gk[:, c * SEQ:(c + 1) * SEQ]).then_inc(gla_in, 1)

        def gq_of(c):
            scaled_line(("mixer", "gq", c), gq[:, c], GDK ** -0.5).then_inc(gla_in, 1)

        dve.wait_ge(soft_out, 1)
        link(dve.scalar_tensor_tensor(fall[:, :], gate_k[:, :], -1.0 / TAU, gate_q[:, :], ALU.mult, ALU.add))
        gq_of(0)
        link(dve.tensor_tensor_scan(decay, const("keep"), fall[:, :], 0.0, ALU.mult, ALU.add))

        gq_of(1)

        def falls(n):
            if n == len(HALVES):
                d, f = (x.rearrange("p (b t) -> p b t", t=CHUNK) for x in (decay, fall[:, :]))
                dve.tensor_tensor(f, d[:, :, CHUNK - 1:CHUNK].to_broadcast([P, GH * SEQ // CHUNK, CHUNK]), d,
                                  ALU.subtract).then_inc(fallen, 1)
                return
            half = HALVES[n]
            d, f = (x.rearrange("p (b s t) -> p b s t", s=2, t=half) for x in (decay, fall[:, :]))
            ref = d[:, :, 0, half - 1:half].to_broadcast([P, GH * SEQ // (2 * half), half])
            link(dve.tensor_tensor(f[:, :, 0], ref, d[:, :, 0], ALU.subtract))
            dve.tensor_tensor(f[:, :, 1], d[:, :, 1], ref, ALU.subtract).then_inc(fallen, 1)

        def by_head(x):
            return x.rearrange("p (g t) -> p g t", t=SEQ)

        falls(0)
        for n in range(len(HALVES) + 1):
            if n == 0:
                for c in range(2, GH):
                    gq_of(c)
                dve.wait_ge(gla_in, 2 * GH)
            dve.wait_ge(risen, n + 1)
            if n < len(HALVES):
                dve.tensor_tensor(by_head(gate_q[:, :]), gq, by_head(fall[:, :]), ALU.mult)
            else:
                dve.wait_ge(grown_ready, 1)
                dve.tensor_tensor(by_head(gate_q[:, :]), gq, grown, ALU.mult)
            dve.tensor_tensor(gate_k[:, :], gk, fall[:, :], ALU.mult).then_inc(level_ready, 1)
            if n < len(HALVES):
                dve.wait_ge(level_ready, n + 1)
                falls(n + 1)
                for kind, c in LEVEL_FILLERS[2 * n:2 * n + 2]:
                    if kind == "gv":
                        if c >= 2:
                            dve.wait_ge(gv_turned, c - 1)
                        scaled_line(("mixer", kind, c), prod2[:, c % 2, 0:SEQ]).then_inc(gv_raw, 1)
                    else:
                        scaled_line(("mixer", kind, c), index_q[:, c]).then_inc(index_q_ready, 1)
            for t in range(TILES):
                s = SCORE[("mixer", "level", n, t)]
                dve.wait_ge(score_done, s + 1)
                mask = levels[:, n].unsqueeze(1).to_broadcast([P, GH, P])
                dve.copy_predicated(pairs[:, t], mask,
                                    score_bank[s % 2][:, :].rearrange("p (g t) -> p g t", t=P)).then_inc(level_used, 1)

        def gr_of(m):
            scaled_line(("mixer", "gr", m), gr[:, m]).then_inc(gr_raw, 1)

        def silu_gr(m):
            dve.wait_ge(tanh_ready, 8 * DEPTH + m + 1)
            dve.scalar_tensor_tensor(gr[:, m], probs[:, m % 2, 0:SEQ], 1.0, gr[:, m], ALU.add,
                                     ALU.mult).then_inc(gates_ready, 1)

        def head_states(g):
            if g:
                dve.wait_ge(gla_done, 2 * g)
            for c in range(3):
                s = SCORE[("mixer", "state", g, c)]
                dve.wait_ge(score_done, s + 1)
                bank = score_bank[s % 2][:, 0:GDV]
                if c == 0:
                    dve.tensor_copy(states[:, 0], bank).then_inc(state_ready, 1)
                else:
                    dve.wait_ge(state_ready, 3 * g + c)
                    end = c * CHUNK + CHUNK - 1
                    dve.scalar_tensor_tensor(states[:, c], states[:, c - 1], grown[:, g, end:end + 1], bank, ALU.mult,
                                             ALU.add).then_inc(state_ready, 1)

        def head_gated(g):
            r = rstd_of(("mixer", "gla", g), SEQ)
            dve.wait_ge(gla_raw, 2 * g + 2)
            for e in range(2):
                m = 2 * g + e
                link(dve.scalar_tensor_tensor(prod[:, e, 0:SEQ], prod[:, e, 0:SEQ], gla_gain[:, m:m + 1], r, ALU.mult,
                                              ALU.mult))
                dve.tensor_tensor(prod2[:, e, 0:SEQ], prod[:, e, 0:SEQ], gr[:, m], ALU.mult).then_inc(gla_full, 1)
            for e in range(2):
                m = 2 * g + e
                dve.wait_ge(gg_hi_ready, m + 1)
                dve.tensor_tensor(gg_lo[:, m], prod2[:, e, 0:SEQ], gg_hi[:, m].bitcast(F32),
                                  ALU.subtract).then_inc(gg_ready, 1)

        def dq_of(m):
            scaled_line(("mixer", "dq", m), dq[:, m], P ** -0.5).then_inc(dq_ready, 1)

        dve.wait_ge(level_ready, len(HALVES) + 1)
        for g in range(GH):
            gr_of(2 * g)
            gr_of(2 * g + 1)
            head_states(g)
            silu_gr(2 * g)
            silu_gr(2 * g + 1)
            if g:
                head_gated(g - 1)
        dq_of(0)
        dq_of(1)
        head_gated(GH - 1)

        def gate_of(name, m):
            scaled_line(("mixer", name, m), mgate[name[1]][:, m]).then_inc(gate_raw, 1)

        gate_of("mg", 0)
        gate_of("mg", 1)

        def choose(t):
            keys = (t + 1) * P
            own = score[:, t, t * P:keys]
            link(dve.tensor_tensor(own, own, const("later"), ALU.add))
            for r in range(TOPK // 8):
                src = work[:, t, 0:keys] if r else score[:, t, 0:keys]
                link(dve.max(best[:, :], src))
                link(dve.match_replace(work[:, t, 0:keys], best[:, :], src, TAKEN))
                m = 2 + TOPK // 16 * t + r // 2
                if r % 2 and m < KT:
                    gate_of("mg", m)
            link(dve.tensor_scalar(score[:, t, 0:keys], work[:, t, 0:keys], TAKEN / 2, NEG, ALU.is_gt, ALU.mult))
            link(dve.tensor_tensor(own, own, const("later"), ALU.add))

        for n, (t, hd) in enumerate((t, hd) for t in range(TILES) for hd in range(SH)):
            keys = (t + 1) * P
            dve.wait_ge(relued, n + 1)
            w = index_w[:, t, hd:hd + 1]
            if hd == 0:
                dve.tensor_scalar(score[:, t, 0:keys], th[:, n % 2, 0:keys], w, None, ALU.mult).then_inc(scored, 1)
            else:
                dve.wait_ge(scored, n)
                dve.scalar_tensor_tensor(score[:, t, 0:keys], th[:, n % 2, 0:keys], w, score[:, t, 0:keys], ALU.mult,
                                         ALU.add).then_inc(scored, 1)
            if n % 2 and n // 2 + 2 < SH:
                dq_of(n // 2 + 2)
        dve.wait_ge(scored, TILES * SH)
        for t in range(TILES):
            choose(t)

        def dsa_maxes(i):
            hd, t = DSA_JOBS[i]
            n, s, keys = JOB[DEPTH] + i, SCORE[("mixer", "dsa", hd, t)], (t + 1) * P
            bank = score_bank[s % 2][:, 0:keys]
            dve.wait_ge(score_done, s + 1)
            link(dve.tensor_tensor(bank, bank, score[:, t, 0:keys], ALU.add))
            dve.tensor_reduce(top[:, n % 2, 0:1], bank, AX.X, ALU.max, negate=True).then_inc(maxed, 1)

        def dsa_shares(i):
            hd, t = DSA_JOBS[i]
            n, keys = JOB[DEPTH] + i, (t + 1) * P
            dve.wait_ge(exped, n + 1)
            link(dve.reciprocal(share[:, n % 2, 0:1], total[:, n % 2, 0:1]))
            dve.tensor_scalar(probs[:, n % 2, 0:keys], probs[:, n % 2, 0:keys], share[:, n % 2, 0:1], None,
                              ALU.mult).then_inc(probs_ready, 1)

        def rest_of_od(i):
            hd, t = DSA_JOBS[i]
            if t == TILES - 1:
                dve.wait_ge(od_hi_ready, hd + 1)
                dve.tensor_tensor(od_lo[:, hd], result_bank[RESULT[("mixer", "dsa", hd)] % 2][:, 0:SEQ],
                                  od_hi[:, hd].bitcast(F32), ALU.subtract).then_inc(od_ready, 1)

        def filled(i):
            name, m = DSA_FILLERS[i]
            if name == "ms":
                gate_of(name, m)
                return
            dve.wait_ge(gate_ready, 16 * DEPTH + m + 1)
            dst = mgate["g"][:, m]
            dve.scalar_tensor_tensor(dst, dst, 1.0, line_wait(("mixer", name, m))[:, 0:SEQ], ALU.add,
                                     ALU.mult).then_inc(y_used, 1)

        for i in range(len(DSA_JOBS) + 2):
            if i < len(DSA_JOBS):
                dsa_maxes(i)
                dsa_shares(i)
                filled(i)
            if i >= 2:
                rest_of_od(i - 2)

        dve.wait_ge(gate_ready, 16 * DEPTH + 2 * KT)
        for m in range(KT):
            bank = line_wait(("mixer", "ys", m))
            dve.scalar_tensor_tensor(prod[:, m % 2, 0:SEQ], mgate["s"][:, m], 1.0, bank[:, 0:SEQ], ALU.add,
                                     ALU.mult).then_inc(y_used, 1)
            dve.wait_ge(y_used, 16 * DEPTH + KT + m + 1)
            dve.tensor_tensor(wide[:, m, 0:SEQ], prod[:, m % 2, 0:SEQ], mgate["g"][:, m],
                              ALU.add).then_inc(full_ready, 1)
            if m:
                rest_of_full("mixed2", m - 1, SEQ)
        rest_of_full("mixed2", KT - 1, SEQ)
        for m in range(KT):
            dve.scalar_tensor_tensor(h[:, m, 0:SEQ], line_wait(("mixer", "mix", m))[:, 0:SEQ], 0.5, h[:, m, 0:SEQ],
                                     ALU.mult, ALU.add).then_inc(h_ready, 1)
            dve.wait_ge(h_ready, H_BATCH["mixer"] + m + 1)
            rest_of_h("ffn1", m, SEQ)
        rstd_of(("ffn1", "norm"), SEQ, scale[:, 0:SEQ])
        dve.wait_ge(p_hi_ready, 1)
        dve.tensor_tensor(p_lo[:, :, :], p_in, p_hi[:, :, :].bitcast(F32), ALU.subtract).then_inc(p_ready, 1)
        ffn(1)

        rstd_of(("embed", "norm"), SEQ, scale[:, 0:SEQ])

        def embedded(m):
            dve.wait_ge(tanh_ready, 8 * DEPTH + KT + m + 1)
            dve.wait_ge(pp_ready, m + 1)
            dve.scalar_tensor_tensor(prod[:, m % 2, 0:SEQ], th[:, m % 2, 0:SEQ], 1.0, pp[:, m], ALU.add,
                                     ALU.mult).then_inc(pg_used, 1)
            dve.wait_ge(pg_used, m + 1)
            dve.tensor_tensor(h[:, m, 0:SEQ], h[:, m, 0:SEQ], prod[:, m % 2, 0:SEQ], ALU.add).then_inc(h_ready, 1)

        for m in range(KT):
            scaled_line(("embed", "pg", m), prod2[:, m % 2, 0:SEQ]).then_inc(pg_raw, 1)
            if m:
                embedded(m - 1)
            if m >= 2:
                add_square("final1", m - 2, m - 2, SEQ)
        embedded(KT - 1)
        add_square("final1", KT - 2, KT - 2, SEQ)
        add_square("final1", KT - 1, KT - 1, SEQ)
        dve.wait_ge(h_ready, H_BATCH["embed"] + KT)
        r = rstd_of(("final1", "norm"), SEQ)
        for k in range(KT):
            dve.scalar_tensor_tensor(wide[:, k, 0:SEQ], h[:, k, 0:SEQ], operand("g_final1")[:, k:k + 1], r, ALU.mult,
                                     ALU.mult).then_inc(out_ready, 1)

    @block.tensor
    def _(pe):
        def unit(key):
            u = UNIT[key]
            if key == LINES[0]:
                pe.wait_ge(lo_cut, 1)
            elif key == UNITS[u][0] or key == LINES[1]:
                pe.wait_ge(lo_cut, cuts(u))
            return w_hi[:, u % CUT].rearrange("p (b c) -> p b c", c=P), \
                w_lo[:, u % CUT].rearrange("p (b c) -> p b c", c=P)

        def line_open(key):
            g = LINE[key]
            if LINE_BEFORE[g]:
                name, count = LINE_BEFORE[g]
                pe.wait_ge(signals[name], count)
            return product_bank[LINE_BANK[g]]

        def line(key, n, src=None, depth=KT, first=0, at=None, ready=None, last=None):
            if at is None:
                at = key[-1] % 2 * KT
            hi, lo = unit(key)
            src_hi, src_lo = src or x_of[key[0]]
            bank = line_open(key)
            for k in range(depth):
                if last and k == depth - 1:
                    last()
                if ready:
                    ready(k)
                here = [(hi[:, at + k], src_hi), (hi[:, at + k], src_lo), (lo[:, at + k], src_hi)]
                for m, (stay, move) in enumerate(here):
                    ins = pe.matmul(bank[:, 0:n], stay, move[:, first + k, 0:n], start=(k, m) == (0, 0),
                                    stop=(k, m) == (depth - 1, 2))
            ins.then_inc(line_done, 1)

        def x_tile(batch):
            return lambda k: pe.wait_ge(x_ready, X_BATCH[batch] + k + 1)

        def stat_open(key):
            s = STAT[key]
            if s:
                pe.wait_ge(stat_read, s)

        def sums(key, tiles, mean):
            stat_open(key)
            for n, sq in enumerate(tiles):
                pe.wait_ge(squares_ready, SQUARES[key] + n + 1)
                ins = pe.matmul(stat_bank[:, 0:sq.shape[-1]], mean, sq, start=n == 0, stop=n == len(tiles) - 1)
            ins.then_inc(stat_done, 1)

        def norm_sum(name, n):
            stat_open((name, "norm"))
            pe.wait_ge(summed, SUMMED[name] + KT)
            pe.matmul(stat_bank[:, 0:n], mean_dm[:, :], sum_of[name][0][:, 0:n], start=True,
                      stop=True).then_inc(stat_done, 1)

        def result_open(key):
            r = RESULT[key]
            if r >= 2:
                name, count = RESULT_READ[RESULTS[r - 2]]
                pe.wait_ge(signals[name], count)
            return result_bank[r % 2]

        def score_open(key):
            s = SCORE[key]
            if s >= 2:
                name, count = SCORE_READ[SCORES[s - 2]]
                pe.wait_ge(signals[name], count)
            return score_bank[s % 2]

        ident = const("ident")

        def layer(i):
            name, W = f"layer{i}", WIDTH[i]
            line((name, "ka"), TOK, at=0, ready=x_tile(name), last=(lambda: norm_sum(name, TOK)) if i else None)
            line((name, "va"), TOK, at=KT)

            def turn_v(n):
                pe.wait_ge(v_raw, 5 * i + n + 1)
                if n:
                    pe.wait_ge(v_ready, 2 * (5 * i + n))
                for t, w in key_tiles(TOK):
                    ins = pe.transpose(turn_bank[0:w, t * P:(t + 1) * P], prod2[:, n % 2, t * P:t * P + w], ident)
                ins.then_inc(v_turned, 1)

            def head_sum(n):
                sums((name, "head", n), [th[:, n % 2, 0:W if n else TOK]], const("head_mean"))

            def rot(n):
                src = ka[:, :] if n == 0 else qa[:, n - 1, 0:W]
                bank = result_open((name, "rot", n))
                pe.wait_ge(normed, 5 * i + n + 1)
                pe.matmul(bank[:, 0:src.shape[-1]], const("rot"), src, start=True, stop=True).then_inc(rot_done, 1)

            for at, key in enumerate(HEAD_LINES):
                line((name, *key), TOK if key[0] in ("kb", "vb") else W)
                if (i, at) == (0, 0):
                    norm_sum(name, TOK)
                    pe.wait_ge(loaded, 16)
                n = at // 2
                if at % 2 and 1 <= n <= PAIRS + 1:
                    rot(n - 1)
                if at % 2 and n <= PAIRS:
                    head_sum(n)
                if at == 1:
                    turn_v(0)
                if key[0] == "vb" and key[1]:
                    turn_v(key[1])
            turn_v(PAIRS)

            def scores(job, n):
                key = (name, *job)
                s = score_open(key)
                if job[0] == "Bm":
                    for hd in [*range(0, HEADS, 2), *range(1, HEADS, 2)]:
                        if hd == 1:
                            ins.then_inc(even_scores, 1)
                            pe.wait_ge(even_scores, i + 1)
                        r = slice(hd % 2 * HD, hd % 2 * HD + HD)
                        ins = pe.matmul(s[0:META, hd * META:(hd + 1) * META], qb[r, hd // 2, SEQ:TOK],
                                        kb[r, hd // 2, SEQ:TOK], start=True, stop=True)
                elif job[0] == "Am":
                    r = slice(job[1] * HD, job[1] * HD + HD)
                    ins = pe.matmul(s[0:PAIRS * META, 0:TOK], q_meta[r, :], ka[r, :], start=True, stop=True)
                else:
                    kind, c, half, t = job
                    r = slice(half * HD, half * HD + HD)
                    q, k = (qa, ka[r, :]) if kind == "A" else (qb, kb[r, c])
                    ins = pe.matmul(s[:, 0:TOK], q[r, c, t * P:(t + 1) * P], k, start=True, stop=kind == "A")
                    if kind == "B":
                        m = PAIRS * i + c
                        pe.wait_ge(rel_ready, m + 1)
                        ins = pe.matmul(s[:, 0:SEQ], const("flip"), rel[:, m % 2, t, half], start=False, stop=True)
                ins.then_inc(score_done, 1)

            def turn(job, n):
                pe.wait_ge(probs_ready, n + 1)
                r = TURN[(name, *job)]
                if r:
                    pe.wait_ge(turned_most, r)
                    pe.wait_ge(turned_rest, r)
                if job[0] == "Bm":
                    for hd in range(HEADS):
                        at = slice(hd * META, (hd + 1) * META)
                        ins = pe.transpose(turn_bank[0:META, at], probs[0:META, n % 2, at], ident[0:META, 0:META])
                else:
                    m = PAIRS * META if job[0] == "Am" else P
                    for kt, w in key_tiles(TOK):
                        ins = pe.transpose(turn_bank[0:w, kt * P:kt * P + m], probs[0:m, n % 2, kt * P:kt * P + w],
                                           ident[0:m, 0:m])
                ins.then_inc(turn_done, 1)

            def values(job, n):
                pe.wait_ge(turned_most, TURN[(name, *job)] + 1)
                pe.wait_ge(turned_rest, TURN[(name, *job)] + 1)
                tn = turned[:, n % 2]
                if job[0] == "Bm":
                    bank = result_open((name, "Bm"))
                    for hd in range(HEADS):
                        r = slice(hd % 2 * HD, hd % 2 * HD + HD)
                        ins = pe.matmul(bank[r, hd // 2 * META:(hd // 2 + 1) * META],
                                        vb[0:META, 2, hd * HD:(hd + 1) * HD], tn[0:META, hd * META:(hd + 1) * META],
                                        start=True, stop=True)
                else:
                    if job[0] == "Am":
                        half, m, at, v = job[1], PAIRS * META, 0, va[:, :, job[1] * HD:(job[1] + 1) * HD]
                        bank = result_open((name, "Am")) if half == 0 else result_bank[RESULT[(name, "Am")] % 2]
                    else:
                        kind, c, half, t = job
                        head = half if kind == "A" else 2 * c + half
                        m, at, v = P, t * P, (va if kind == "A" else vb)[:, :, head * HD:(head + 1) * HD]
                        key = (name, kind, c)
                        bank = result_open(key) if (half, t) == (0, 0) else result_bank[RESULT[key] % 2]
                    r = slice(half * HD, half * HD + HD)
                    for kt, w in key_tiles(TOK):
                        ins = pe.matmul(bank[r, at:at + m], v[0:w, kt], tn[0:w, kt * P:kt * P + m], start=kt == 0,
                                        stop=kt == 2)
                ins.then_inc(valued, 1)

            pe.wait_ge(roped, 9 * i + (9 if W == TOK else 5))
            pe.wait_ge(kq_ready, 8 * i + 8)
            pe.wait_ge(v_ready, 10 * i + 10)
            J, jobs = len(JOBS[i]), JOBS[i]
            for t in range(J + 2):
                if t < J:
                    scores(jobs[t], JOB[i] + t)
                if t < len(FILLERS):
                    kind, m = FILLERS[t]
                    if kind == "ya":
                        pe.wait_ge(y_ready, KT * i + PAIRS)
                        line((name, kind, m), W, y_of[name], PAIRS, 0, m % 4 * PAIRS)
                    else:
                        line((name, kind, m), W)
                if 1 <= t <= J:
                    turn(jobs[t - 1], JOB[i] + t - 1)
                if t >= 2:
                    values(jobs[t - 2], JOB[i] + t - 2)
            for m in range(KT):
                line((name, "yb", m), W, y_of[name], PAIRS, PAIRS, m % 4 * PAIRS,
                     ready=(lambda k: pe.wait_ge(y_ready, KT * i + PAIRS + k + 1)) if m == 0 else None)
            for m in range(KT):
                line((name, "out", m), W, x_of[f"mixed{i}"], ready=x_tile(f"mixed{i}") if m == 0 else None)

        pe.wait_ge(set_up, 2)
        for i in range(DEPTH):
            layer(i)

        def two_norm_sums():
            stat_open(("ffn0", "norm"))
            pe.wait_ge(summed, SUMMED["final0"] + 2 * KT)
            for n in range(2):
                pe.matmul(stat_bank[:, n * SEQ:(n + 1) * SEQ], mean_dm[:, :], sum_of["final0"][n][:, 0:SEQ],
                          start=True, stop=True).then_inc(stat_done, 1)

        def ffn(f):
            name = f"ffn{f}"
            for j in range(FT):
                if j == 0:
                    line((name, "gate", j), SEQ, at=0, ready=x_tile(name),
                         last=(two_norm_sums, lambda: norm_sum(name, SEQ))[f])
                else:
                    line((name, "gate", j), SEQ, at=0)
                line((name, "up", j), SEQ, at=KT)
            for m in range(KT):
                for half in range(2):
                    first = half * FT // 2
                    line((name, "down", m, half), SEQ, (act_hi, act_lo), FT // 2, first, 0,
                         ready=(lambda k: pe.wait_ge(act_ready, FT * f + first + k + 1)) if m == 0 else None)

        ffn(0)

        line(("mixer", "low"), SEQ, at=0, ready=x_tile("mixer"), last=lambda: norm_sum("mixer", SEQ))
        line(("mixer", "ckv"), SEQ, at=KT)
        line(("mixer", "gk", 0), SEQ)
        bank = result_open(("mixer", "index_w"))
        pe.wait_ge(low_ready, 1)
        for t in range(TILES):
            ins = pe.transpose(bank[:, t * SH:(t + 1) * SH], low[32:32 + SH, t * P:(t + 1) * P],
                               ident[32:32 + SH, 32:32 + SH])
        ins.then_inc(index_w_turned, 1)
        pe.wait_ge(loaded2, 48)
        for i in range(GH // 2):
            bank = score_open(("mixer", "alpha", i))
            for g in range(2 * i, 2 * i + 2):
                ins = pe.matmul(bank[:, g % 2 * SEQ:(g % 2 + 1) * SEQ],
                                operand("alpha_w", LOWRANK)[:, g * GDK:(g + 1) * GDK], low[0:LOWRANK],
                                start=True, stop=True)
            ins.then_inc(score_done, 1)
        pe.wait_ge(gla_in, 1)
        bank = result_open(("mixer", "rel"))
        pe.matmul(bank[0:SH, :], operand("rel", 32), const("bucket", 32), start=True, stop=True).then_inc(row_done, 1)
        line(("mixer", "gk", 1), SEQ)
        pe.wait_ge(means_ready, 2)
        sums(("mixer", "ckv"), [th[:, 0, 0:SEQ]], mean_p[:, :])
        line(("mixer", "gk", 2), SEQ)
        line(("mixer", "gk", 3), SEQ)
        for c in range(GH):
            line(("mixer", "gq", c), SEQ)
        pe.wait_ge(ckv_ready, 1)
        pe.wait_ge(turned_rest, TURN[("mixer", "ckv")])
        for t in range(TILES):
            ins = pe.transpose(turn_bank[:, t * P:(t + 1) * P], ckv[:, t * P:(t + 1) * P], ident)
        ins.then_inc(turn_done, 1)

        def turn_gv(c):
            pe.wait_ge(gv_raw, c + 1)
            if c:
                pe.wait_ge(gv_ready, c)
            else:
                pe.wait_ge(turned_most, TURN[("mixer", "ckv")] + 1)
            for t in range(TILES):
                ins = pe.transpose(turn_bank[:, t * P:(t + 1) * P], prod2[:, c % 2, t * P:(t + 1) * P], ident)
            ins.then_inc(gv_turned, 1)

        for n in range(len(HALVES) + 1):
            for kind, c in LEVEL_FILLERS[2 * n:2 * n + 2]:
                line(("mixer", kind, c), SEQ)
            last = n == len(HALVES)
            if n:
                for kind, c in LEVEL_FILLERS[2 * n - 2:2 * n]:
                    if kind == "gv":
                        turn_gv(c)
            if not last:
                pe.wait_ge(level_ready, n + 1)
            for t in range(TILES):
                bank = score_open(("mixer", "level", n, t))
                for g in range(GH):
                    at = slice(g * SEQ + t * P, g * SEQ + (t + 1) * P)
                    keys, queries = (gk, gq[:, g, t * P:(t + 1) * P]) if last else (gate_k, gate_q[:, at])
                    ins = pe.matmul(bank[:, g * P:(g + 1) * P], keys[:, at], queries, start=True, stop=True)
                ins.then_inc(score_done, 1)
        line(("mixer", "gr", 0), SEQ)
        pe.wait_ge(level_ready, len(HALVES) + 1)
        for t in range(TILES):
            bank = score_open(("mixer", "kdt", t))
            for g in range(GH):
                ins = pe.transpose(bank[:, g * P:(g + 1) * P], gate_k[:, g * SEQ + t * P:g * SEQ + (t + 1) * P], ident)
            ins.then_inc(score_done, 1)
        pe.wait_ge(gv_ready, 2 * GH)

        def head_mean_gla(g):
            sums(("mixer", "gla", g), [th[:, e, 0:SEQ] for e in range(2)], mean_gdv[:, :])

        for g in range(GH):
            if g:
                line(("mixer", "gr", 2 * g), SEQ)
            line(("mixer", "gr", 2 * g + 1), SEQ)
            if g:
                head_mean_gla(g - 1)
            for c in range(3):
                pe.wait_ge(kdt_ready, c // 2 + 1)
                bank = score_open(("mixer", "state", g, c))
                rows = slice(c % 2 * CHUNK, (c % 2 + 1) * CHUNK)
                at = (c // 2 * GH + g) * P
                pe.matmul(bank[:, 0:GDV], fall[rows, at:at + P], gv[rows, c // 2, g * GDV:(g + 1) * GDV],
                          start=True, stop=True).then_inc(score_done, 1)
            for e in range(2):
                bank = result_open(("mixer", "gla", g, e))
                pe.wait_ge(level_used, TILES * (len(HALVES) + 1))
                out_rows = slice(g * GDV + e * P, g * GDV + (e + 1) * P)
                for t in range(TILES):
                    pe.matmul(bank[:, t * P:(t + 1) * P], gv[:, t, out_rows], pairs[:, t, g], start=t == 0, stop=False)
                pe.wait_ge(state_ready, 3 * g + 3)
                for c in range(1, SEQ // CHUNK):
                    at = slice(c * CHUNK, (c + 1) * CHUNK)
                    ins = pe.matmul(bank[:, at], states[:, c - 1, e * P:(e + 1) * P],
                                    gate_q[:, g * SEQ + c * CHUNK:g * SEQ + (c + 1) * CHUNK], start=False,
                                    stop=c == SEQ // CHUNK - 1)
                ins.then_inc(gla_done, 1)

        line(("mixer", "dq", 0), SEQ)
        line(("mixer", "dq", 1), SEQ)
        head_mean_gla(GH - 1)
        for m in range(2):
            line(("mixer", "mg", m), SEQ)
        pe.wait_ge(index_q_ready, PAIRS)
        pe.wait_ge(index_k_ready, 2)
        for n, (t, hd) in enumerate((t, hd) for t in range(TILES) for hd in range(SH)):
            bank = score_open(("mixer", "dots", t, hd))
            rows = slice(hd % 2 * HD, (hd % 2 + 1) * HD)
            pe.matmul(bank[:, 0:(t + 1) * P], index_q[rows, hd // 2, t * P:(t + 1) * P], index_k[rows, 0:(t + 1) * P],
                      start=True, stop=True).then_inc(score_done, 1)
            if n % 2 and n // 2 + 2 < SH:
                line(("mixer", "dq", n // 2 + 2), SEQ)
        for m in range(2, KT):
            line(("mixer", "mg", m), SEQ)

        def dsa_scores(i):
            hd, t = DSA_JOBS[i]
            bank = score_open(("mixer", "dsa", hd, t))
            pe.wait_ge(dq_ready, hd + 1)
            keys = (t + 1) * P
            pe.matmul(bank[:, 0:keys], dq[:, hd, t * P:(t + 1) * P], ckv[:, 0:keys], start=True, stop=False)
            pe.wait_ge(rbias_in[hd % 2], 16 * TILES * (hd // 2 + 1))
            pe.matmul(bank[:, 0:keys], const("flip"), rbias[:, hd % 2, t * P:t * P + keys], start=False,
                      stop=True).then_inc(score_done, 1)

        def dsa_turn(i):
            hd, t = DSA_JOBS[i]
            n = JOB[DEPTH] + i
            pe.wait_ge(probs_ready, n + 1)
            pe.wait_ge(turned_most, TURN[("mixer", "dsa", hd, t)])
            for kt in range(t + 1):
                ins = pe.transpose(turn_bank[:, kt * P:(kt + 1) * P], probs[:, n % 2, kt * P:(kt + 1) * P], ident)
            ins.then_inc(turn_done, 1)

        def dsa_values(i):
            hd, t = DSA_JOBS[i]
            n, key = JOB[DEPTH] + i, ("mixer", "dsa", hd)
            bank = result_open(key) if t == 0 else result_bank[RESULT[key] % 2]
            pe.wait_ge(turned_most, TURN[("mixer", "dsa", hd, t)] + 1)
            for kt in range(t + 1):
                ins = pe.matmul(bank[:, t * P:(t + 1) * P], ckv_t[:, kt], turned[:, n % 2, kt * P:(kt + 1) * P],
                                start=kt == 0, stop=kt == t)
            ins.then_inc(valued, 1)

        for i in range(len(DSA_JOBS) + 2):
            if i < len(DSA_JOBS):
                dsa_scores(i)
                if i == KT:
                    pe.wait_ge(gg_ready, KT)
                name, m = DSA_FILLERS[i]
                line(("mixer", name, m), SEQ, (gg_hi, gg_lo) if name == "yg" else None)
            if 1 <= i <= len(DSA_JOBS):
                dsa_turn(i - 1)
            if i >= 2:
                dsa_values(i - 2)
        for m in range(KT):
            line(("mixer", "ys", m), SEQ, (od_hi, od_lo),
                 ready=(lambda k: pe.wait_ge(od_ready, k + 1)) if m == 0 else None)
        for m in range(KT):
            line(("mixer", "mix", m), SEQ, x_of["mixed2"], ready=x_tile("mixed2") if m == 0 else None)

        ffn(1)
        pe.wait_ge(p_ready, 1)
        for m in range(KT):
            line(("embed", "pp", m), SEQ, (p_hi, p_lo), 2, 0, 2 * m)
        for m in range(KT):
            if m == 0:
                line(("embed", "pg", m), SEQ, ready=x_tile("embed"), last=lambda: norm_sum("embed", SEQ))
            else:
                line(("embed", "pg", m), SEQ)
        norm_sum("final1", SEQ)

    al.close()


def pair_heads(width=HD):
    return np.concatenate([np.r_[c * width:(c + 1) * width, (c + PAIRS) * width:(c + PAIRS + 1) * width]
                           for c in range(PAIRS)])


def blocks_of(w):
    k, n = w.shape
    return w.reshape(k // P, P, n // P, P).transpose(1, 2, 0, 3).reshape(P, -1)


def weight_stream(a):
    rows = []
    cols = np.cumsum([0, 512, 128, 128, 512, 512, 512, 512, 512, 1024, 1024])
    heads = pair_heads()
    for i in range(DEPTH):
        qa, ka, va, za, qb, kb, vb, zb, ga, gb = (a["w_in"][i][:, cols[j]:cols[j + 1]] for j in range(10))
        rows += [blocks_of(w) for w in (ka, va, qa[:, heads], kb, qb, vb, za[:, heads], zb, ga, gb)]
        rows += [blocks_of(w) for w in (a["w_o_attn"][i][heads], a["w_o_na"][i], a["w_out"][i])]

    def ffn(w_in, w_out):
        both = np.stack([w_in[:, :DFF].reshape(DM, FT, P), w_in[:, DFF:].reshape(DM, FT, P)], 2)
        down = blocks_of(w_out).reshape(P, 2 * KT, FT // 2 * P)
        down = np.pad(down, ((0, 0), (0, 0), (0, (UB - FT // 2) * P)))
        return [blocks_of(both.reshape(DM, 2 * DFF)), down.reshape(P, -1)]

    rows += ffn(a["ffn1_w_in_2"][0], a["ffn1_w_out_2"][0])
    sizes = (GH * GDK, GH * GDK, GH * GDV, GH * GDV, LOWRANK, SH * P, P, SH * HD, HD, SH, 2 * DM)
    cols = np.cumsum((0,) + sizes)
    gq, gk, gv, gr, ga, dq, dkv, iq, ik, iw, gates = (a["mix_w_in_2"][0][:, cols[j]:cols[j + 1]] for j in range(11))
    low = np.zeros((DM, P), np.float32)
    low[:, :LOWRANK], low[:, 32:32 + SH], low[:, HD:] = ga, iw, ik
    n = 2 * P
    rows += [blocks_of(w) for w in (low, dkv, gk, gq, gv, iq, gr, dq[:, :n], gates[:, :n], dq[:, n:], gates[:, n:])]
    rows += [blocks_of(a[n][0]) for n in ("gla_w_out_2", "dsa_w_out_2", "mix_w_out_2")]
    rows += ffn(a["ffn2_w_in_2"][0], a["ffn2_w_out_2"][0])
    rows += [blocks_of(a["ple_w_proj_2"][0]), blocks_of(a["ple_w_gate_2"][0])]
    return np.ascontiguousarray(np.concatenate(rows, 1).reshape(P, len(UNITS), UB * P).transpose(1, 0, 2))


def by_feature(v):
    return v.reshape(-1, P).T


def small_operands(a):
    s, s2 = np.zeros((P, SMALL_W), np.float32), np.zeros((P, SMALL2_W), np.float32)

    def put(name, v):
        at, w = (SMALL.get(name) or SMALL2[name])
        (s if name in SMALL else s2)[:v.shape[0], at:at + w] = v

    gains = dict(layer0=a["norm_g"][0], layer1=a["norm_g"][1], final0=a["final_norm_g"], ffn0=a["ffn1_norm_2"][0],
                 mixer=a["mix_norm_2"][0], ffn1=a["ffn2_norm_2"][0], embed=a["ple_norm_2"][0], final1=a["final_norm_2"])
    for name, g in gains.items():
        put(f"g_{name}", by_feature(g))
    for i in range(DEPTH):
        put(f"q_gain{i}", np.tile(a["q_norm_g"][i], 2)[:, None])
        put(f"k_gain{i}", np.tile(a["k_norm_g"][i], 2)[:, None])
    put("gla_gain", by_feature(a["gla_out_norm_2"][0]))
    put("ckv_gain", by_feature(a["ckv_norm_2"][0]))
    put("alpha_b", by_feature(a["gla_alpha_b_2"][0]))
    put("alpha_w", a["gla_alpha_w_2"][0])
    put("rel", a["rel_bias_2"])
    return s, s2


def constants():
    c, c2 = np.zeros((P, CONST_W), np.float32), np.zeros((P, CONST2_W), np.float32)

    def put(name, v):
        at, w = (CONST.get(name) or CONST2[name])
        (c if name in CONST else c2)[:v.shape[0], at:at + w] = v

    p = np.arange(P)
    put("ident", np.eye(P))
    put("flip", np.eye(P)[::-1])
    put("head_mean", (p[:, None] // HD == p[None] // HD) / HD)
    quarter = HD // 4
    rot = np.zeros((P, P))
    for m in range(P):
        low = m % (2 * quarter) < quarter
        rot[m + quarter if low else m - quarter, m] = -1.0 if low else 1.0
    put("rot", rot)
    t = np.arange(SEQ)
    zeros = np.zeros(META)
    row = np.concatenate([t // GRID_W, zeros]).astype(np.float32)
    col = np.concatenate([t % GRID_W, zeros]).astype(np.float32)
    inv = np.float32(10000.0) ** (-np.arange(0, HD // 2, 2, dtype=np.float32) / np.float32(HD // 2))
    ang = np.concatenate([np.tile(row[:, None] * inv, 2), np.tile(col[:, None] * inv, 2)], 1).astype(np.float32)
    put("cos", np.tile(np.cos(ang).T, (2, 1)))
    put("sin", np.tile(np.sin(ang).T, (2, 1)))
    g = np.arange(GRID_W)
    start = np.clip(g - WIN // 2, 0, GRID_W - WIN)[:, None]
    put("window", np.tile(np.where((g[None] >= start) & (g[None] < start + WIN), 0.0, NEG)[::-1], (2, 1)))
    put("keep", np.tile((np.arange(GH * SEQ) % CHUNK != 0)[None], (P, 1)))
    put("later", np.where(p[None] <= p[:, None], 0.0, NEG))
    d = np.maximum(SEQ - 1 - np.arange(2 * SEQ), 0)
    half = 16
    ratio = np.maximum(d, 1).astype(np.float32) / np.float32(half)
    large = half + (np.log(ratio) / np.float32(np.log(128 / half)) * np.float32(half)).astype(np.int32)
    bucket = np.where(d < half, d, np.minimum(large, 31))
    put("bucket", np.arange(32)[:, None] == bucket[None])
    return c, c2


def level_masks():
    s, t = np.arange(P)[:, None], np.arange(P)[None]
    m = [(s // (2 * h) == t // (2 * h)) & (s // h % 2 == 0) & (t // h % 2 == 1) for h in HALVES] + [s == t]
    return np.ascontiguousarray(np.stack(m, 1).astype(np.uint32))


def kernel(**inputs):
    import concourse.bacc as bacc
    from concourse.bass_utils import run_bass_kernel_spmd

    a = {n: np.asarray(v) for n, v in inputs.items()}
    tokens = np.concatenate([a["x"][0], a["meta_tokens"]])
    arrays = {
        "weights": weight_stream(a),
        "tokens": np.ascontiguousarray(tokens.reshape(TOK, KT, P).transpose(2, 1, 0)),
        "embeds": np.ascontiguousarray(a["p_2"][0, 0].reshape(SEQ, -1, P).transpose(2, 1, 0)),
        "small": small_operands(a)[0],
        "small2": small_operands(a)[1],
        "rpb": np.ascontiguousarray(a["na_rpb"]),
        "consts": constants()[0],
        "consts2": constants()[1],
        "levels": level_masks(),
    }
    nc = bacc.Bacc("TRN2", target_bir_lowering=False, num_devices=1)
    arrays = {f"in_{n}": v for n, v in arrays.items()}
    args = [nc.dram_tensor(n, v.shape, mybir.dt.from_np(v.dtype), kind="ExternalInput").ap() for n, v in arrays.items()]
    out = nc.dram_tensor("out", (P, KT, SEQ), F32, kind="ExternalOutput").ap()
    hybrid_blocks_kernel(nc, *args, out)
    r = run_bass_kernel_spmd(nc, [arrays], core_ids=[0])
    y = r.results[0]["out"]
    return np.ascontiguousarray(y.transpose(2, 1, 0)).reshape(1, SEQ, DM)
```
